# Optimizing a Trainium2 kernel written in Bass

```python
import jax, jax.numpy as jnp
from jax import lax
import numpy as np

D_MODEL = 1024
BATCH = 1
SEQ = 512
DEPTH = 2

CHUNK = 64
Q_BLOCK = 128

MLA_HEADS = 8
MLA_NOPE = 64
MLA_ROPE = 32
MLA_V = 64
Q_LORA = 384
KV_LORA = 256
ROPE_THETA = 10000.0

FOX_HEADS = 8
FOX_HEAD_DIM = 64

CONV_CHANNELS = 512
CONV_WIDTH = 31

FFN_HIDDEN = -(-8 * D_MODEL // (3 * 256)) * 256

N_BRANCHES = 3
RMS_EPS = 1e-6
LN_EPS = 1e-5

IN_SIZES = (
    Q_LORA,
    KV_LORA,
    MLA_ROPE,
    FOX_HEADS * FOX_HEAD_DIM,
    FOX_HEADS * FOX_HEAD_DIM,
    FOX_HEADS * FOX_HEAD_DIM,
    FOX_HEADS,
    2 * CONV_CHANNELS,
    N_BRANCHES * D_MODEL,
)
IN_WIDTH = int(sum(IN_SIZES))
IN_SPLITS = [int(v) for v in np.cumsum(IN_SIZES)[:-1]]

kernel_name = "hybrid_mla_fox_conformer_gated"

def rmsnorm(x, g):
    xf = x.astype(jnp.float32)
    y = xf * lax.rsqrt(jnp.mean(xf * xf, axis=-1, keepdims=True) + RMS_EPS)
    return (y * g.astype(jnp.float32)).astype(x.dtype)

def layernorm(x, g, b):
    xf = x.astype(jnp.float32)
    mu = jnp.mean(xf, axis=-1, keepdims=True)
    var = jnp.mean(jnp.square(xf - mu), axis=-1, keepdims=True)
    y = (xf - mu) * lax.rsqrt(var + LN_EPS)
    return (y * g.astype(jnp.float32) + b.astype(jnp.float32)).astype(x.dtype)

def apply_rope(x, cos, sin):
    half = x.shape[-1] // 2
    x1 = x[..., :half].astype(jnp.float32)
    x2 = x[..., half:].astype(jnp.float32)
    return jnp.concatenate([x1 * cos - x2 * sin, x2 * cos + x1 * sin], axis=-1).astype(x.dtype)

def block_attention(q, k, v, scale, diag_mask, cum=None):
    S = q.shape[2]
    outs = []
    for q0 in range(0, S, Q_BLOCK):
        q1 = q0 + Q_BLOCK
        s = jnp.einsum('bhqd,bhkd->bhqk', q[:, :, q0:q1], k[:, :, :q1]).astype(jnp.float32) * scale
        if cum is not None:
            s = s + cum[:, :, q0:q1, None] - cum[:, :, None, :q1]
        mask = jnp.concatenate([jnp.ones((Q_BLOCK, q0), dtype=bool), diag_mask], axis=1)
        s = jnp.where(mask, s, -jnp.inf)
        p = jax.nn.softmax(s, axis=-1).astype(v.dtype)
        outs.append(jnp.einsum('bhqk,bhkd->bhqd', p, v[:, :, :q1]))
    return jnp.concatenate(outs, axis=2)

def causal_depthwise_conv(u, w, b):
    y = lax.conv_general_dilated(
        u, w[:, None, :], window_strides=(1,), padding=[(CONV_WIDTH - 1, 0)],
        dimension_numbers=('NWC', 'WIO', 'NWC'), feature_group_count=u.shape[-1])
    return y + b

def setup_inputs(seed: int = 0) -> dict:
    key = jax.random.key(seed)
    ks = jax.random.split(key, 24)
    f32 = jnp.float32
    L = DEPTH

    def nrm(k, shape, fan_in, scale=1.0):
        return jax.random.normal(k, shape, f32) * (scale * fan_in ** -0.5)

    def gain(k, shape):
        return 1.0 + 0.05 * jax.random.normal(k, shape, f32)

    out_scale = (2.0 * DEPTH) ** -0.5
    x = jax.random.normal(ks[0], (BATCH, SEQ, D_MODEL), f32)
    positions = (jax.random.randint(ks[1], (BATCH, 1), 0, 4096, dtype=jnp.int32)
                 + jnp.arange(SEQ, dtype=jnp.int32)[None, :])
    b_forget = (jnp.linspace(1.0, 6.0, FOX_HEADS, dtype=f32)[None, :]
                + 0.1 * jax.random.normal(ks[10], (L, FOX_HEADS), f32))
    return {
        "x": x,
        "positions": positions,
        "norm_mix_g": gain(ks[2], (L, D_MODEL)),
        "w_in": nrm(ks[3], (L, D_MODEL, IN_WIDTH), D_MODEL),
        "b_gate": 0.01 * jax.random.normal(ks[4], (L, N_BRANCHES * D_MODEL), f32),
        "q_norm_g": gain(ks[5], (L, Q_LORA)),
        "w_uq": nrm(ks[6], (L, Q_LORA, MLA_HEADS * (MLA_NOPE + MLA_ROPE)), Q_LORA),
        "kv_norm_g": gain(ks[7], (L, KV_LORA)),
        "w_ukv": nrm(ks[8], (L, KV_LORA, MLA_HEADS * (MLA_NOPE + MLA_V)), KV_LORA),
        "b_forget": b_forget,
        "dw_kernel": nrm(ks[11], (L, CONV_WIDTH, CONV_CHANNELS), CONV_WIDTH),
        "dw_bias": 0.01 * jax.random.normal(ks[12], (L, CONV_CHANNELS), f32),
        "conv_ln_g": gain(ks[13], (L, CONV_CHANNELS)),
        "conv_ln_b": 0.01 * jax.random.normal(ks[14], (L, CONV_CHANNELS), f32),
        "w_bo_a": nrm(ks[15], (L, MLA_HEADS * MLA_V, D_MODEL), MLA_HEADS * MLA_V),
        "w_bo_b": nrm(ks[16], (L, FOX_HEADS * FOX_HEAD_DIM, D_MODEL), FOX_HEADS * FOX_HEAD_DIM),
        "w_bo_c": nrm(ks[17], (L, CONV_CHANNELS, D_MODEL), CONV_CHANNELS),
        "w_out": nrm(ks[18], (L, D_MODEL, D_MODEL), D_MODEL, out_scale),
        "norm_ffn_g": gain(ks[19], (L, D_MODEL)),
        "w_ffn_gate": nrm(ks[20], (L, D_MODEL, FFN_HIDDEN), D_MODEL),
        "w_ffn_up": nrm(ks[21], (L, D_MODEL, FFN_HIDDEN), D_MODEL),
        "w_ffn_down": nrm(ks[22], (L, FFN_HIDDEN, D_MODEL), FFN_HIDDEN, out_scale),
        "final_norm_g": gain(ks[23], (D_MODEL,)),
    }

def reference(x, positions, norm_mix_g, w_in, b_gate, q_norm_g, w_uq, kv_norm_g, w_ukv,
              b_forget, dw_kernel, dw_bias, conv_ln_g, conv_ln_b, w_bo_a, w_bo_b, w_bo_c,
              w_out, norm_ffn_g, w_ffn_gate, w_ffn_up, w_ffn_down, final_norm_g):
    B, S, _ = x.shape

    inv_freq = 1.0 / (ROPE_THETA ** (jnp.arange(0, MLA_ROPE, 2, dtype=jnp.float32) / MLA_ROPE))
    ang = positions.astype(jnp.float32)[..., None] * inv_freq
    cos, sin = jnp.cos(ang), jnp.sin(ang)

    idx = jnp.arange(Q_BLOCK)
    chunk_mask = (idx[:, None] // CHUNK) >= (idx[None, :] // CHUNK)
    frame_mask = idx[:, None] >= idx[None, :]

    mla_scale = (MLA_NOPE + MLA_ROPE) ** -0.5
    fox_scale = FOX_HEAD_DIM ** -0.5

    for l in range(DEPTH):
        h = rmsnorm(x, norm_mix_g[l])
        proj = jnp.einsum('bsd,dn->bsn', h, w_in[l])
        (c_q, c_kv, k_r, q_b, k_b, v_b, f_logit, conv_in, gate_logit) = jnp.split(proj, IN_SPLITS, axis=-1)

        q_a = (rmsnorm(c_q, q_norm_g[l]) @ w_uq[l]).reshape(B, S, MLA_HEADS, MLA_NOPE + MLA_ROPE)
        q_rope = apply_rope(q_a[..., MLA_NOPE:], cos[:, :, None, :], sin[:, :, None, :])
        kv = (rmsnorm(c_kv, kv_norm_g[l]) @ w_ukv[l]).reshape(B, S, MLA_HEADS, MLA_NOPE + MLA_V)
        k_rope = apply_rope(k_r, cos, sin)
        k_rope = jnp.broadcast_to(k_rope[:, :, None, :], (B, S, MLA_HEADS, MLA_ROPE))
        qa = jnp.concatenate([q_a[..., :MLA_NOPE], q_rope], axis=-1).transpose(0, 2, 1, 3)
        ka = jnp.concatenate([kv[..., :MLA_NOPE], k_rope], axis=-1).transpose(0, 2, 1, 3)
        va = kv[..., MLA_NOPE:].transpose(0, 2, 1, 3)
        o_a = block_attention(qa, ka, va, mla_scale, chunk_mask)
        o_a = o_a.transpose(0, 2, 1, 3).reshape(B, S, MLA_HEADS * MLA_V) @ w_bo_a[l]

        log_f = jax.nn.log_sigmoid(f_logit.astype(jnp.float32) + b_forget[l].astype(jnp.float32))
        cum = jnp.cumsum(log_f, axis=1).transpose(0, 2, 1)
        qf = q_b.reshape(B, S, FOX_HEADS, FOX_HEAD_DIM).transpose(0, 2, 1, 3)
        kf = k_b.reshape(B, S, FOX_HEADS, FOX_HEAD_DIM).transpose(0, 2, 1, 3)
        vf = v_b.reshape(B, S, FOX_HEADS, FOX_HEAD_DIM).transpose(0, 2, 1, 3)
        o_b = block_attention(qf, kf, vf, fox_scale, frame_mask, cum)
        o_b = o_b.transpose(0, 2, 1, 3).reshape(B, S, FOX_HEADS * FOX_HEAD_DIM) @ w_bo_b[l]

        u = conv_in[..., :CONV_CHANNELS] * jax.nn.sigmoid(conv_in[..., CONV_CHANNELS:])
        u = causal_depthwise_conv(u, dw_kernel[l], dw_bias[l])
        u = jax.nn.silu(layernorm(u, conv_ln_g[l], conv_ln_b[l]))
        o_c = u @ w_bo_c[l]

        g = jax.nn.sigmoid(gate_logit + b_gate[l])
        g_a, g_b, g_c = jnp.split(g, N_BRANCHES, axis=-1)
        y = g_a * o_a + g_b * o_b + g_c * o_c
        x = x + y @ w_out[l]

        h = rmsnorm(x, norm_ffn_g[l])
        ff = jax.nn.silu(h @ w_ffn_gate[l]) * (h @ w_ffn_up[l])
        x = x + ff @ w_ffn_down[l]

    return rmsnorm(x, final_norm_g)


_drawn_inputs = setup_inputs


def setup_inputs(seed=0):
    import zlib

    import numpy as np

    out = dict(_drawn_inputs(seed))
    spreads = {}
    factors = {'norm_mix_g': 3.176,
     'b_gate': 8.0,
     'q_norm_g': 8.0,
     'kv_norm_g': 8.0,
     'dw_bias': 8.0,
     'conv_ln_g': 3.938,
     'conv_ln_b': 8.0}
    for name, (base, spread) in spreads.items():
        noise = np.random.default_rng([zlib.crc32(name.encode()), seed]).standard_normal(out[name].shape)
        drawn = base * np.exp(spread * noise) if base else spread * noise
        out[name] = __import__('jax').numpy.asarray(drawn.astype(out[name].dtype))
    for name, factor in factors.items():
        out[name] = (out[name] * factor).astype(out[name].dtype)
    return out
```

```python
from contextlib import ExitStack, contextmanager

import numpy as np

import concourse.bass as bass
from concourse import mybir

F32 = mybir.dt.float32
F32R = mybir.dt.float32r
BF16 = mybir.dt.bfloat16
I32 = mybir.dt.int32
ALU = mybir.AluOpType
ACT = mybir.ActivationFunctionType
AX_X = mybir.AxisListType.X

P = 128
DEPTH, D, T = 2, 1024, 512
DT = D // P
TT = T // P
Q_LORA, KV_LORA = 384, 256
NOPE, ROPE, VDIM, HEADS = 64, 32, 64, 8
PAIRS = HEADS // 2
CONV, TAPS = 512, 31
CT = CONV // P
FFN = 2816
FT = FFN // P
THETA = 10000.0
RMS_EPS, LN_EPS = 1e-6, 1e-5
MLA_SCALE = (NOPE + ROPE) ** -0.5
FOX_SCALE = NOPE ** -0.5
CHUNK_MASK = 64
MASKED = -1e30

C_Q = 0
C_KV = C_Q + Q_LORA
C_KR = C_KV + KV_LORA
C_QB = C_KR + ROPE
C_KB = C_QB + HEADS * NOPE
C_VB = C_KB + HEADS * NOPE
C_F = C_VB + HEADS * NOPE
C_CONV = C_F + HEADS
C_GATE = C_CONV + 2 * CONV
IN_WIDTH = C_GATE + 3 * D

R_MIX, R_FFN, R_BG, R_Q, R_KV, R_DWB, R_LNG, R_LNB = 0, 8, 16, 40, 43, 45, 49, 53
ROWS = 57
PARAM_ROWS = DEPTH * ROWS + DT
MISC = 2 * ROPE + HEADS

CONV_CH, LAT_CH, UP_CH, QKV_CH, MERGE_CH, OUT_CH, FFN_CH, DOWN_CH = 8, 8, 8, 12, 48, 8, 44, 24
CHUNKS = CONV_CH + LAT_CH + UP_CH + QKV_CH + MERGE_CH + OUT_CH + FFN_CH + DOWN_CH
TILES = 8 + 6 + 16 + 12 + 48 + 8 + 44 + 8
EVENTS = 8 + 8 + 16 + 12 + 48 + 8 + 44 + 24
STEPS = 2 * HEADS * TT
RAW, SPLIT = 4, 2
DOWN_K = (8, 8, 6)

RAW_CREDIT, MM_CREDIT, EVAC_CREDIT, EXP_CREDIT, TURN_CREDIT, O_CREDIT, STD_CREDIT = RAW, 1, 2, 4, 2, 1, 1

TAPS_EARLY, TAPS_MLA, TAPS_FOX = 3, 4, 3


CHUNK_LIST = (
    [(1024, None, 1, 1)] * 8
    + [(1024, None, 1, 1)] * 2 + [(512, None, 1, 1)] * 2 + [(1024, None, 1, 1)] * 2 + [(0, "misc", 1, 2)] * 2
    + [(768, None, 2, 3)] * 2 + [(0, "rope", 2, 3)] * 2 + [(512, None, 2, 2)] * 4
    + [(1024, None, 1, 1)] * 12
    + ([(1024, None, 1, 1)] * 3 + [(512, None, 1, 1)] * 3) * 8
    + [(1024, None, 1, 1)] * 8
    + [(1024, None, 1, 1)] * 44
    + [(P * k, None, 1, 1) for k in DOWN_K] * 8
)
assert len(CHUNK_LIST) == CHUNKS and sum(c[2] for c in CHUNK_LIST) == EVENTS
RING_COUNTS = [16 * sum(c[3] for c in CHUNK_LIST[i::RAW]) for i in range(RAW)]
LAT_TAPS = (6, 6, 4, 4, 2, 6, 6, 0)
SQUARES, FEEDS = 5 + CT + 2 * DT, 5 + CT + DT + DT + FT + DT
OWN = 1 + 4 + 5 + 3 + STEPS + CT + DT + FT

TWO_PI = 2 * np.pi
ROUND = 1.5 * 2.0 ** 23
PI_PARTS = (6.28125, 4058 / 2.0 ** 21, 3.0199160e-7)
PI_DOWN = 3.1415925


def split_views(kind, size, to, of):
    H = ROPE // 2
    if kind == "misc":
        a = of[:, 0:4 * (ROPE + HEADS)].rearrange("p (k c) -> p k c", k=4)
        b = to[:, 0:4 * MISC].rearrange("p (k c) -> p k c", k=4)
        return [(b[:, :, 0:ROPE], a[:, :, 0:ROPE]), (b[:, :, ROPE:ROPE + H], a[:, :, H:ROPE]),
                (b[:, :, ROPE + H:2 * ROPE], a[:, :, 0:H]), (b[:, :, 2 * ROPE:MISC], a[:, :, ROPE:ROPE + HEADS])]
    if kind == "rope":
        a = of[:, 0:3 * P].rearrange("p (k g c) -> p k g c", k=3, c=ROPE)
        b = to[:, 0:6 * P].rearrange("p (k s g c) -> p k s g c", k=3, s=2, c=ROPE)
        straight = [(b[:, k, 0], a[:, k]) for k in range(3)]
        return straight + [x for k in range(3) for x in ((b[:, k, 1, :, 0:H], a[:, k, :, H:ROPE]),
                                                         (b[:, k, 1, :, H:ROPE], a[:, k, :, 0:H]))]
    return [(to[:, 0:size], of[:, 0:size])]


def tile_of(t, j):
    return t[:, bass.ds(j, 1), :].rearrange("p a t -> p (a t)")


def head_of(t, pair, e):
    return t[:, bass.ds(pair * 2 + e, 1), :].rearrange("p a t -> p (a t)")


class Count:

    def __init__(self, start=0):
        self.n, self.dyn = start, 0

    def add(self, by=1):
        self.n += by
        return self.value

    @property
    def value(self):
        return self.dyn + self.n


@contextmanager
def repeat(eng, times, per):
    with eng.Fori(0, times) as i:
        old = [(c, c.n, c.dyn) for c, _ in per]
        for c, by in per:
            if by:
                c.dyn = c.dyn + i * by
        yield i
        for (c, by), (_, n, _) in zip(per, old):
            assert c.n - n == by, f"a turn adds {c.n - n}, not {by} ({[k for k, (q, _) in enumerate(per) if q is c]})"
        for (c, by), (_, n, dyn) in zip(per, old):
            c.n, c.dyn = n + by * times, dyn


def trunk(nc, dram, out):
    KB = 1024
    base = nc.sbuf_base + (-nc.sbuf_base) % 64
    free = [base]

    def at(name, off, shape, dt=F32):
        return nc.alloc_sbuf_tensor_at(name, shape, dt, offset=off)

    def sb(name, shape, dt=F32):
        size = int(np.prod(shape[1:])) * (2 if dt == BF16 else 4)
        t = at(name, free[0], shape, dt)
        free[0] += size + (-size) % 32
        assert free[0] <= nc.sbuf_usable_end, (name, free[0] - nc.sbuf_usable_end)
        return t

    x_t = sb("x_t", [P, DT, T])
    h_hi = sb("h_hi", [P, DT, T], F32R)
    h_lo = sb("h_lo", [P, DT, T], F32R)
    raw = [sb(f"raw{i}", [P, 1024]) for i in range(RAW)]
    w_hi = [sb(f"w_hi{i}", [P, 1024], F32R) for i in range(SPLIT)]
    w_lo = [sb(f"w_lo{i}", [P, 1024], F32R) for i in range(SPLIT)]
    rstd_x = sb("rstd_x", [P, T])
    cos_t = sb("cos_t", [P, T])
    sin_t = sb("sin_t", [P, T])
    tmp = [sb(f"tmp{i}", [P, T]) for i in range(4)]
    v_st = sb("v_st", [P, TT, P])
    u_pad = sb("u_pad", [P, CT, TAPS - 1 + T])
    c_off = free[0]
    c_acc = sb("c_acc", [P, CT, T])
    ones = sb("ones", [P, P])
    ident = sb("ident", [P, P])
    ident_b = sb("ident_b", [P, P], BF16)
    mask_b = sb("mask_b", [P, 2, P], BF16)
    params = sb("params", [P, PARAM_ROWS])
    par = sb("par", [P, ROWS + DT])
    dwk = sb("dwk", [P, CT, DEPTH * TAPS])
    dwk_l = sb("dwk_l", [P, CT, TAPS])
    b_f = sb("b_f", [P, DEPTH])
    eps_t = sb("eps_t", [P, 2])
    neg_max = sb("neg_max", [P, 4])
    row_sum = sb("row_sum", [P, 4])
    row_inv = sb("row_inv", [P, 4])
    f_sum = sb("f_sum", [P, T])
    r0 = free[0]
    free[0] += 88 * KB
    assert free[0] <= nc.sbuf_usable_end, free[0] - nc.sbuf_usable_end
    q_t = at("q_t", r0, [P, HEADS, T])
    k_t = at("k_t", r0 + 16 * KB, [P, HEADS, T])
    v_n = at("v_n", r0 + 32 * KB, [P, TT, HEADS * VDIM])
    oa_hi = at("oa_hi", r0 + 40 * KB, [P, PAIRS, T], F32R)
    oa_lo = at("oa_lo", r0 + 48 * KB, [P, PAIRS, T], F32R)
    ob_hi = at("ob_hi", r0 + 56 * KB, [P, PAIRS, T], F32R)
    ob_lo = at("ob_lo", r0 + 64 * KB, [P, PAIRS, T], F32R)
    p_b = [at(f"p_b{i}", r0 + (72 + 2 * i) * KB, [P, T]) for i in range(2)]
    p_t = at("p_t", r0 + 76 * KB, [P, TT, T])
    q_st = [at(f"q_st{i}", r0 + (84 + 2 * i) * KB, [P, T]) for i in range(2)]
    c_hi = at("c_hi", r0 + 40 * KB, [P, 5, T], F32R)
    c_lo = at("c_lo", r0 + 50 * KB, [P, 5, T], F32R)
    rstd_q = at("rstd_q", r0 + 60 * KB, [P, T])
    rstd_kv = at("rstd_kv", r0 + 62 * KB, [P, T])
    lat_sq = [at(f"lat_sq{i}", r0 + (64 + 2 * i) * KB, [P, T]) for i in range(2)]
    lat_acc = at("lat_acc", r0 + 68 * KB, [P, T])
    lat_std = at("lat_std", r0 + 70 * KB, [P, T])
    x_sq = [at(f"x_sq{i}", c_off + 2 * i * KB, [P, T]) for i in range(2)]
    x_acc = at("x_acc", c_off + 4 * KB, [P, T])
    x_std = at("x_std", c_off + 6 * KB, [P, T])
    ln_sq = [at(f"ln_sq{i}", r0 + (32 + 2 * i) * KB, [P, T]) for i in range(2)]
    ln_acc = at("ln_acc", r0 + 36 * KB, [P, T])
    ln_std = at("ln_std", r0 + 38 * KB, [P, T])
    oc_hi = at("oc_hi", r0 + 72 * KB, [P, CT, T], F32R)
    oc_lo = at("oc_lo", r0 + 80 * KB, [P, CT, T], F32R)
    gate = [at(f"gate{i}", r0 + (32 + 2 * i) * KB, [P, T]) for i in range(3)]
    y_sum = at("y_sum", r0 + 38 * KB, [P, T])
    y_hi = at("y_hi", r0, [P, DT, T], F32R)
    y_lo = at("y_lo", r0 + 16 * KB, [P, DT, T], F32R)
    f_hi = at("f_hi", r0, [P, FT, T], F32R)
    f_lo = at("f_lo", r0 + 44 * KB, [P, FT, T], F32R)
    x_rows = at("x_rows", r0, [P, TT, D])
    out_rows = at("out_rows", r0, [P, TT, D])
    par_rows = at("par_rows", r0 + 16 * KB, [P, P])
    dw_rows = at("dw_rows", r0 + 17 * KB, [P, CONV])
    const_sb = at("const_sb", r0 + 20 * KB, [P, 3 * P + 2])
    pos_i = at("pos_i", r0 + 22 * KB, [P, T], I32)
    pos_f = at("pos_f", r0 + 24 * KB, [P, T])
    ang = at("ang", r0 + 26 * KB, [P, T])

    with ExitStack() as ctx:
        bank = [ctx.enter_context(nc.psum_tensor(f"bank{i}", [P, 512], F32)) for i in range(8)]
        s_bank, t_bank, o_bank, stat_bank = bank[0:4], bank[4:6], bank[6], bank[7]

        def sem(name):
            return ctx.enter_context(nc.semaphore(name))

        raw_ready = [sem(f"raw_ready{i}") for i in range(RAW)]
        hi_done = sem("hi_done")
        lo_done = sem("lo_done")
        mm_done = sem("mm_done")
        evac_done = sem("evac_done")
        x_ready = sem("x_ready")
        feed_hi = sem("feed_hi")
        feed_lo = sem("feed_lo")
        sq_ready = sem("sq_ready")
        sq_added = sem("sq_added")
        acc_zero = sem("acc_zero")
        stat_done = sem("stat_done")
        std_ready = sem("std_ready")
        rstd_ready = sem("rstd_ready")
        sig_done = sem("sig_done")
        act_own = sem("act_own")
        dve_own = sem("dve_own")
        forget_z = sem("forget_z")
        forget_l = sem("forget_l")
        cum_ready = sem("cum_ready")
        cum_put = sem("cum_put")
        kr_ready = sem("kr_ready")
        kr_put = sem("kr_put")
        vt_done = sem("vt_done")
        v_ready = sem("v_ready")
        st_ready = sem("st_ready")
        ones_put = sem("ones_put")
        score_done = sem("score_done")
        max_ready = sem("max_ready")
        exp_done = sem("exp_done")
        norm_done = sem("norm_done")
        turn_done = sem("turn_done")
        turn_out = sem("turn_out")
        pv_done = sem("pv_done")
        o_hi_done = sem("o_hi_done")
        o_lo_done = sem("o_lo_done")
        tap_done = sem("tap_done")
        centred = sem("centred")
        conv_pre = sem("conv_pre")
        conv_out = sem("conv_out")
        y_ready = sem("y_ready")
        ff_ready = sem("ff_ready")
        out_tile = sem("out_tile")
        out_turned = sem("out_turned")
        out_copied = sem("out_copied")
        put_done = sem("put_done")
        in_x = sem("in_x")
        in_par = sem("in_par")
        in_dw = sem("in_dw")
        in_const = sem("in_const")
        in_pos = sem("in_pos")
        in_bf = sem("in_bf")
        const_ok = sem("const_ok")
        par_turned = sem("par_turned")
        par_ok = sem("par_ok")
        x_turned = sem("x_turned")
        angles = sem("angles")
        trig = sem("trig")
        wait_held = sem("wait_held")
        zero_ok = sem("zero_ok")

        def passed(eng):
            eng.sem_inc(wait_held, 1)

        block = ctx.enter_context(nc.Block())

        @block.sync
        def _(sp):
            n = [0]
            freed = Count()

            def load(*parts):
                slot = n[0] % RAW
                sp.wait_ge(lo_done, freed.add())
                for to, src in parts:
                    sp.dma_start(to(raw[slot]), src).then_inc(raw_ready[slot], 16)
                n[0] += 1

            def block_of(w, row, k_tiles, col):
                src = w[bass.ds(row, k_tiles * P), bass.ds(col, P)].rearrange("(k p) c -> p k c", p=P)
                load((lambda r: r[:, 0:k_tiles * P].rearrange("p (k c) -> p k c", k=k_tiles), src))

            w_in, w_out, w_gate, w_up, w_down = (dram[k] for k in ("w_in", "w_out", "w_ffn_gate", "w_ffn_up", "w_ffn_down"))
            w_bo = [dram[k] for k in ("w_bo_a", "w_bo_b", "w_bo_c")]

            for t in range(TT):
                sp.dma_start(x_rows[:, t, :], dram["x"][t * P:(t + 1) * P, :]).then_inc(in_x, 16)
            sp.dma_start(const_sb[:], dram["consts"]).then_inc(in_const, 16)
            sp.dma_start(pos_i[:], dram["positions"].broadcast_to([P, T])).then_inc(in_pos, 16)
            for l in range(DEPTH):
                for name, row, rows in (("norm_mix_g", R_MIX, 8), ("norm_ffn_g", R_FFN, 8), ("b_gate", R_BG, 24),
                                        ("q_norm_g", R_Q, 3), ("kv_norm_g", R_KV, 2), ("dw_bias", R_DWB, 4),
                                        ("conv_ln_g", R_LNG, 4), ("conv_ln_b", R_LNB, 4)):
                    sp.dma_start(par_rows[l * ROWS + row:l * ROWS + row + rows, :],
                                 dram[name][l, :].rearrange("(r c) -> r c", c=P)).then_inc(in_par, 16)
            sp.dma_start(par_rows[DEPTH * ROWS:PARAM_ROWS, :],
                         dram["final_norm_g"].rearrange("(r c) -> r c", c=P)).then_inc(in_par, 16)
            sp.dma_start(dw_rows[0:DEPTH * TAPS, :], dram["dw_kernel"]).then_inc(in_dw, 16)
            with nc.allow_non_contiguous_dma("16 biases"):
                sp.dma_start(b_f[2 * ROPE:MISC, :], dram["b_forget"].rearrange("l h -> h l")).then_inc(in_bf, 16)

            with repeat(sp, DEPTH, [(freed, CHUNKS)]) as l:
                row = l * D
                with repeat(sp, 2, [(freed, 4)]) as i:
                    for e in range(2):
                        block_of(w_in, row, DT, i * (2 * P) + (C_CONV + CONV + e * P))
                        block_of(w_in, row, DT, i * (2 * P) + (C_CONV + e * P))
                block_of(w_in, row, DT, C_Q)
                block_of(w_in, row, DT, C_Q + P)
                block_of(w_in, row, 4, C_Q + 2 * P)
                block_of(w_in, row + 4 * P, 4, C_Q + 2 * P)
                block_of(w_in, row, DT, C_KV)
                block_of(w_in, row, DT, C_KV + P)
                with nc.allow_non_contiguous_dma("narrow columns"):
                    for half in range(2):
                        rows = w_in[bass.ds(row + half * 4 * P, 4 * P), :]
                        view = lambda r, a, b: r[:, 0:4 * (ROPE + HEADS)].rearrange("p (k c) -> p k c", k=4)[:, :, a:b]
                        load((lambda r: view(r, 0, ROPE), rows[:, C_KR:C_KR + ROPE].rearrange("(k p) c -> p k c", p=P)),
                             (lambda r: view(r, ROPE, ROPE + HEADS), rows[:, C_F:C_F + HEADS].rearrange("(k p) c -> p k c", p=P)))
                def heads_of(w, row, k_tiles, width, col, cols, b):
                    parts = []
                    for k in range(k_tiles):
                        src = w[bass.ds(row + k * P, P), 4 * b * width:(4 * b + 4) * width].rearrange("p (h c) -> p h c", c=width)
                        to = lambda r, k=k: r[:, 4 * cols * k:4 * cols * (k + 1)].rearrange("p (h c) -> p h c", h=4)
                        parts.append((to, src[:, :, col:col + cols]))
                    load(*parts)

                for b in range(2):
                    heads_of(dram["w_uq"], l * Q_LORA, 3, NOPE + ROPE, 0, NOPE, b)
                for b in range(2):
                    heads_of(dram["w_uq"], l * Q_LORA, 3, NOPE + ROPE, NOPE, ROPE, b)
                for part in (0, NOPE):
                    for b in range(2):
                        heads_of(dram["w_ukv"], l * KV_LORA, 2, NOPE + VDIM, part, NOPE, b)
                for i in range(QKV_CH):
                    block_of(w_in, row, DT, C_QB + i * P)
                    if i == 3:
                        sp.wait_ge(cum_ready, l + 1)
                        sp.wait_ge(score_done, l * STEPS + STEPS // 2)
                        sp.dma_start(k_t[NOPE:NOPE + 1, :, :], f_sum[2 * ROPE:MISC, :]).then_inc(cum_put, 16)
                with repeat(sp, 4, [(freed, 12)]) as i:
                    for e in range(2):
                        for b in range(3):
                            block_of(w_in, row, DT, i * (2 * P) + (C_GATE + b * D + e * P))
                        for b in range(3):
                            block_of(w_bo[b], l * 512, 4, i * (2 * P) + e * P)
                with repeat(sp, 2, [(freed, 4)]) as i:
                    for e in range(4):
                        block_of(w_out, row, DT, i * (4 * P) + e * P)
                with repeat(sp, FT // 2, [(freed, 4)]) as i:
                    for e in range(2):
                        block_of(w_gate, row, DT, i * (2 * P) + e * P)
                        block_of(w_up, row, DT, i * (2 * P) + e * P)
                with repeat(sp, 2, [(freed, 12)]) as i:
                    for e in range(4):
                        for b in range(3):
                            block_of(w_down, l * FFN + 8 * b * P, DOWN_K[b], i * (4 * P) + e * P)
            block_of(w_in, 0, DT, C_CONV + CONV)

            sp.wait_ge(out_copied, DT)
            for t in range(TT):
                sp.dma_start(out[t * P:(t + 1) * P, :], out_rows[:, t, :]).then_inc(put_done, 16)
            sp.wait_ge(put_done, 16 * TT)

        @block.gpsimd
        def _(pool):
            sq, zero, stat = Count(), Count(), Count()
            score, pv, evac, vr, co, op = Count(), Count(), Count(EVAC_CREDIT), Count(), Count(), Count()

            def clear(acc):
                nc.gpsimd.memset(acc[:], 0.0).then_inc(acc_zero, 1)
                pool.wait_ge(acc_zero, zero.add())

            def add_square(acc, ring, i):
                pool.wait_ge(sq_ready, sq.add())
                nc.gpsimd.tensor_tensor(acc[:], acc[:], ring[i % 2][:], ALU.add).then_inc(sq_added, 1)
                pool.wait_ge(sq_added, sq.value)

            def attention(rows):
                pool.wait_ge(evac_done, evac.value)
                pool.wait_ge(v_ready, vr.add(4))
                passed(pool)

                def stage(pair, first):
                    for e in range(2):
                        if not first:
                            pool.wait_ge(score_done, score.value - 4 + 4 * e)
                            passed(pool)
                        nc.gpsimd.tensor_copy(q_st[e][0:rows, :], head_of(q_t, pair, e)[0:rows, :]).then_inc(st_ready, 1)
                        if e == 0:
                            if not first:
                                pool.wait_ge(pv_done, pv.value)
                                passed(pool)
                            nc.gpsimd.tensor_copy(v_st[:], v_n[:, :, bass.ds(pair * P, P)]).then_inc(st_ready, 1)
                    score.add(8)
                    pv.add(2)

                stage(0, True)
                with repeat(pool, PAIRS - 1, [(score, 8), (pv, 2)]) as i:
                    stage(i + 1, False)

            for s, credit in ((lo_done, RAW_CREDIT), (mm_done, MM_CREDIT), (evac_done, EVAC_CREDIT), (exp_done, EXP_CREDIT),
                              (turn_out, TURN_CREDIT), (o_lo_done, O_CREDIT), (std_ready, STD_CREDIT)):
                pool.sem_inc(s, credit)
            nc.gpsimd.memset(ones[:], 1.0).then_inc(zero_ok, 1)
            nc.gpsimd.memset(eps_t[:, 0:1], RMS_EPS).then_inc(zero_ok, 1)
            nc.gpsimd.memset(eps_t[:, 1:2], LN_EPS).then_inc(zero_ok, 1)
            nc.gpsimd.memset(u_pad[:, :, 0:TAPS - 1], 0.0).then_inc(zero_ok, 1)
            clear(x_acc)
            for j in range(DT):
                add_square(x_acc, x_sq, j)
            with repeat(pool, DEPTH, [(sq, SQUARES), (zero, 5), (stat, 6), (score, STEPS), (pv, 2 * HEADS),
                                      (evac, TILES), (vr, 8), (co, CT), (op, 2)]):
                pool.wait_ge(stat_done, stat.add())
                passed(pool)
                clear(lat_acc)
                for j in range(3):
                    add_square(lat_acc, lat_sq, j)
                pool.wait_ge(stat_done, stat.add())
                passed(pool)
                clear(lat_acc)
                for j in range(2):
                    add_square(lat_acc, lat_sq, j + 1)
                stat.add()
                evac.add(30)
                attention(NOPE + ROPE)
                pool.wait_ge(score_done, score.value)
                pool.wait_ge(pv_done, pv.value)
                passed(pool)
                for e in range(2):
                    nc.gpsimd.memset(q_st[e][NOPE:NOPE + 1, :], 1.0).then_inc(ones_put, 1)
                pool.wait_ge(ones_put, op.add(2))
                evac.add(12)
                attention(NOPE)
                pool.wait_ge(pv_done, pv.value)
                passed(pool)
                clear(ln_acc)
                for j in range(CT):
                    add_square(ln_acc, ln_sq, j)
                stat.add(2)
                pool.wait_ge(conv_out, co.add(CT))
                passed(pool)
                clear(x_acc)
                for j in range(DT):
                    add_square(x_acc, x_sq, j)
                pool.wait_ge(stat_done, stat.add())
                passed(pool)
                clear(x_acc)
                for j in range(DT):
                    add_square(x_acc, x_sq, j)
                evac.add(TILES - 42)

        @block.scalar
        def _(act):
            ev, evac, sqa, stat, own = Count(), Count(EVAC_CREDIT), Count(), Count(), Count()
            vt, mx, tn, pv, ohi, fl, kr, yr, fr, ce, cp, co = (Count() for _ in range(12))
            rr = [Count() for _ in range(RAW)]

            def split(i):
                size, kind, _, dmas = CHUNK_LIST[i % CHUNKS]
                slot = i % RAW
                act.wait_ge(raw_ready[slot], rr[slot].add(16 * dmas))
                act.wait_ge(mm_done, ev.add(CHUNK_LIST[(i - 2) % CHUNKS][2]))
                last = None
                for to, of in split_views(kind, size, w_hi[i % SPLIT], raw[slot]):
                    last = nc.scalar.copy(to, of)
                last.then_inc(hi_done, 1)

            def feed(src, gain, hi, sq, i, first=False):
                nc.scalar.activation(hi, src, ACT.Copy, scale=gain).then_inc(feed_hi, 1)
                if not first:
                    act.wait_ge(sq_added, sqa.value - 1)
                    passed(act)
                sqa.add()
                nc.scalar.activation(sq[i % 2][:], src, ACT.Square).then_inc(sq_ready, 1)

            def root(std, size, eps):
                act.wait_ge(stat_done, stat.add())
                nc.scalar.activation(std[:], stat_bank[:], ACT.Sqrt, scale=1.0 / size,
                                     bias=eps_t[:, eps:eps + 1]).then_inc(std_ready, 1)

            def attention(hi_out):
                def turn(s, first):
                    act.wait_ge(turn_done, tn.add())
                    if s % 4 == 0:
                        if not (first and s == 0):
                            act.wait_ge(pv_done, pv.value)
                        pv.add()
                    q = s % 4
                    nc.scalar.copy(p_t[:, 0:q + 1, q * P:(q + 1) * P],
                                   t_bank[s % 2][:, 0:(q + 1) * P].rearrange("p (k q) -> p k q", q=P)).then_inc(turn_out, 1)

                def pair_out(pair):
                    act.wait_ge(pv_done, ohi.add(2))
                    nc.scalar.copy(tile_of(hi_out, pair), o_bank[:]).then_inc(o_hi_done, 1)

                def body(pair, first):
                    for s in range(8):
                        act.wait_ge(max_ready, mx.add())
                        w = (s % 4 + 1) * P
                        nc.scalar.activation(p_b[s % 2][:, 0:w], s_bank[s % 4][:, 0:w], ACT.Exp,
                                             bias=neg_max[:, s % 4:s % 4 + 1],
                                             accum_out=row_sum[:, s % 4:s % 4 + 1]).then_inc(exp_done, 1)
                        if s > 0:
                            turn(s - 1, first)
                        if s == 3 and not first:
                            pair_out(pair - 1)
                    turn(7, first)

                body(0, True)
                with repeat(act, PAIRS - 1, [(mx, 8), (tn, 8), (pv, 2), (ohi, 2)]) as i:
                    body(i + 1, False)
                pair_out(PAIRS - 1)

            def value_tile(j):
                act.wait_ge(vt_done, vt.add())
                nc.scalar.copy(v_n[:, :, j * P:(j + 1) * P],
                               t_bank[j % 2][:].rearrange("p (t c) -> p t c", t=TT)).then_inc(v_ready, 1)

            act.wait_ge(par_turned, 1)
            nc.scalar.copy(params[:], t_bank[0][:, 0:PARAM_ROWS]).then_inc(par_ok, 1)
            for c in range(CT):
                act.wait_ge(par_turned, c + 2)
                nc.scalar.copy(dwk[:, c, :], t_bank[(c + 1) % 2][:, 0:DEPTH * TAPS]).then_inc(par_ok, 1)
            act.wait_ge(par_ok, 1)
            for j in range(DT):
                act.wait_ge(x_turned, j + 1)
                nc.scalar.copy(x_t[:, j, :], t_bank[(j + 1) % 2][:]).then_inc(x_ready, 1)
                act.wait_ge(x_ready, j + 1)
                if j == 0:
                    act.wait_ge(acc_zero, 1)
                feed(x_t[:, j, :], params[:, j:j + 1], h_hi[:, j, :], x_sq, j, j < 2)
            act.wait_ge(angles, 2)
            nc.scalar.activation(cos_t[:], tmp[2][:], ACT.Sin).then_inc(trig, 1)
            nc.scalar.activation(sin_t[:], tmp[3][:], ACT.Sin, scale=const_sb[:, 3 * P + 1:3 * P + 2]).then_inc(trig, 1)
            act.wait_ge(raw_ready[0], rr[0].add(16))
            nc.scalar.copy(w_hi[0][:], raw[0][:]).then_inc(hi_done, 1)
            act.wait_ge(zero_ok, 3)

            with repeat(act, DEPTH, [(ev, EVENTS), (evac, TILES), (sqa, SQUARES), (stat, 6), (own, 1), (vt, 8),
                                     (mx, STEPS), (tn, STEPS), (pv, 2 * HEADS), (ohi, 2 * HEADS), (fl, 1), (kr, 1),
                                     (yr, DT), (fr, FT), (ce, CT), (cp, CT), (co, CT), *zip(rr, RING_COUNTS)]):
                root(x_std, D, 0)
                with repeat(act, 2, [(ev, 4), (evac, 4), *((r, 16) for r in rr)]):
                    for c in range(4):
                        split(c + 1)
                        evac.add()
                        if c % 2 == 0:
                            act.wait_ge(evac_done, evac.value)
                            nc.scalar.activation(tmp[1][:], tmp[0][:], ACT.Sigmoid).then_inc(sig_done, 1)
                j = 0
                for c in range(8):
                    split(9 + c)
                    if c in (0, 1, 3, 4, 5):
                        act.wait_ge(evac_done, evac.add())
                        feed(tmp[j % 2][:], par[:, R_Q + j:R_Q + j + 1], c_hi[:, j, :], lat_sq, j if j < 3 else j)
                        j += 1
                    if c == 4:
                        root(lat_std, Q_LORA, 0)
                evac.add()
                root(lat_std, KV_LORA, 0)
                act.wait_ge(forget_z, fl.add())
                nc.scalar.activation(f_sum[2 * ROPE:MISC, :], f_sum[2 * ROPE:MISC, :], ACT.Exp).then_inc(act_own, 1)
                act.wait_ge(act_own, own.add())
                nc.scalar.activation(tmp[3][2 * ROPE:MISC, :], f_sum[2 * ROPE:MISC, :], ACT.Ln, bias=1.0).then_inc(forget_l, 1)
                act.wait_ge(kr_ready, kr.add())
                nc.scalar.copy(k_t[NOPE:NOPE + ROPE, :, :],
                               tmp[0][0:ROPE, :].unsqueeze(1).broadcast_to([ROPE, HEADS, T])).then_inc(kr_put, 1)
                tile = 0
                for c in range(8):
                    split(17 + c)
                    for m in range(2):
                        evac.add()
                        if c >= 6:
                            if tile:
                                value_tile(tile - 1)
                            tile += 1
                value_tile(3)
                attention(oa_hi)
                for c in range(QKV_CH):
                    split(25 + c)
                    evac.add()
                    if c >= 9:
                        value_tile(c - 9)
                value_tile(3)
                attention(ob_hi)
                for c in range(CT):
                    act.wait_ge(centred, ce.add())
                    act.wait_ge(sq_added, sqa.value - 1)
                    sqa.add()
                    nc.scalar.activation(ln_sq[c % 2][:], c_acc[:, c, :], ACT.Square).then_inc(sq_ready, 1)
                stat.add()
                root(ln_std, CONV, 1)
                for c in range(CT):
                    act.wait_ge(conv_pre, cp.add())
                    nc.scalar.activation(tmp[c % 2][:], c_acc[:, c, :], ACT.Sigmoid).then_inc(sig_done, 1)
                    if c > 0:
                        act.wait_ge(conv_out, co.add())
                        nc.scalar.copy(oc_hi[:, c - 1, :], c_acc[:, c - 1, :]).then_inc(feed_hi, 1)
                act.wait_ge(conv_out, co.add())
                nc.scalar.copy(oc_hi[:, CT - 1, :], c_acc[:, CT - 1, :]).then_inc(feed_hi, 1)
                with repeat(act, 4, [(ev, 12), (evac, 12), (yr, 2), *((r, 48) for r in rr)]) as i:
                    for c in range(12):
                        split(36 + c + 1)
                        e, b = c // 6, c % 6
                        evac.add()
                        if b < 3:
                            act.wait_ge(evac_done, evac.value)
                            col = i * 2 + (R_BG + b * DT + e)
                            nc.scalar.activation(gate[b][:], tmp[b][:], ACT.Sigmoid,
                                                 bias=par[:, bass.ds(col, 1)]).then_inc(sig_done, 1)
                        if b == 5:
                            act.wait_ge(y_ready, yr.add())
                            nc.scalar.copy(tile_of(y_hi, i * 2 + e), y_sum[:]).then_inc(feed_hi, 1)
                with repeat(act, 2, [(ev, 4), (evac, 4), (sqa, 4), *((r, 16) for r in rr)]) as i:
                    for c in range(4):
                        split(84 + c + 1)
                        act.wait_ge(evac_done, evac.add())
                        j = i * 4 + c
                        feed(tile_of(x_t, j), par[:, bass.ds(j + R_FFN, 1)], tile_of(h_hi, j), x_sq, c)
                root(x_std, D, 0)
                with repeat(act, FT // 2, [(ev, 4), (evac, 4), (fr, 2), *((r, 16) for r in rr)]) as i:
                    for c in range(4):
                        split(92 + c + 1)
                        evac.add()
                        if c % 2 == 0:
                            act.wait_ge(evac_done, evac.value)
                            nc.scalar.activation(tmp[1][:], tmp[0][:], ACT.Sigmoid).then_inc(sig_done, 1)
                        else:
                            act.wait_ge(ff_ready, fr.add())
                            nc.scalar.copy(tile_of(f_hi, i * 2 + c // 2), tmp[2][:]).then_inc(feed_hi, 1)
                with repeat(act, 2, [(ev, 12), (evac, 4), (sqa, 4), *((r, 48) for r in rr)]) as i:
                    for c in range(12):
                        split(136 + c + 1)
                        if c % 3 == 2:
                            act.wait_ge(evac_done, evac.add())
                            j = i * 4 + c // 3
                            feed(tile_of(x_t, j), par[:, bass.ds(j + ROWS, 1)], tile_of(h_hi, j), x_sq, c // 3)
            root(x_std, D, 0)
            for j in range(DT):
                act.wait_ge(out_turned, j + 1)
                nc.scalar.copy(out_rows[:, :, j * P:(j + 1) * P],
                               t_bank[j % 2][:].rearrange("p (t c) -> p t c", t=TT)).then_inc(out_copied, 1)

        @block.vector
        def _(dve):
            hi, mm, own, taps = Count(), Count(MM_CREDIT), Count(), Count()
            sg, fh, sqr, std, score, ex, ohi, krp, vt, fl, ce, rst, stat = (Count() for _ in range(13))
            std.n, out_n = STD_CREDIT, Count(EVAC_CREDIT)
            ex.n = EXP_CREDIT

            def mine(ins):
                ins.then_inc(dve_own, 1)
                dve.wait_ge(dve_own, own.add())

            def split(i):
                size, kind = CHUNK_LIST[i % CHUNKS][:2]
                dve.wait_ge(hi_done, hi.add())
                h, last = w_hi[i % SPLIT], None
                for (to, of), (part, _) in zip(split_views(kind, size, w_lo[i % SPLIT], raw[i % RAW]),
                                               split_views(kind, size, h, raw[i % RAW])):
                    last = nc.vector.tensor_tensor(to, of, part.bitcast(F32), ALU.subtract)
                last.then_inc(lo_done, 1)

            def tile_ready():
                dve.wait_ge(mm_done, mm.add())

            def evacuated(ins):
                ins.then_inc(evac_done, 1)
                out_n.add()

            def evacuated_here():
                dve.wait_ge(evac_done, out_n.value)

            def scaled(to, b, by, rows=slice(0, P), scale=None):
                if scale is None:
                    return nc.vector.tensor_tensor(to, s_bank[b][rows, :], by[rows, :], ALU.mult)
                return nc.vector.scalar_tensor_tensor(to, s_bank[b][rows, :], scale, by[rows, :], ALU.mult, ALU.mult)

            def feed_low(src, gain, h, lo):
                dve.wait_ge(feed_hi, fh.add())
                if gain is None:
                    ins = nc.vector.tensor_tensor(lo, src, h.bitcast(F32), ALU.subtract)
                else:
                    ins = nc.vector.scalar_tensor_tensor(lo, src, gain, h.bitcast(F32), ALU.mult, ALU.subtract)
                ins.then_inc(feed_lo, 1)

            def factor(root_t, to):
                dve.wait_ge(std_ready, std.add())
                nc.vector.reciprocal(to[:], root_t[:]).then_inc(rstd_ready, 1)
                dve.wait_ge(rstd_ready, rst.add())
                passed(dve)

            def tap(c, k, first=False):
                if not first:
                    dve.wait_ge(tap_done, taps.value)
                if isinstance(k, int) and k == 0:
                    ins = nc.vector.tensor_scalar(c_acc[:, c, :], u_pad[:, c, 0:T], dwk_l[:, c, 0:1],
                                                  par[:, R_DWB + c:R_DWB + c + 1], ALU.mult, ALU.add)
                else:
                    ins = nc.vector.scalar_tensor_tensor(c_acc[:, c, :], u_pad[:, c, bass.ds(k, T)], dwk_l[:, c, bass.ds(k, 1)],
                                                         c_acc[:, c, :], ALU.mult, ALU.add)
                ins.then_inc(tap_done, 1)
                taps.add()

            def attention(hi_out, lo_out, tap0, tap_n):
                def normalise(s):
                    dve.wait_ge(exp_done, ex.add())
                    mine(nc.vector.reciprocal(row_inv[:, s % 4:s % 4 + 1], row_sum[:, s % 4:s % 4 + 1]))
                    w = (s % 4 + 1) * P
                    nc.vector.tensor_scalar(p_b[s % 2][:, 0:w], p_b[s % 2][:, 0:w], row_inv[:, s % 4:s % 4 + 1], None,
                                            ALU.mult).then_inc(norm_done, 1)

                def pair_low(pair):
                    dve.wait_ge(o_hi_done, ohi.add())
                    h = tile_of(hi_out, pair)
                    nc.vector.tensor_tensor(tile_of(lo_out, pair), o_bank[:], h.bitcast(F32), ALU.subtract).then_inc(o_lo_done, 1)

                def body(pair, first):
                    for s in range(8):
                        dve.wait_ge(score_done, score.add())
                        w = (s % 4 + 1) * P
                        nc.vector.tensor_reduce(neg_max[:, s % 4:s % 4 + 1], s_bank[s % 4][:, 0:w], AX_X, ALU.max,
                                                negate=True).then_inc(max_ready, 1)
                        if s > 0:
                            normalise(s - 1)
                        if s == 4 and not first:
                            pair_low(pair - 1)
                        if s in (1, 3, 5, 7) and (s - 1) // 2 < tap_n:
                            tap(CT - 1, pair * tap_n + (tap0 + (s - 1) // 2))
                    normalise(7)

                body(0, True)
                with repeat(dve, PAIRS - 1, [(score, 8), (ex, 8), (own, 8), (ohi, 1), (taps, tap_n)]) as i:
                    body(i + 1, False)
                pair_low(PAIRS - 1)

            dve.wait_ge(in_const, 16)
            nc.vector.tensor_copy(ident[:], const_sb[:, 0:P]).then_inc(const_ok, 1)
            nc.vector.tensor_copy(ident_b[:], const_sb[:, 0:P]).then_inc(const_ok, 1)
            nc.vector.tensor_copy(mask_b[:], const_sb[:, P:3 * P].rearrange("p (m k) -> p m k", m=2)).then_inc(const_ok, 1)
            for j in range(DT):
                feed_low(x_t[:, j, :], params[:, j:j + 1], h_hi[:, j, :], h_lo[:, j, :])
                sqr.add()
            dve.wait_ge(in_pos, 16)
            mine(nc.vector.tensor_copy(pos_f[:], pos_i[:]))
            mine(nc.vector.tensor_scalar(ang[:], pos_f[:], const_sb[:, 3 * P:3 * P + 1], None, ALU.mult))
            for shift, to in ((0.25, tmp[2]), (0.0, tmp[3])):
                k = tmp[0]
                mine(nc.vector.tensor_scalar(k[:], ang[:], 1.0 / TWO_PI, shift, ALU.mult, ALU.add))
                mine(nc.vector.tensor_scalar(k[:], k[:], ROUND, None, ALU.add))
                mine(nc.vector.tensor_scalar(k[:], k[:], -ROUND, None, ALU.add))
                mine(nc.vector.scalar_tensor_tensor(to[:], k[:], -PI_PARTS[0], ang[:], ALU.mult, ALU.add))
                mine(nc.vector.scalar_tensor_tensor(to[:], k[:], -PI_PARTS[1], to[:], ALU.mult, ALU.add))
                mine(nc.vector.scalar_tensor_tensor(to[:], k[:], -PI_PARTS[2], to[:], ALU.mult, ALU.add))
                if shift:
                    mine(nc.vector.tensor_scalar(to[:], to[:], TWO_PI / 4, None, ALU.add))
                nc.vector.tensor_scalar(to[:], to[:], PI_DOWN, -PI_DOWN, ALU.min, ALU.max).then_inc(angles, 1)
            dve.wait_ge(trig, 2)
            dve.wait_ge(in_bf, 16)
            dve.wait_ge(par_ok, 1 + CT)
            dve.wait_ge(zero_ok, 4)
            dve.wait_ge(hi_done, hi.add())
            nc.vector.tensor_tensor(w_lo[0][:], raw[0][:], w_hi[0][:].bitcast(F32), ALU.subtract).then_inc(lo_done, 1)

            with repeat(dve, DEPTH, [(hi, CHUNKS), (mm, EVENTS), (out_n, TILES), (own, OWN), (taps, CT * TAPS), (sg, 4 + 4 + 24 + 22),
                                     (fh, FEEDS), (sqr, SQUARES), (std, 5), (score, STEPS), (ex, STEPS), (ohi, HEADS),
                                     (krp, 1), (vt, 8), (fl, 1), (ce, CT), (rst, 5), (stat, 6)]) as l:
                dve.wait_ge(feed_lo, fh.value)
                nc.vector.tensor_copy(par[:], params[:, bass.ds(l * ROWS, ROWS + DT)])
                mine(nc.vector.tensor_copy(dwk_l[:], dwk[:, :, bass.ds(l * TAPS, TAPS)]))
                factor(x_std, rstd_x)
                with repeat(dve, 2, [(hi, 4), (mm, 4), (out_n, 4), (own, 2), (sg, 2)]) as i:
                    for c in range(4):
                        split(c + 1)
                        tile_ready()
                        if c % 2 == 0:
                            evacuated(scaled(tmp[0][:], c % 2, rstd_x))
                        else:
                            evacuated(scaled(tmp[2][:], c % 2, rstd_x))
                            evacuated_here()
                            dve.wait_ge(sig_done, sg.add())
                            mine(nc.vector.tensor_tensor(u_pad[:, bass.ds(i * 2 + c // 2, 1), TAPS - 1:].rearrange("p a t -> p (a t)"),
                                                         tmp[2][:], tmp[1][:], ALU.mult))
                todo = [(0, k) for k in range(TAPS)] + [(CT - 1, k) for k in range(TAPS_EARLY)]
                j = t = 0
                for c in range(8):
                    split(9 + c)
                    if c in (0, 1, 3, 4, 5):
                        tile_ready()
                        if j >= 2:
                            dve.wait_ge(sq_ready, sqr.value - 1)
                        evacuated(scaled(tmp[j % 2][:], t % 2, rstd_x))
                    elif c != 7:
                        mm.add()
                    for _ in range(LAT_TAPS[c]):
                        tap(*todo[0], first=(len(todo) == TAPS + TAPS_EARLY))
                        todo.pop(0)
                    if c in (0, 1, 3, 4, 5):
                        feed_low(tmp[j % 2][:], par[:, R_Q + j:R_Q + j + 1], c_hi[:, j, :], c_lo[:, j, :])
                        sqr.add()
                        j, t = j + 1, t + 1
                    if c == 4:
                        factor(lat_std, rstd_q)
                assert not todo
                tile_ready()
                dve.wait_ge(sq_ready, sqr.value)
                evacuated(nc.vector.tensor_tensor(tmp[2][0:MISC, :], s_bank[1][0:MISC, :], rstd_x[0:MISC, :], ALU.mult))
                evacuated_here()
                F = slice(2 * ROPE, MISC)
                mine(nc.vector.tensor_scalar(tmp[2][F, :], tmp[2][F, :], b_f[F, bass.ds(l, 1)], None, ALU.add))
                mine(nc.vector.tensor_scalar(f_sum[F, :], tmp[2][F, :], -1.0, None, ALU.mult))
                nc.vector.tensor_tensor(f_sum[F, :], f_sum[F, :], tmp[2][F, :], ALU.min).then_inc(forget_z, 1)
                mine(nc.vector.tensor_tensor(tmp[3][0:ROPE, :], tmp[2][0:ROPE, :], cos_t[0:ROPE, :], ALU.mult))
                mine(nc.vector.tensor_tensor(tmp[1][0:ROPE, :], tmp[2][ROPE:2 * ROPE, :], sin_t[ROPE:2 * ROPE, :], ALU.mult))
                nc.vector.tensor_tensor(tmp[0][0:ROPE, :], tmp[3][0:ROPE, :], tmp[1][0:ROPE, :], ALU.add).then_inc(kr_ready, 1)
                mine(nc.vector.tensor_scalar(tmp[2][F, :], tmp[2][F, :], 0.0, None, ALU.min))
                dve.wait_ge(forget_l, fl.add())
                nc.vector.tensor_tensor_scan(f_sum[F, :], tmp[3][F, :], tmp[2][F, :], 0.0, ALU.add, ALU.subtract).then_inc(cum_ready, 1)
                factor(lat_std, rstd_kv)
                dve.wait_ge(kr_put, krp.add())
                j = t = 0
                for c in range(8):
                    split(17 + c)
                    for m in range(2):
                        tile_ready()
                        tile = 2 * c + m
                        b = tile % 2
                        if c < 2:
                            for e in range(2):
                                ins = scaled(q_t[0:NOPE, 2 * tile + e, :], b, rstd_q, slice(NOPE * e, NOPE * (e + 1)), MLA_SCALE)
                            evacuated(ins)
                        elif c < 4:
                            if c == 2 and m == 0:
                                nc.vector.scalar_tensor_tensor(tmp[2][:], cos_t[:], MLA_SCALE, rstd_q[:], ALU.mult, ALU.mult)
                                mine(nc.vector.scalar_tensor_tensor(tmp[3][:], sin_t[:], MLA_SCALE, rstd_q[:], ALU.mult, ALU.mult))
                            evacuated(scaled(tmp[m][:], b, tmp[2 + m]))
                            if m == 1:
                                evacuated_here()
                                for g in range(4):
                                    rows = slice(ROPE * g, ROPE * (g + 1))
                                    ins = nc.vector.tensor_tensor(q_t[NOPE:NOPE + ROPE, 4 * (c - 2) + g, :], tmp[0][rows, :],
                                                                  tmp[1][rows, :], ALU.add)
                                mine(ins)
                        elif c < 6:
                            for e in range(2):
                                ins = scaled(k_t[0:NOPE, 2 * (tile - 8) + e, :], b, rstd_kv, slice(NOPE * e, NOPE * (e + 1)))
                            evacuated(ins)
                        else:
                            v = tile - 12
                            if v >= 2:
                                dve.wait_ge(vt_done, vt.value - 1)
                            vt.add()
                            evacuated(scaled(tmp[v % 2][:], b, rstd_kv))
                attention(oa_hi, oa_lo, TAPS_EARLY, TAPS_MLA)
                todo = [(c, k) for c in (1, 2) for k in range(TAPS)]
                for c in range(QKV_CH):
                    split(25 + c)
                    tile_ready()
                    if c < 8:
                        to = (q_t, k_t)[c // 4]
                        for e in range(2):
                            ins = scaled(to[0:NOPE, 2 * (c % 4) + e, :], c % 2, rstd_x, slice(NOPE * e, NOPE * (e + 1)),
                                         FOX_SCALE if c < 4 else None)
                        evacuated(ins)
                    else:
                        v = c - 8
                        if v >= 2:
                            dve.wait_ge(vt_done, vt.value - 1)
                        vt.add()
                        evacuated(scaled(tmp[v % 2][:], c % 2, rstd_x))
                    for _ in range(6 if c < 2 else 5):
                        tap(*todo.pop(0))
                assert not todo
                attention(ob_hi, ob_lo, TAPS_EARLY + PAIRS * TAPS_MLA, TAPS_FOX)
                dve.wait_ge(stat_done, l * 6 + 4)
                for c in range(CT):
                    nc.vector.scalar_tensor_tensor(c_acc[:, c, :], stat_bank[:], -1.0 / CONV, c_acc[:, c, :],
                                                   ALU.mult, ALU.add).then_inc(centred, 1)
                ce.add(CT)
                stat.add(6)
                factor(ln_std, tmp[2])
                sqr.add(CT)
                for c in range(CT):
                    mine(nc.vector.tensor_tensor(c_acc[:, c, :], c_acc[:, c, :], tmp[2][:], ALU.mult))
                    nc.vector.tensor_scalar(c_acc[:, c, :], c_acc[:, c, :], par[:, R_LNG + c:R_LNG + c + 1],
                                            par[:, R_LNB + c:R_LNB + c + 1], ALU.mult, ALU.add).then_inc(conv_pre, 1)
                for c in range(CT):
                    dve.wait_ge(sig_done, sg.add())
                    nc.vector.tensor_tensor(c_acc[:, c, :], c_acc[:, c, :], tmp[c % 2][:], ALU.mult).then_inc(conv_out, 1)
                    feed_low(c_acc[:, c, :], None, oc_hi[:, c, :], oc_lo[:, c, :])
                with repeat(dve, 4, [(hi, 12), (mm, 12), (out_n, 12), (own, 2), (sg, 6), (fh, 2)]) as i:
                    for c in range(12):
                        split(36 + c + 1)
                        tile_ready()
                        e, b = c // 6, c % 6
                        if b < 3:
                            evacuated(scaled(tmp[b][:], c % 2, rstd_x))
                            continue
                        dve.wait_ge(sig_done, sg.add())
                        if b == 3:
                            evacuated(scaled(y_sum[:], c % 2, gate[0]))
                        else:
                            evacuated(scaled(tmp[3][:], c % 2, gate[b - 3]))
                            evacuated_here()
                            ins = nc.vector.tensor_tensor(y_sum[:], y_sum[:], tmp[3][:], ALU.add)
                            if b == 5:
                                ins.then_inc(y_ready, 1)
                                feed_low(y_sum[:], None, tile_of(y_hi, i * 2 + e), tile_of(y_lo, i * 2 + e))
                            else:
                                mine(ins)
                with repeat(dve, 2, [(hi, 4), (mm, 4), (out_n, 4), (fh, 4), (sqr, 4)]) as i:
                    for c in range(4):
                        split(84 + c + 1)
                        tile_ready()
                        j = i * 4 + c
                        evacuated(nc.vector.tensor_tensor(tile_of(x_t, j), s_bank[c % 2][:], tile_of(x_t, j), ALU.add))
                        feed_low(tile_of(x_t, j), par[:, bass.ds(j + R_FFN, 1)], tile_of(h_hi, j), tile_of(h_lo, j))
                        sqr.add()
                factor(x_std, rstd_x)
                with repeat(dve, FT // 2, [(hi, 4), (mm, 4), (out_n, 4), (own, 2), (sg, 2), (fh, 2)]) as i:
                    for c in range(4):
                        split(92 + c + 1)
                        if c % 2 == 0:
                            tile_ready()
                            evacuated(scaled(tmp[0][:], 0, rstd_x))
                            continue
                        dve.wait_ge(sig_done, sg.add())
                        mine(nc.vector.tensor_tensor(tmp[2][:], tmp[0][:], tmp[1][:], ALU.mult))
                        tile_ready()
                        evacuated(scaled(tmp[3][:], 1, rstd_x))
                        evacuated_here()
                        nc.vector.tensor_tensor(tmp[2][:], tmp[2][:], tmp[3][:], ALU.mult).then_inc(ff_ready, 1)
                        feed_low(tmp[2][:], None, tile_of(f_hi, i * 2 + c // 2), tile_of(f_lo, i * 2 + c // 2))
                with repeat(dve, 2, [(hi, 12), (mm, 12), (out_n, 4), (fh, 4), (sqr, 4)]) as i:
                    for c in range(12):
                        split(136 + c + 1)
                        tile_ready()
                        if c % 3 == 2:
                            j = i * 4 + c // 3
                            evacuated(nc.vector.tensor_tensor(tile_of(x_t, j), s_bank[(c // 3) % 2][:], tile_of(x_t, j), ALU.add))
                            feed_low(tile_of(x_t, j), par[:, bass.ds(j + ROWS, 1)], tile_of(h_hi, j), tile_of(h_lo, j))
                            sqr.add()
            factor(x_std, rstd_x)
            for j in range(DT):
                if j >= 2:
                    dve.wait_ge(out_turned, j - 1)
                nc.vector.scalar_tensor_tensor(tmp[j % 2][:], x_t[:, j, :], params[:, DEPTH * ROWS + j:DEPTH * ROWS + j + 1],
                                               rstd_x[:], ALU.mult, ALU.mult).then_inc(out_tile, 1)

        @block.tensor
        def _(pe):
            lo, ev, fl, sqa, std = Count(RAW_CREDIT), Count(), Count(), Count(), Count(STD_CREDIT)
            st, ex, nm, to, ol, vr, taps, nt = Count(), Count(), Count(), Count(TURN_CREDIT), Count(), Count(), Count(), [0]
            pair_lo = Count(O_CREDIT)
            cumc = Count()

            def products(bank_t, rows, slot, cols, m, k_tiles, rhs, k0, first, last):
                for k in range(k_tiles):
                    w = slice(k * cols + m * P, k * cols + m * P + rows)
                    a, b = rhs(k0 + k)
                    for p, (wt, x) in enumerate(((w_hi, a), (w_hi, b), (w_lo, a))):
                        ins = nc.tensor.matmul(bank_t[0:rows, :], wt[slot][:, w], x,
                                               start=first and k == 0 and p == 0, stop=last and k == k_tiles - 1 and p == 2)
                return ins

            def chunk(i, rhs, tiles=1, k_tiles=DT, cols=P, k0=0, first=True, last=True, rows=P, between=None):
                pe.wait_ge(lo_done, lo.add())
                for m in range(tiles):
                    if first:
                        pe.wait_ge(evac_done, ev.add())
                        nt[0] += 1
                    products(s_bank[(nt[0] - 1) % 2], rows, i % SPLIT, cols, m, k_tiles, rhs, k0, first, last).then_inc(mm_done, 1)
                    if between:
                        between(m)

            h = lambda k: (h_hi[:, k, :], h_lo[:, k, :])

            def statistic(src, n_sq):
                pe.wait_ge(sq_added, sqa.add(n_sq))
                pe.wait_ge(std_ready, std.value)
                nc.tensor.matmul(stat_bank[:], ones[:], src[:], start=True, stop=True).then_inc(stat_done, 1)
                std.add()

            def turn_values(j, back):
                pe.wait_ge(evac_done, ev.value + (EVAC_CREDIT - back))
                if j >= 2:
                    pe.wait_ge(v_ready, vr.value - 1)
                vr.add()
                for t in range(TT):
                    ins = nc.tensor.transpose(t_bank[j % 2][:, t * P:(t + 1) * P], tmp[j % 2][:, t * P:(t + 1) * P], ident[:])
                ins.then_inc(vt_done, 1)

            def attention(rows, kind):
                def logits(pair, s):
                    e, q = s // 4, s % 4
                    pe.wait_ge(exp_done, ex.add())
                    if q == 0:
                        pe.wait_ge(st_ready, st.value + 1 + 2 * e)
                    w = (q + 1) * P
                    nc.tensor.matmul(s_bank[q][:, 0:w], q_st[e][0:rows, q * P:w], head_of(k_t, pair, e)[0:rows, 0:w],
                                     start=True, stop=True)
                    nc.tensor.matmul(s_bank[q][:, q * P:w], ident_b[:], mask_b[:, kind, :], start=False, stop=True,
                                     skip_group_check=True).then_inc(score_done, 1)

                def turn(s):
                    pe.wait_ge(norm_done, nm.add())
                    pe.wait_ge(turn_out, to.value - 1)
                    to.add()
                    for k in range(s % 4 + 1):
                        ins = nc.tensor.transpose(t_bank[s % 2][:, k * P:(k + 1) * P], p_b[s % 2][:, k * P:(k + 1) * P], ident[:])
                    ins.then_inc(turn_done, 1)

                def values(e):
                    if e == 0:
                        pe.wait_ge(o_lo_done, pair_lo.value)
                        pe.wait_ge(st_ready, st.value + 2)
                    pe.wait_ge(turn_out, to.value)
                    for k in range(TT):
                        ins = nc.tensor.matmul(o_bank[e * VDIM:(e + 1) * VDIM, k * P:T], v_st[:, k, e * VDIM:(e + 1) * VDIM],
                                               p_t[:, k, k * P:T], start=(k == 0), stop=True, skip_group_check=True)
                    ins.then_inc(pv_done, 1)

                def body(pair, last):
                    for s in range(8):
                        if s < 6:
                            logits(pair, s + 2)
                        else:
                            if s == 6:
                                st.add(3)
                            if not last:
                                logits(pair + 1, s - 6)
                        if s == 4:
                            values(0)
                        turn(s)
                    values(1)
                    pair_lo.add()

                logits(0, 0)
                logits(0, 1)
                with repeat(pe, PAIRS - 1, [(st, 3), (ex, 8), (nm, 8), (to, 8), (pair_lo, 1)]) as i:
                    body(i, False)
                body(PAIRS - 1, True)

            pe.wait_ge(const_ok, 3)
            pe.wait_ge(in_par, 16 * (8 * DEPTH + 1))
            nc.tensor.transpose(t_bank[0][:, 0:PARAM_ROWS], par_rows[0:PARAM_ROWS, :], ident[0:PARAM_ROWS, 0:PARAM_ROWS]).then_inc(par_turned, 1)
            pe.wait_ge(in_dw, 16)
            R = DEPTH * TAPS
            for c in range(CT):
                if c >= 1:
                    pe.wait_ge(par_ok, c)
                nc.tensor.transpose(t_bank[(c + 1) % 2][:, 0:R], dw_rows[0:R, c * P:(c + 1) * P], ident[0:R, 0:R]).then_inc(par_turned, 1)
            pe.wait_ge(in_x, 16 * TT)
            for j in range(DT):
                pe.wait_ge(par_ok, CT if j == 0 else 1 + CT)
                if j >= 2:
                    pe.wait_ge(x_ready, j - 1)
                for t in range(TT):
                    ins = nc.tensor.transpose(t_bank[(j + 1) % 2][:, t * P:(t + 1) * P], x_rows[:, t, j * P:(j + 1) * P], ident[:])
                ins.then_inc(x_turned, 1)
            fl.add(DT)
            pe.wait_ge(zero_ok, 1)

            with repeat(pe, DEPTH, [(lo, CHUNKS), (ev, TILES), (fl, FEEDS), (sqa, SQUARES), (std, 5), (st, 3 * HEADS), (ex, STEPS),
                                    (nm, STEPS), (to, STEPS), (pair_lo, HEADS), (vr, 8), (taps, CT * TAPS), (cumc, 16)]):
                pe.wait_ge(feed_lo, fl.value)
                statistic(x_acc, DT)
                with repeat(pe, 2, [(lo, 4), (ev, 4)]):
                    for c in range(4):
                        chunk(c, h)
                chunk(8, h)
                chunk(9, h)
                chunk(10, h, k_tiles=4, last=False)
                chunk(11, h, k_tiles=4, k0=4, first=False)
                chunk(12, h)
                statistic(lat_acc, 3)
                chunk(13, h)
                chunk(14, h, k_tiles=4, cols=MISC, rows=MISC, last=False)
                chunk(15, h, k_tiles=4, k0=4, cols=MISC, rows=MISC, first=False)
                statistic(lat_acc, 2)
                pe.wait_ge(feed_lo, fl.add(5))
                cq = lambda k: (c_hi[:, k, :], c_lo[:, k, :])
                ckv = lambda k: (c_hi[:, 3 + k, :], c_lo[:, 3 + k, :])
                for c in range(4):
                    chunk(16 + c, cq, tiles=2, k_tiles=3, cols=2 * P)
                for c in range(2):
                    chunk(20 + c, ckv, tiles=2, k_tiles=2, cols=2 * P)
                chunk(22, ckv, tiles=2, k_tiles=2, cols=2 * P, between=lambda m: turn_values(0, 1) if m == 1 else None)
                chunk(23, ckv, tiles=2, k_tiles=2, cols=2 * P, between=lambda m: turn_values(1 + m, 1))
                turn_values(3, 0)
                pe.wait_ge(evac_done, ev.value + EVAC_CREDIT)
                attention(NOPE + ROPE, 0)
                pe.wait_ge(exp_done, ex.value + EXP_CREDIT)
                for c in range(QKV_CH):
                    chunk(24 + c, h)
                    if c >= 9:
                        turn_values(c - 9, 1)
                turn_values(3, 0)
                pe.wait_ge(evac_done, ev.value + EVAC_CREDIT)
                pe.wait_ge(cum_put, cumc.add(16))
                attention(NOPE + 1, 1)
                pe.wait_ge(exp_done, ex.value + EXP_CREDIT)
                pe.wait_ge(tap_done, taps.add(CT * TAPS))
                for c in range(CT):
                    ins = nc.tensor.matmul(stat_bank[:], ones[:], c_acc[:, c, :], start=(c == 0), stop=(c == CT - 1))
                ins.then_inc(stat_done, 1)
                statistic(ln_acc, CT)
                pe.wait_ge(feed_lo, fl.add(CT))
                pe.wait_ge(o_lo_done, pair_lo.value)
                passed(pe)
                outs = [lambda k, a=a, b=b: (a[:, k, :], b[:, k, :]) for a, b in ((oa_hi, oa_lo), (ob_hi, ob_lo), (oc_hi, oc_lo))]
                with repeat(pe, 4, [(lo, 12), (ev, 12)]):
                    for c in range(12):
                        b = c % 6
                        if b < 3:
                            chunk(36 + c, h)
                        else:
                            chunk(36 + c, outs[b - 3], k_tiles=4)
                pe.wait_ge(feed_lo, fl.add(DT))
                passed(pe)
                y = lambda k: (y_hi[:, k, :], y_lo[:, k, :])
                with repeat(pe, 2, [(lo, 4), (ev, 4)]):
                    for c in range(4):
                        chunk(84 + c, y)
                pe.wait_ge(feed_lo, fl.add(DT))
                statistic(x_acc, DT)
                with repeat(pe, FT // 2, [(lo, 4), (ev, 4)]):
                    for c in range(4):
                        chunk(92 + c, h)
                pe.wait_ge(feed_lo, fl.add(FT))
                passed(pe)
                f = lambda k: (f_hi[:, k, :], f_lo[:, k, :])
                with repeat(pe, 2, [(lo, 12), (ev, 4)]):
                    for c in range(12):
                        b = c % 3
                        chunk(136 + c, f, k_tiles=DOWN_K[b], k0=8 * b, first=(b == 0), last=(b == 2))
                fl.add(DT)
            pe.wait_ge(feed_lo, fl.value)
            statistic(x_acc, DT)
            for j in range(DT):
                pe.wait_ge(out_tile, j + 1)
                if j >= 2:
                    pe.wait_ge(out_copied, j - 1)
                for t in range(TT):
                    ins = nc.tensor.transpose(t_bank[j % 2][:, t * P:(t + 1) * P], tmp[j % 2][:, t * P:(t + 1) * P], ident[:])
                ins.then_inc(out_turned, 1)


def kernel(**inputs):
    import concourse.bacc as bacc
    from concourse.bass_utils import run_bass_kernel_spmd

    shapes = {
        "x": (T, D), "positions": (1, T), "norm_mix_g": (DEPTH, D), "w_in": (DEPTH * D, IN_WIDTH),
        "b_gate": (DEPTH, 3 * D), "q_norm_g": (DEPTH, Q_LORA), "w_uq": (DEPTH * Q_LORA, HEADS * (NOPE + ROPE)),
        "kv_norm_g": (DEPTH, KV_LORA), "w_ukv": (DEPTH * KV_LORA, HEADS * (NOPE + VDIM)), "b_forget": (DEPTH, HEADS),
        "dw_kernel": (DEPTH * TAPS, CONV), "dw_bias": (DEPTH, CONV), "conv_ln_g": (DEPTH, CONV), "conv_ln_b": (DEPTH, CONV),
        "w_bo_a": (DEPTH * 512, D), "w_bo_b": (DEPTH * 512, D), "w_bo_c": (DEPTH * CONV, D), "w_out": (DEPTH * D, D),
        "norm_ffn_g": (DEPTH, D), "w_ffn_gate": (DEPTH * D, FFN), "w_ffn_up": (DEPTH * D, FFN),
        "w_ffn_down": (DEPTH * FFN, D), "final_norm_g": (D,),
    }
    consts = np.zeros((P, 3 * P + 2), np.float32)
    q, k = np.arange(P)[:, None], np.arange(P)[None, :]
    consts[:, 0:P] = q == k
    consts[:, P:2 * P] = np.where(q // CHUNK_MASK >= k // CHUNK_MASK, 0, MASKED)
    consts[:, 2 * P:3 * P] = np.where(q >= k, 0, MASKED)
    freq = np.float32(1) / np.float32(THETA) ** (np.arange(0, ROPE, 2, dtype=np.float32) / np.float32(ROPE))
    consts[:, 3 * P] = freq[np.arange(P) % (ROPE // 2)]
    consts[:, 3 * P + 1] = np.where(np.arange(P) % ROPE < ROPE // 2, -1, 1)

    nc = bacc.Bacc("TRN2", target_bir_lowering=False, num_devices=1)
    arrays, dram = {}, {}
    for name, shape in shapes.items():
        arrays["in_" + name] = np.ascontiguousarray(inputs[name]).reshape(shape)
    arrays["in_consts"] = consts
    for name, a in arrays.items():
        dram[name[3:]] = nc.dram_tensor(name, a.shape, mybir.dt.from_np(a.dtype), kind="ExternalInput").ap()
    out = nc.dram_tensor("out_x", (T, D), F32, kind="ExternalOutput").ap()
    trunk(nc, dram, out)
    r = run_bass_kernel_spmd(nc, [arrays], core_ids=[0])
    return r.results[0]["out_x"].reshape(1, T, D)
```

```python
from contextlib import ExitStack, contextmanager

import numpy as np

import concourse.bass as bass
from concourse import mybir

F32 = mybir.dt.float32
F32R = mybir.dt.float32r
BF16 = mybir.dt.bfloat16
I32 = mybir.dt.int32
ALU = mybir.AluOpType
ACT = mybir.ActivationFunctionType
AX_X = mybir.AxisListType.X

P = 128
DEPTH, D, T = 2, 1024, 512
DT = D // P
TT = T // P
Q_LORA, KV_LORA = 384, 256
NOPE, ROPE, VDIM, HEADS = 64, 32, 64, 8
PAIRS = HEADS // 2
CONV, TAPS = 512, 31
CT = CONV // P
FFN = 2816
FT = FFN // P
THETA = 10000.0
RMS_EPS, LN_EPS = 1e-6, 1e-5
MLA_SCALE = (NOPE + ROPE) ** -0.5
FOX_SCALE = NOPE ** -0.5
CHUNK_MASK = 64
MASKED = -1e30

C_Q = 0
C_KV = C_Q + Q_LORA
C_KR = C_KV + KV_LORA
C_QB = C_KR + ROPE
C_KB = C_QB + HEADS * NOPE
C_VB = C_KB + HEADS * NOPE
C_F = C_VB + HEADS * NOPE
C_CONV = C_F + HEADS
C_GATE = C_CONV + 2 * CONV
IN_WIDTH = C_GATE + 3 * D

R_MIX, R_FFN, R_BG, R_Q, R_KV, R_DWB, R_LNG, R_LNB = 0, 8, 16, 40, 43, 45, 49, 53
ROWS = 57
PARAM_ROWS = DEPTH * ROWS + DT
MISC = 2 * ROPE + HEADS

CONV_CH, LAT_CH, UP_CH, QKV_CH, MERGE_CH, OUT_CH, FFN_CH, DOWN_CH = 8, 8, 8, 12, 48, 8, 44, 24
CHUNKS = CONV_CH + LAT_CH + UP_CH + QKV_CH + MERGE_CH + OUT_CH + FFN_CH + DOWN_CH
TILES = 8 + 6 + 16 + 12 + 48 + 8 + 44 + 8
EVENTS = 8 + 8 + 16 + 12 + 48 + 8 + 44 + 24
BANKS = 4
STEPS = 2 * HEADS * TT
RAW, SPLIT = 4, 2
DOWN_K = (8, 8, 6)

RAW_CREDIT, EVAC_CREDIT, EXP_CREDIT, TURN_CREDIT, O_CREDIT, STD_CREDIT = RAW, BANKS, BANKS, 2, 1, 1

LAT_TAPS = (2, 2, 2, 2, 2, 3, 2, 0)
PAIR_TAPS = 4
QKV_TAPS = (4,) + (3,) * 11
LN_TURNS = 3
PASS1_TAPS = ((1, 2), (2, 6))
PASS1_TURNS = D // P - LN_TURNS
assert sum(LAT_TAPS) + PAIRS * PAIR_TAPS == TAPS
TAP1_FOX = sum(QKV_TAPS) - TAPS - 1
TAP1_MERGE = TAP1_FOX + PAIRS * PAIR_TAPS
assert TAP1_MERGE + PASS1_TURNS * 2 == TAPS and 1 + PASS1_TURNS * 6 == TAPS
P_AT = (0, P, 3 * P, 6 * P)


CHUNK_LIST = (
    [(1024, None, 1, 1)] * 8
    + [(1024, None, 1, 1)] * 2 + [(512, None, 1, 1)] * 2 + [(1024, None, 1, 1)] * 2 + [(0, "misc", 1, 2)] * 2
    + [(768, None, 2, 3)] * 2 + [(0, "rope", 2, 3)] * 2 + [(512, None, 2, 2)] * 4
    + [(1024, None, 1, 1)] * 12
    + ([(1024, None, 1, 1)] * 2 + [(512, None, 1, 1)] * 2) * 12
    + [(1024, None, 1, 1)] * 8
    + [(1024, None, 1, 1)] * 44
    + [(P * k, None, 1, 1) for k in DOWN_K] * 8
)
assert len(CHUNK_LIST) == CHUNKS and sum(c[2] for c in CHUNK_LIST) == EVENTS
RING_COUNTS = [16 * sum(c[3] for c in CHUNK_LIST[i::RAW]) for i in range(RAW)]
SQUARES, FEEDS = 5 + CT + 2 * DT, 5 + CT + DT + DT + FT + DT
LAT, UP, QKV, MERGE, MERGE2, OUT, FF, DOWN = 8, 16, 24, 36, 68, 84, 92, 136
OWN = 1 + 4 + 5 + 3 + STEPS + DT + 1 + FT

TWO_PI = 2 * np.pi
ROUND = 1.5 * 2.0 ** 23
PI_PARTS = (6.28125, 4058 / 2.0 ** 21, 3.0199160e-7)
PI_DOWN = 3.1415925


def split_views(kind, size, to, of):
    H = ROPE // 2
    if kind == "misc":
        a = of[:, 0:4 * (ROPE + HEADS)].rearrange("p (k c) -> p k c", k=4)
        b = to[:, 0:4 * MISC].rearrange("p (k c) -> p k c", k=4)
        return [(b[:, :, 0:ROPE], a[:, :, 0:ROPE]), (b[:, :, ROPE:ROPE + H], a[:, :, H:ROPE]),
                (b[:, :, ROPE + H:2 * ROPE], a[:, :, 0:H]), (b[:, :, 2 * ROPE:MISC], a[:, :, ROPE:ROPE + HEADS])]
    if kind == "rope":
        a = of[:, 0:3 * P].rearrange("p (k g c) -> p k g c", k=3, c=ROPE)
        b = to[:, 0:6 * P].rearrange("p (k s g c) -> p k s g c", k=3, s=2, c=ROPE)
        straight = [(b[:, k, 0], a[:, k]) for k in range(3)]
        return straight + [x for k in range(3) for x in ((b[:, k, 1, :, 0:H], a[:, k, :, H:ROPE]),
                                                         (b[:, k, 1, :, H:ROPE], a[:, k, :, 0:H]))]
    return [(to[:, 0:size], of[:, 0:size])]


def tile_of(t, j):
    return t[:, bass.ds(j, 1), :].rearrange("p a t -> p (a t)")


def head_of(t, pair, e):
    return t[:, bass.ds(pair * 2 + e, 1), :].rearrange("p a t -> p (a t)")


class Count:

    def __init__(self, start=0):
        self.n, self.dyn = start, 0

    def add(self, by=1):
        self.n += by
        return self.value

    @property
    def value(self):
        return self.dyn + self.n


@contextmanager
def repeat(eng, times, per):
    with eng.Fori(0, times) as i:
        old = [(c, c.n, c.dyn) for c, _ in per]
        for c, by in per:
            if by:
                c.dyn = c.dyn + i * by
        yield i
        for (c, by), (_, n, _) in zip(per, old):
            assert c.n - n == by, f"a turn adds {c.n - n}, not {by} ({[k for k, (q, _) in enumerate(per) if q is c]})"
        for (c, by), (_, n, dyn) in zip(per, old):
            c.n, c.dyn = n + by * times, dyn


def trunk(nc, dram, out):
    KB = 1024
    base = nc.sbuf_base + (-nc.sbuf_base) % 64
    free = [base]

    def at(name, off, shape, dt=F32):
        return nc.alloc_sbuf_tensor_at(name, shape, dt, offset=off)

    def sb(name, shape, dt=F32):
        size = int(np.prod(shape[1:])) * (2 if dt == BF16 else 4)
        t = at(name, free[0], shape, dt)
        free[0] += size + (-size) % 32
        assert free[0] <= nc.sbuf_usable_end, (name, free[0] - nc.sbuf_usable_end)
        return t

    x_t = sb("x_t", [P, DT, T])
    h_hi = sb("h_hi", [P, DT, T], F32R)
    h_lo = sb("h_lo", [P, DT, T], F32R)
    raw = [sb(f"raw{i}", [P, 1024]) for i in range(RAW)]
    w_hi = [sb(f"w_hi{i}", [P, 1024], F32R) for i in range(SPLIT)]
    w_lo = [sb(f"w_lo{i}", [P, 1024], F32R) for i in range(SPLIT)]
    rstd_x = sb("rstd_x", [P, T])
    cos_t = sb("cos_t", [P, T])
    sin_t = sb("sin_t", [P, T])
    tmp = [sb(f"tmp{i}", [P, T]) for i in range(4)]
    v_st = sb("v_st", [P, TT, P])
    u_pad = sb("u_pad", [P, CT, TAPS - 1 + T])
    c_off = free[0]
    c_acc = sb("c_acc", [P, CT, T])
    ones = sb("ones", [P, P])
    ident = sb("ident", [P, P])
    ident_b = sb("ident_b", [P, P], BF16)
    mask_b = sb("mask_b", [P, 2, P], BF16)
    params = sb("params", [P, PARAM_ROWS])
    par = sb("par", [P, ROWS + DT])
    dwk = sb("dwk", [P, CT, DEPTH * TAPS])
    dwk_l = sb("dwk_l", [P, CT, TAPS])
    b_f = sb("b_f", [P, DEPTH])
    eps_t = sb("eps_t", [P, 2])
    neg_max = sb("neg_max", [P, 4])
    row_sum = sb("row_sum", [P, 4])
    row_inv = sb("row_inv", [P, 4])
    f_sum = sb("f_sum", [P, T])
    r0 = free[0]
    free[0] += 89 * KB
    assert free[0] <= nc.sbuf_usable_end, free[0] - nc.sbuf_usable_end
    q_t = at("q_t", r0, [P, HEADS, T])
    k_t = at("k_t", r0 + 16 * KB, [P, HEADS, T])
    v_n = at("v_n", r0 + 32 * KB, [P, TT, HEADS * VDIM])
    oa_hi = at("oa_hi", r0 + 40 * KB, [P, PAIRS, T], F32R)
    oa_lo = at("oa_lo", r0 + 48 * KB, [P, PAIRS, T], F32R)
    ob_hi = at("ob_hi", r0 + 56 * KB, [P, PAIRS, T], F32R)
    ob_lo = at("ob_lo", r0 + 64 * KB, [P, PAIRS, T], F32R)
    p_b = at("p_b", r0 + 72 * KB, [P, 10 * P])
    p_t = at("p_t", r0 + 77 * KB, [P, TT, T])
    q_st = [at(f"q_st{i}", r0 + (85 + 2 * i) * KB, [P, T]) for i in range(2)]
    c_hi = at("c_hi", r0 + 40 * KB, [P, 5, T], F32R)
    c_lo = at("c_lo", r0 + 50 * KB, [P, 5, T], F32R)
    rstd_q = at("rstd_q", r0 + 60 * KB, [P, T])
    rstd_kv = at("rstd_kv", r0 + 62 * KB, [P, T])
    lat_sq = [at(f"lat_sq{i}", r0 + (64 + 2 * i) * KB, [P, T]) for i in range(2)]
    lat_acc = at("lat_acc", r0 + 68 * KB, [P, T])
    lat_std = at("lat_std", r0 + 70 * KB, [P, T])
    x_sq = [at(f"x_sq{i}", c_off + 2 * i * KB, [P, T]) for i in range(2)]
    x_acc = at("x_acc", c_off + 4 * KB, [P, T])
    x_std = at("x_std", c_off + 6 * KB, [P, T])
    ln_sq = [at(f"ln_sq{i}", r0 + 2 * i * KB, [P, T]) for i in range(2)]
    ln_acc = at("ln_acc", r0 + 4 * KB, [P, T])
    ln_std = at("ln_std", r0 + 6 * KB, [P, T])
    ln_rstd = ln_acc
    ln_sig = at("ln_sig", r0 + 8 * KB, [P, CT, T])
    oc_hi = at("oc_hi", r0 + 73 * KB, [P, CT, T], F32R)
    oc_lo = at("oc_lo", r0 + 81 * KB, [P, CT, T], F32R)
    gate = [at(f"gate{i}", r0 + (32 + 2 * i) * KB, [P, T]) for i in range(2)]
    y_sum = [at(f"y_sum{i}", r0 + (36 + 2 * i) * KB, [P, T]) for i in range(2)]
    y_hi = at("y_hi", r0, [P, DT, T], F32R)
    y_ab = at("y_ab", r0 + 16 * KB, [P, DT, T])
    y_lo = at("y_lo", r0 + 16 * KB, [P, DT, T], F32R)
    f_hi = at("f_hi", r0, [P, FT, T], F32R)
    f_lo = at("f_lo", r0 + 44 * KB, [P, FT, T], F32R)
    x_rows = at("x_rows", r0, [P, TT, D])
    out_rows = at("out_rows", r0, [P, TT, D])
    par_rows = at("par_rows", r0 + 16 * KB, [P, P])
    dw_rows = at("dw_rows", r0 + 17 * KB, [P, CONV])
    const_sb = at("const_sb", r0 + 20 * KB, [P, 3 * P + 2])
    pos_i = at("pos_i", r0 + 22 * KB, [P, T], I32)
    pos_f = at("pos_f", r0 + 24 * KB, [P, T])
    ang = at("ang", r0 + 26 * KB, [P, T])

    with ExitStack() as ctx:
        bank = [ctx.enter_context(nc.psum_tensor(f"bank{i}", [P, 512], F32)) for i in range(8)]
        s_bank, t_bank, o_bank, stat_bank = bank[0:4], bank[4:6], bank[6], bank[7]

        def sem(name):
            return ctx.enter_context(nc.semaphore(name))

        raw_ready = [sem(f"raw_ready{i}") for i in range(RAW)]
        hi_done = sem("hi_done")
        lo_done = sem("lo_done")
        mm_done = sem("mm_done")
        evac_done = sem("evac_done")
        x_ready = sem("x_ready")
        feed_hi = sem("feed_hi")
        feed_lo = sem("feed_lo")
        sq_ready = sem("sq_ready")
        sq_added = sem("sq_added")
        acc_zero = sem("acc_zero")
        stat_done = sem("stat_done")
        std_ready = sem("std_ready")
        rstd_ready = sem("rstd_ready")
        sig_done = sem("sig_done")
        act_own = sem("act_own")
        dve_own = sem("dve_own")
        forget_z = sem("forget_z")
        forget_l = sem("forget_l")
        cum_ready = sem("cum_ready")
        cum_put = sem("cum_put")
        kr_ready = sem("kr_ready")
        kr_put = sem("kr_put")
        vt_done = sem("vt_done")
        v_ready = sem("v_ready")
        st_ready = sem("st_ready")
        ones_put = sem("ones_put")
        score_done = sem("score_done")
        max_ready = sem("max_ready")
        exp_done = sem("exp_done")
        norm_done = sem("norm_done")
        turn_done = sem("turn_done")
        turn_out = sem("turn_out")
        pv_done = sem("pv_done")
        o_hi_done = sem("o_hi_done")
        o_lo_done = sem("o_lo_done")
        tap_done = sem("tap_done")
        centred = sem("centred")
        conv_pre = sem("conv_pre")
        conv_out = sem("conv_out")
        y_ready = sem("y_ready")
        ff_ready = sem("ff_ready")
        out_tile = sem("out_tile")
        out_turned = sem("out_turned")
        out_copied = sem("out_copied")
        put_done = sem("put_done")
        in_x = sem("in_x")
        in_par = sem("in_par")
        in_dw = sem("in_dw")
        in_const = sem("in_const")
        in_pos = sem("in_pos")
        in_bf = sem("in_bf")
        const_ok = sem("const_ok")
        par_turned = sem("par_turned")
        par_ok = sem("par_ok")
        x_turned = sem("x_turned")
        angles = sem("angles")
        trig = sem("trig")
        wait_held = sem("wait_held")
        zero_ok = sem("zero_ok")

        def passed(eng):
            eng.sem_inc(wait_held, 1)

        block = ctx.enter_context(nc.Block())

        @block.sync
        def _(sp):
            n = [0]
            freed = Count()

            def load(*parts):
                slot = n[0] % RAW
                sp.wait_ge(lo_done, freed.add())
                for to, src in parts:
                    sp.dma_start(to(raw[slot]), src).then_inc(raw_ready[slot], 16)
                n[0] += 1

            def block_of(w, row, k_tiles, col):
                src = w[bass.ds(row, k_tiles * P), bass.ds(col, P)].rearrange("(k p) c -> p k c", p=P)
                load((lambda r: r[:, 0:k_tiles * P].rearrange("p (k c) -> p k c", k=k_tiles), src))

            w_in, w_out, w_gate, w_up, w_down = (dram[k] for k in ("w_in", "w_out", "w_ffn_gate", "w_ffn_up", "w_ffn_down"))
            w_bo = [dram[k] for k in ("w_bo_a", "w_bo_b", "w_bo_c")]

            sp.dma_start(pos_i[:], dram["positions"].broadcast_to([P, T])).then_inc(in_pos, 16)
            sp.dma_start(const_sb[:], dram["consts"]).then_inc(in_const, 16)
            for t in range(TT):
                sp.dma_start(x_rows[:, t, :], dram["x"][t * P:(t + 1) * P, :]).then_inc(in_x, 16)

            with repeat(sp, DEPTH, [(freed, CHUNKS)]) as l:
                row = l * D
                with repeat(sp, 2, [(freed, 4)]) as i:
                    for e in range(2):
                        block_of(w_in, row, DT, i * (2 * P) + (C_CONV + CONV + e * P))
                        block_of(w_in, row, DT, i * (2 * P) + (C_CONV + e * P))
                block_of(w_in, row, DT, C_Q)
                block_of(w_in, row, DT, C_Q + P)
                block_of(w_in, row, 4, C_Q + 2 * P)
                block_of(w_in, row + 4 * P, 4, C_Q + 2 * P)
                block_of(w_in, row, DT, C_KV)
                block_of(w_in, row, DT, C_KV + P)
                with nc.allow_non_contiguous_dma("narrow columns"):
                    for half in range(2):
                        rows = w_in[bass.ds(row + half * 4 * P, 4 * P), :]
                        view = lambda r, a, b: r[:, 0:4 * (ROPE + HEADS)].rearrange("p (k c) -> p k c", k=4)[:, :, a:b]
                        load((lambda r: view(r, 0, ROPE), rows[:, C_KR:C_KR + ROPE].rearrange("(k p) c -> p k c", p=P)),
                             (lambda r: view(r, ROPE, ROPE + HEADS), rows[:, C_F:C_F + HEADS].rearrange("(k p) c -> p k c", p=P)))
                def heads_of(w, row, k_tiles, width, col, cols, b):
                    parts = []
                    for k in range(k_tiles):
                        src = w[bass.ds(row + k * P, P), 4 * b * width:(4 * b + 4) * width].rearrange("p (h c) -> p h c", c=width)
                        to = lambda r, k=k: r[:, 4 * cols * k:4 * cols * (k + 1)].rearrange("p (h c) -> p h c", h=4)
                        parts.append((to, src[:, :, col:col + cols]))
                    load(*parts)

                for b in range(2):
                    heads_of(dram["w_uq"], l * Q_LORA, 3, NOPE + ROPE, 0, NOPE, b)
                for b in range(2):
                    heads_of(dram["w_uq"], l * Q_LORA, 3, NOPE + ROPE, NOPE, ROPE, b)
                for part in (0, NOPE):
                    for b in range(2):
                        heads_of(dram["w_ukv"], l * KV_LORA, 2, NOPE + VDIM, part, NOPE, b)
                for i in range(QKV_CH):
                    block_of(w_in, row, DT, C_QB + i * P)
                    if i == 3:
                        sp.wait_ge(cum_ready, l + 1)
                        sp.wait_ge(score_done, l * STEPS + STEPS // 2)
                        sp.dma_start(k_t[NOPE:NOPE + 1, :, :], f_sum[2 * ROPE:MISC, :]).then_inc(cum_put, 16)
                with repeat(sp, DT, [(freed, 4)]) as i:
                    for b in range(2):
                        block_of(w_in, row, DT, i * P + (C_GATE + b * D))
                    for b in range(2):
                        block_of(w_bo[b], l * 512, 4, i * P)
                with repeat(sp, DT // 2, [(freed, 4)]) as i:
                    for e in range(2):
                        block_of(w_in, row, DT, i * (2 * P) + (C_GATE + 2 * D + e * P))
                    for e in range(2):
                        block_of(w_bo[2], l * 512, 4, i * (2 * P) + e * P)
                with repeat(sp, 2, [(freed, 4)]) as i:
                    for e in range(4):
                        block_of(w_out, row, DT, i * (4 * P) + e * P)
                with repeat(sp, FT // 2, [(freed, 4)]) as i:
                    for e in range(2):
                        block_of(w_gate, row, DT, i * (2 * P) + e * P)
                        block_of(w_up, row, DT, i * (2 * P) + e * P)
                with repeat(sp, 2, [(freed, 12)]) as i:
                    for e in range(4):
                        for b in range(3):
                            block_of(w_down, l * FFN + 8 * b * P, DOWN_K[b], i * (4 * P) + e * P)
            block_of(w_in, 0, DT, C_CONV + CONV)
            block_of(w_in, 0, DT, C_CONV)

            sp.wait_ge(out_copied, DT)
            for t in range(TT):
                sp.dma_start(out[t * P:(t + 1) * P, :], out_rows[:, t, :]).then_inc(put_done, 16)
            sp.wait_ge(put_done, 16 * TT)

        @block.gpsimd
        def _(pool):
            sq, zero, stat = Count(), Count(), Count()
            score, pv, evac, vr, fed, op = Count(), Count(), Count(EVAC_CREDIT), Count(), Count(DT), Count()

            def clear(acc):
                nc.gpsimd.memset(acc[:], 0.0).then_inc(acc_zero, 1)
                pool.wait_ge(acc_zero, zero.add())

            def add_square(acc, ring, i):
                pool.wait_ge(sq_ready, sq.add())
                nc.gpsimd.tensor_tensor(acc[:], acc[:], ring[i % 2][:], ALU.add).then_inc(sq_added, 1)
                pool.wait_ge(sq_added, sq.value)

            def attention(rows):
                pool.wait_ge(evac_done, evac.value)
                passed(pool)

                def stage(pair, first):
                    for e in range(2):
                        if not first:
                            pool.wait_ge(score_done, score.value - 4 + 4 * e)
                            passed(pool)
                        nc.gpsimd.tensor_copy(q_st[e][0:rows, :], head_of(q_t, pair, e)[0:rows, :]).then_inc(st_ready, 1)
                    if first:
                        pool.wait_ge(v_ready, vr.add(4))
                    else:
                        pool.wait_ge(pv_done, pv.value)
                    passed(pool)
                    nc.gpsimd.tensor_copy(v_st[:], v_n[:, :, bass.ds(pair * P, P)]).then_inc(st_ready, 1)
                    score.add(8)
                    pv.add(2)

                stage(0, True)
                with repeat(pool, PAIRS - 1, [(score, 8), (pv, 2)]) as i:
                    stage(i + 1, False)

            for s, credit in ((lo_done, RAW_CREDIT), (evac_done, EVAC_CREDIT), (exp_done, EXP_CREDIT),
                              (turn_out, TURN_CREDIT), (o_lo_done, O_CREDIT), (std_ready, STD_CREDIT)):
                pool.sem_inc(s, credit)
            nc.gpsimd.memset(ones[:], 1.0).then_inc(zero_ok, 1)
            nc.gpsimd.memset(eps_t[:, 0:1], RMS_EPS).then_inc(zero_ok, 1)
            nc.gpsimd.memset(eps_t[:, 1:2], LN_EPS).then_inc(zero_ok, 1)
            nc.gpsimd.memset(u_pad[:, :, 0:TAPS - 1], 0.0).then_inc(zero_ok, 1)
            clear(x_acc)
            for j in range(DT):
                add_square(x_acc, x_sq, j)
            with repeat(pool, DEPTH, [(sq, SQUARES), (zero, 5), (stat, 6), (score, STEPS), (pv, 2 * HEADS),
                                      (evac, TILES), (vr, 8), (fed, FEEDS), (op, 2)]):
                pool.wait_ge(stat_done, stat.add())
                passed(pool)
                clear(lat_acc)
                for j in range(3):
                    add_square(lat_acc, lat_sq, j)
                pool.wait_ge(stat_done, stat.add())
                passed(pool)
                clear(lat_acc)
                for j in range(2):
                    add_square(lat_acc, lat_sq, j + 1)
                stat.add()
                evac.add(26)
                attention(NOPE + ROPE)
                pool.wait_ge(score_done, score.value)
                pool.wait_ge(pv_done, pv.value)
                passed(pool)
                for e in range(2):
                    nc.gpsimd.memset(q_st[e][NOPE:NOPE + 1, :], 1.0).then_inc(ones_put, 1)
                pool.wait_ge(ones_put, op.add(2))
                evac.add(12)
                attention(NOPE)
                pool.wait_ge(pv_done, pv.value)
                passed(pool)
                clear(ln_acc)
                for j in range(CT):
                    add_square(ln_acc, ln_sq, j)
                stat.add(2)
                pool.wait_ge(feed_lo, fed.add(5 + CT))
                passed(pool)
                clear(x_acc)
                for j in range(DT):
                    add_square(x_acc, x_sq, j)
                pool.wait_ge(stat_done, stat.add())
                passed(pool)
                clear(x_acc)
                for j in range(DT):
                    add_square(x_acc, x_sq, j)
                evac.add(TILES - 38)
                fed.add(FEEDS - 5 - CT)

        @block.scalar
        def _(act):
            ev, evac, sqa, stat, own, rst = Count(), Count(EVAC_CREDIT), Count(), Count(), Count(), Count(2)
            vt, mx, tn, pv, ohi, fl, kr, yr, fr, ce, cp, co = (Count() for _ in range(12))
            rr = [Count() for _ in range(RAW)]

            def split(i):
                size, kind, _, dmas = CHUNK_LIST[i % CHUNKS]
                slot = i % RAW
                act.wait_ge(raw_ready[slot], rr[slot].add(16 * dmas))
                act.wait_ge(mm_done, ev.add(CHUNK_LIST[(i - 2) % CHUNKS][2]))
                last = None
                for to, of in split_views(kind, size, w_hi[i % SPLIT], raw[slot]):
                    last = nc.scalar.copy(to, of)
                last.then_inc(hi_done, 1)

            def feed(src, gain, hi, sq, i, first=False):
                nc.scalar.activation(hi, src, ACT.Copy, scale=gain).then_inc(feed_hi, 1)
                if not first:
                    act.wait_ge(sq_added, sqa.value - 1)
                    passed(act)
                sqa.add()
                nc.scalar.activation(sq[i % 2][:], src, ACT.Square).then_inc(sq_ready, 1)

            def root(std, size, eps):
                act.wait_ge(stat_done, stat.add())
                nc.scalar.activation(std[:], stat_bank[:], ACT.Sqrt, scale=1.0 / size,
                                     bias=eps_t[:, eps:eps + 1]).then_inc(std_ready, 1)

            def attention(hi_out):
                def turn(s, first=False):
                    act.wait_ge(turn_done, tn.add())
                    if s % 4 == 0:
                        if not (first and s == 0):
                            act.wait_ge(pv_done, pv.value)
                        pv.add()
                    q = s % 4
                    nc.scalar.copy(p_t[:, 0:q + 1, q * P:(q + 1) * P],
                                   t_bank[s % 2][:, 0:(q + 1) * P].rearrange("p (k q) -> p k q", q=P)).then_inc(turn_out, 1)

                def pair_out(pair):
                    act.wait_ge(pv_done, ohi.add(2))
                    nc.scalar.copy(tile_of(hi_out, pair), o_bank[:]).then_inc(o_hi_done, 1)

                def body(pair, first):
                    for s in range(8):
                        act.wait_ge(max_ready, mx.add())
                        w = (s % 4 + 1) * P
                        nc.scalar.activation(p_b[:, P_AT[s % 4]:P_AT[s % 4] + w], s_bank[s % 4][:, 0:w], ACT.Exp,
                                             bias=neg_max[:, s % 4:s % 4 + 1],
                                             accum_out=row_sum[:, s % 4:s % 4 + 1]).then_inc(exp_done, 1)
                        if s >= 2 or not first:
                            turn((s - 2) % 8, first)
                        if s == 2 and not first:
                            pair_out(pair - 1)

                body(0, True)
                with repeat(act, PAIRS - 1, [(mx, 8), (tn, 8), (pv, 2), (ohi, 2)]) as i:
                    body(i + 1, False)
                turn(6)
                turn(7)
                pair_out(PAIRS - 1)

            def value_tile(j):
                act.wait_ge(vt_done, vt.add())
                nc.scalar.copy(v_n[:, :, j * P:(j + 1) * P],
                               t_bank[j % 2][:].rearrange("p (t c) -> p t c", t=TT)).then_inc(v_ready, 1)

            for l in range(DEPTH):
                for name, row, rows in (("norm_mix_g", R_MIX, 8), ("norm_ffn_g", R_FFN, 8), ("b_gate", R_BG, 24),
                                        ("q_norm_g", R_Q, 3), ("kv_norm_g", R_KV, 2), ("dw_bias", R_DWB, 4),
                                        ("conv_ln_g", R_LNG, 4), ("conv_ln_b", R_LNB, 4)):
                    act.dma_start(par_rows[l * ROWS + row:l * ROWS + row + rows, :],
                                  dram[name][l, :].rearrange("(r c) -> r c", c=P)).then_inc(in_par, 16)
            act.dma_start(par_rows[DEPTH * ROWS:PARAM_ROWS, :],
                          dram["final_norm_g"].rearrange("(r c) -> r c", c=P)).then_inc(in_par, 16)
            act.dma_start(dw_rows[0:DEPTH * TAPS, :], dram["dw_kernel"]).then_inc(in_dw, 16)
            with nc.allow_non_contiguous_dma("16 biases"):
                act.dma_start(b_f[2 * ROPE:MISC, :], dram["b_forget"].rearrange("l h -> h l")).then_inc(in_bf, 16)
            act.wait_ge(angles, 2)
            nc.scalar.activation(cos_t[:], tmp[2][:], ACT.Sin).then_inc(trig, 1)
            nc.scalar.activation(sin_t[:], tmp[3][:], ACT.Sin, scale=const_sb[:, 3 * P + 1:3 * P + 2]).then_inc(trig, 1)
            act.wait_ge(par_turned, 1)
            nc.scalar.copy(params[:], t_bank[0][:, 0:PARAM_ROWS]).then_inc(par_ok, 1)
            for c in range(CT):
                act.wait_ge(par_turned, c + 2)
                nc.scalar.copy(dwk[:, c, :], t_bank[(c + 1) % 2][:, 0:DEPTH * TAPS]).then_inc(par_ok, 1)
            act.wait_ge(par_ok, 1)
            for c in range(2):
                act.wait_ge(raw_ready[c], rr[c].add(16))
                nc.scalar.copy(w_hi[c][:], raw[c][:]).then_inc(hi_done, 1)
            act.wait_ge(acc_zero, 1)
            for j in range(DT):
                act.wait_ge(x_ready, j + 1)
                feed(x_t[:, j, :], params[:, j:j + 1], h_hi[:, j, :], x_sq, j, j < 2)
            act.wait_ge(zero_ok, 3)

            with repeat(act, DEPTH, [(ev, EVENTS), (evac, TILES), (sqa, SQUARES), (stat, 6), (own, 1), (rst, 5), (vt, 8),
                                     (mx, STEPS), (tn, STEPS), (pv, 2 * HEADS), (ohi, 2 * HEADS), (fl, 1), (kr, 1),
                                     (yr, DT), (fr, FT), (ce, CT), (cp, CT), (co, CT), *zip(rr, RING_COUNTS)]):
                for c in range(CONV_CH):
                    split(c + 2)
                    if c == 0:
                        root(x_std, D, 0)
                    evac.add()
                    if c % 2 == 0:
                        act.wait_ge(evac_done, evac.value)
                        nc.scalar.activation(tmp[1][:], tmp[0][:], ACT.Sigmoid).then_inc(sig_done, 1)
                j = 0
                for c in range(LAT_CH):
                    split(LAT + c + 2)
                    if c in (0, 1, 3, 4, 5):
                        act.wait_ge(evac_done, evac.add())
                        feed(tmp[j % 2][:], par[:, R_Q + j:R_Q + j + 1], c_hi[:, j, :], lat_sq, j)
                        j += 1
                    if c == 4:
                        root(lat_std, Q_LORA, 0)
                evac.add()
                act.wait_ge(forget_z, fl.add())
                nc.scalar.activation(f_sum[2 * ROPE:MISC, :], f_sum[2 * ROPE:MISC, :], ACT.Exp).then_inc(act_own, 1)
                act.wait_ge(act_own, own.add())
                nc.scalar.activation(tmp[3][2 * ROPE:MISC, :], f_sum[2 * ROPE:MISC, :], ACT.Ln, bias=1.0).then_inc(forget_l, 1)
                act.wait_ge(kr_ready, kr.add())
                nc.scalar.copy(k_t[NOPE:NOPE + ROPE, :, :],
                               tmp[0][0:ROPE, :].unsqueeze(1).broadcast_to([ROPE, HEADS, T])).then_inc(kr_put, 1)
                tile = 0
                for c in range(UP_CH):
                    split(UP + c + 2)
                    if c == 0:
                        act.wait_ge(rstd_ready, rst.value)
                        root(lat_std, KV_LORA, 0)
                    for m in range(2):
                        evac.add()
                        if c >= 6:
                            if tile:
                                value_tile(tile - 1)
                            tile += 1
                rst.add(5)
                value_tile(3)
                attention(oa_hi)
                for c in range(QKV_CH):
                    split(QKV + c + 2)
                    evac.add()
                    if c >= 9:
                        value_tile(c - 9)
                value_tile(3)
                attention(ob_hi)

                def pass1(j, turn=None):
                    for c in range(4):
                        if (turn, c) == (1, 1):
                            stat.add()
                            root(ln_std, CONV, 1)
                        split(MERGE + c + 2)
                        evac.add()
                        if c < 2:
                            act.wait_ge(evac_done, evac.value)
                            nc.scalar.activation(gate[c][:], tmp[c][:], ACT.Sigmoid,
                                                 bias=par[:, bass.ds(j + (R_BG + c * DT), 1)]).then_inc(sig_done, 1)
                        if (turn, c) == (0, 2):
                            for k in range(CT):
                                act.wait_ge(centred, ce.add())
                                act.wait_ge(sq_added, sqa.value - 1)
                                sqa.add()
                                nc.scalar.activation(ln_sq[k % 2][:], c_acc[:, k, :], ACT.Square).then_inc(sq_ready, 1)
                        if (turn, c) == (1, 2):
                            for k in range(CT):
                                act.wait_ge(conv_pre, cp.add())
                                nc.scalar.activation(ln_sig[:, k, :], c_acc[:, k, :], ACT.Sigmoid).then_inc(sig_done, 1)
                        if (turn, c) == (1, 3):
                            for k in range(CT):
                                act.wait_ge(conv_out, co.add())
                                nc.scalar.copy(oc_hi[:, k, :], c_acc[:, k, :]).then_inc(feed_hi, 1)

                with repeat(act, PASS1_TURNS, [(ev, 4), (evac, 4), *((r, 16) for r in rr)]) as i:
                    pass1(i)
                for turn in range(LN_TURNS):
                    pass1(PASS1_TURNS + turn, turn)
                with repeat(act, DT // 2, [(ev, 4), (evac, 4), (yr, 2), *((r, 16) for r in rr)]) as i:
                    for c in range(4):
                        split(MERGE2 + c + 2)
                        evac.add()
                        if c < 2:
                            act.wait_ge(evac_done, evac.value)
                            nc.scalar.activation(gate[c][:], tmp[c][:], ACT.Sigmoid,
                                                 bias=par[:, bass.ds(i * 2 + (R_BG + 2 * DT + c), 1)]).then_inc(sig_done, 1)
                        else:
                            act.wait_ge(y_ready, yr.add())
                            nc.scalar.copy(tile_of(y_hi, i * 2 + (c - 2)), y_sum[c - 2][:]).then_inc(feed_hi, 1)
                with repeat(act, 2, [(ev, 4), (evac, 4), (sqa, 4), *((r, 16) for r in rr)]) as i:
                    for c in range(4):
                        split(OUT + c + 2)
                        act.wait_ge(evac_done, evac.add())
                        j = i * 4 + c
                        feed(tile_of(x_t, j), par[:, bass.ds(j + R_FFN, 1)], tile_of(h_hi, j), x_sq, c)

                def hidden(i, first=False):
                    for c in range(4):
                        split(FF + c + 2)
                        if first and c == 0:
                            root(x_std, D, 0)
                        evac.add()
                        if c % 2 == 0:
                            act.wait_ge(evac_done, evac.value)
                            nc.scalar.activation(tmp[1][:], tmp[0][:], ACT.Sigmoid).then_inc(sig_done, 1)
                        else:
                            act.wait_ge(ff_ready, fr.add())
                            nc.scalar.copy(tile_of(f_hi, i * 2 + c // 2), tmp[2][:]).then_inc(feed_hi, 1)

                hidden(0, True)
                with repeat(act, FT // 2 - 1, [(ev, 4), (evac, 4), (fr, 2), *((r, 16) for r in rr)]) as i:
                    hidden(i + 1)
                with repeat(act, 2, [(ev, 12), (evac, 4), (sqa, 4), *((r, 48) for r in rr)]) as i:
                    for c in range(12):
                        split(DOWN + c + 2)
                        if c % 3 == 2:
                            act.wait_ge(evac_done, evac.add())
                            j = i * 4 + c // 3
                            feed(tile_of(x_t, j), par[:, bass.ds(j + ROWS, 1)], tile_of(h_hi, j), x_sq, c // 3)
            root(x_std, D, 0)
            for j in range(DT):
                act.wait_ge(out_turned, j + 1)
                nc.scalar.copy(out_rows[:, :, j * P:(j + 1) * P],
                               t_bank[j % 2][:].rearrange("p (t c) -> p t c", t=TT)).then_inc(out_copied, 1)

        @block.vector
        def _(dve):
            hi, mm, own, taps = Count(), Count(), Count(), Count()
            sg, fh, sqr, std, score, ex, ohi, krp, vt, fl, ce, rst, stat = (Count() for _ in range(13))
            std.n, out_n = STD_CREDIT, Count(EVAC_CREDIT)
            ex.n = EXP_CREDIT

            def mine(ins):
                ins.then_inc(dve_own, 1)
                dve.wait_ge(dve_own, own.add())

            def mine_later(ins):
                ins.then_inc(dve_own, 1)
                own.add()

            def mine_now():
                dve.wait_ge(dve_own, own.value)

            def split(i):
                size, kind = CHUNK_LIST[i % CHUNKS][:2]
                dve.wait_ge(hi_done, hi.add())
                h, last = w_hi[i % SPLIT], None
                for (to, of), (part, _) in zip(split_views(kind, size, w_lo[i % SPLIT], raw[i % RAW]),
                                               split_views(kind, size, h, raw[i % RAW])):
                    last = nc.vector.tensor_tensor(to, of, part.bitcast(F32), ALU.subtract)
                last.then_inc(lo_done, 1)

            tiles = [0]

            def tile_ready():
                dve.wait_ge(mm_done, mm.add())
                tiles[0] += 1
                return (tiles[0] - 1) % BANKS

            def evacuated(ins):
                ins.then_inc(evac_done, 1)
                out_n.add()

            def evacuated_here():
                dve.wait_ge(evac_done, out_n.value)

            def scaled(to, b, by, rows=slice(0, P), scale=None):
                if scale is None:
                    return nc.vector.tensor_tensor(to, s_bank[b][rows, :], by[rows, :], ALU.mult)
                return nc.vector.scalar_tensor_tensor(to, s_bank[b][rows, :], scale, by[rows, :], ALU.mult, ALU.mult)

            def feed_low(src, gain, h, lo):
                dve.wait_ge(feed_hi, fh.add())
                if gain is None:
                    ins = nc.vector.tensor_tensor(lo, src, h.bitcast(F32), ALU.subtract)
                else:
                    ins = nc.vector.scalar_tensor_tensor(lo, src, gain, h.bitcast(F32), ALU.mult, ALU.subtract)
                ins.then_inc(feed_lo, 1)

            def factor(root_t, to):
                dve.wait_ge(std_ready, std.add())
                nc.vector.reciprocal(to[:], root_t[:]).then_inc(rstd_ready, 1)
                dve.wait_ge(rstd_ready, rst.add())
                passed(dve)

            def tap(c, k, first=False):
                if not first:
                    dve.wait_ge(tap_done, taps.value)
                if isinstance(k, int) and k == 0:
                    ins = nc.vector.tensor_scalar(c_acc[:, c, :], u_pad[:, c, 0:T], dwk_l[:, c, 0:1],
                                                  par[:, R_DWB + c:R_DWB + c + 1], ALU.mult, ALU.add)
                else:
                    ins = nc.vector.scalar_tensor_tensor(c_acc[:, c, :], u_pad[:, c, bass.ds(k, T)], dwk_l[:, c, bass.ds(k, 1)],
                                                         c_acc[:, c, :], ALU.mult, ALU.add)
                ins.then_inc(tap_done, 1)
                taps.add()

            def attention(hi_out, lo_out, channel, tap0):
                def normalise(s):
                    dve.wait_ge(exp_done, ex.add())
                    mine(nc.vector.reciprocal(row_inv[:, s % 4:s % 4 + 1], row_sum[:, s % 4:s % 4 + 1]))
                    p = p_b[:, P_AT[s % 4]:P_AT[s % 4] + (s % 4 + 1) * P]
                    nc.vector.tensor_scalar(p, p, row_inv[:, s % 4:s % 4 + 1], None, ALU.mult).then_inc(norm_done, 1)

                def pair_low(pair):
                    dve.wait_ge(o_hi_done, ohi.add())
                    h = tile_of(hi_out, pair)
                    nc.vector.tensor_tensor(tile_of(lo_out, pair), o_bank[:], h.bitcast(F32), ALU.subtract).then_inc(o_lo_done, 1)

                def body(pair, first):
                    for s in range(8):
                        dve.wait_ge(score_done, score.add())
                        w = (s % 4 + 1) * P
                        nc.vector.tensor_reduce(neg_max[:, s % 4:s % 4 + 1], s_bank[s % 4][:, 0:w], AX_X, ALU.max,
                                                negate=True).then_inc(max_ready, 1)
                        if s > 0 or not first:
                            normalise((s - 1) % 8)
                        if s == 3 and not first:
                            pair_low(pair - 1)
                        if s % 2 == 1:
                            tap(channel, pair * PAIR_TAPS + (tap0 + (s - 1) // 2))

                body(0, True)
                with repeat(dve, PAIRS - 1, [(score, 8), (ex, 8), (own, 8), (ohi, 1), (taps, PAIR_TAPS)]) as i:
                    body(i + 1, False)
                normalise(7)
                pair_low(PAIRS - 1)
                tiles[0] = 0

            dve.wait_ge(in_const, 16)
            nc.vector.tensor_copy(ident[:], const_sb[:, 0:P]).then_inc(const_ok, 1)
            dve.wait_ge(in_pos, 16)
            mine(nc.vector.tensor_copy(pos_f[:], pos_i[:]))
            mine(nc.vector.tensor_scalar(ang[:], pos_f[:], const_sb[:, 3 * P:3 * P + 1], None, ALU.mult))
            for shift, to in ((0.25, tmp[2]), (0.0, tmp[3])):
                k = tmp[0]
                mine(nc.vector.tensor_scalar(k[:], ang[:], 1.0 / TWO_PI, shift, ALU.mult, ALU.add))
                mine(nc.vector.tensor_scalar(k[:], k[:], ROUND, None, ALU.add))
                mine(nc.vector.tensor_scalar(k[:], k[:], -ROUND, None, ALU.add))
                mine(nc.vector.scalar_tensor_tensor(to[:], k[:], -PI_PARTS[0], ang[:], ALU.mult, ALU.add))
                mine(nc.vector.scalar_tensor_tensor(to[:], k[:], -PI_PARTS[1], to[:], ALU.mult, ALU.add))
                mine(nc.vector.scalar_tensor_tensor(to[:], k[:], -PI_PARTS[2], to[:], ALU.mult, ALU.add))
                if shift:
                    mine(nc.vector.tensor_scalar(to[:], to[:], TWO_PI / 4, None, ALU.add))
                nc.vector.tensor_scalar(to[:], to[:], PI_DOWN, -PI_DOWN, ALU.min, ALU.max).then_inc(angles, 1)
            nc.vector.tensor_copy(ident_b[:], const_sb[:, 0:P]).then_inc(const_ok, 1)
            nc.vector.tensor_copy(mask_b[:], const_sb[:, P:3 * P].rearrange("p (m k) -> p m k", m=2)).then_inc(const_ok, 1)
            dve.wait_ge(par_ok, 1 + CT)
            for j in range(DT):
                dve.wait_ge(x_turned, j + 1)
                nc.vector.tensor_copy(x_t[:, j, :], t_bank[(j + 1) % 2][:]).then_inc(x_ready, 1)
                if j < 2:
                    dve.wait_ge(hi_done, hi.add())
                    nc.vector.tensor_tensor(w_lo[j][:], raw[j][:], w_hi[j][:].bitcast(F32), ALU.subtract).then_inc(lo_done, 1)
                else:
                    feed_low(x_t[:, j - 2, :], params[:, j - 2:j - 1], h_hi[:, j - 2, :], h_lo[:, j - 2, :])
            for j in range(DT - 2, DT):
                feed_low(x_t[:, j, :], params[:, j:j + 1], h_hi[:, j, :], h_lo[:, j, :])
            sqr.add(DT)
            dve.wait_ge(trig, 2)
            dve.wait_ge(in_bf, 16)
            dve.wait_ge(zero_ok, 4)

            with repeat(dve, DEPTH, [(hi, CHUNKS), (mm, EVENTS), (out_n, TILES), (own, OWN), (taps, CT * TAPS), (sg, 4 + 4 + 24 + 22),
                                     (fh, FEEDS), (sqr, SQUARES), (std, 5), (score, STEPS), (ex, STEPS), (ohi, HEADS),
                                     (krp, 1), (vt, 8), (fl, 1), (ce, CT), (rst, 5), (stat, 6)]) as l:
                dve.wait_ge(feed_lo, fh.value)
                nc.vector.tensor_copy(par[:], params[:, bass.ds(l * ROWS, ROWS + DT)])
                mine(nc.vector.tensor_copy(dwk_l[:], dwk[:, :, bass.ds(l * TAPS, TAPS)]))
                for c in range(CONV_CH):
                    if c == 0:
                        split(c + 2)
                        factor(x_std, rstd_x)
                    b = tile_ready()
                    evacuated(scaled(tmp[c % 2 * 2][:], b, rstd_x))
                    if c > 0:
                        split(c + 2)
                    if c % 2 == 1:
                        evacuated_here()
                        dve.wait_ge(sig_done, sg.add())
                        mine(nc.vector.tensor_tensor(u_pad[:, c // 2, TAPS - 1:], tmp[2][:], tmp[1][:], ALU.mult))
                j = k = 0
                for c in range(LAT_CH):
                    if c in (0, 1, 3, 4, 5):
                        b = tile_ready()
                        if j >= 2:
                            dve.wait_ge(sq_ready, sqr.value - 1)
                        evacuated(scaled(tmp[j % 2][:], b, rstd_x))
                    elif c != 7:
                        mm.add()
                    split(LAT + c + 2)
                    for _ in range(LAT_TAPS[c]):
                        tap(0, k, first=(k == 0))
                        k += 1
                    if c in (0, 1, 3, 4, 5):
                        feed_low(tmp[j % 2][:], par[:, R_Q + j:R_Q + j + 1], c_hi[:, j, :], c_lo[:, j, :])
                        sqr.add()
                        j += 1
                    if c == 4:
                        factor(lat_std, rstd_q)
                b = tile_ready()
                dve.wait_ge(sq_ready, sqr.value)
                evacuated(nc.vector.tensor_tensor(tmp[2][0:MISC, :], s_bank[b][0:MISC, :], rstd_x[0:MISC, :], ALU.mult))
                evacuated_here()
                F = slice(2 * ROPE, MISC)
                mine(nc.vector.tensor_scalar(tmp[2][F, :], tmp[2][F, :], b_f[F, bass.ds(l, 1)], None, ALU.add))
                mine(nc.vector.tensor_scalar(f_sum[F, :], tmp[2][F, :], -1.0, None, ALU.mult))
                nc.vector.tensor_tensor(f_sum[F, :], f_sum[F, :], tmp[2][F, :], ALU.min).then_inc(forget_z, 1)
                mine(nc.vector.tensor_tensor(tmp[3][0:ROPE, :], tmp[2][0:ROPE, :], cos_t[0:ROPE, :], ALU.mult))
                mine(nc.vector.tensor_tensor(tmp[1][0:ROPE, :], tmp[2][ROPE:2 * ROPE, :], sin_t[ROPE:2 * ROPE, :], ALU.mult))
                nc.vector.tensor_tensor(tmp[0][0:ROPE, :], tmp[3][0:ROPE, :], tmp[1][0:ROPE, :], ALU.add).then_inc(kr_ready, 1)
                mine(nc.vector.tensor_scalar(tmp[2][F, :], tmp[2][F, :], 0.0, None, ALU.min))
                dve.wait_ge(forget_l, fl.add())
                nc.vector.tensor_tensor_scan(f_sum[F, :], tmp[3][F, :], tmp[2][F, :], 0.0, ALU.add, ALU.subtract).then_inc(cum_ready, 1)
                dve.wait_ge(kr_put, krp.add())
                for c in range(UP_CH):
                    for m in range(2):
                        b = tile_ready()
                        tile = 2 * c + m
                        if c < 2:
                            for e in range(2):
                                ins = scaled(q_t[0:NOPE, 2 * tile + e, :], b, rstd_q, slice(NOPE * e, NOPE * (e + 1)), MLA_SCALE)
                            evacuated(ins)
                        elif c < 4:
                            if c == 2 and m == 0:
                                nc.vector.scalar_tensor_tensor(tmp[2][:], cos_t[:], MLA_SCALE, rstd_q[:], ALU.mult, ALU.mult)
                                mine(nc.vector.scalar_tensor_tensor(tmp[3][:], sin_t[:], MLA_SCALE, rstd_q[:], ALU.mult, ALU.mult))
                            evacuated(scaled(tmp[m][:], b, tmp[2 + m]))
                            if m == 1:
                                evacuated_here()
                                for g in range(4):
                                    rows = slice(ROPE * g, ROPE * (g + 1))
                                    ins = nc.vector.tensor_tensor(q_t[NOPE:NOPE + ROPE, 4 * (c - 2) + g, :], tmp[0][rows, :],
                                                                  tmp[1][rows, :], ALU.add)
                                mine(ins)
                        elif c < 6:
                            for e in range(2):
                                ins = scaled(k_t[0:NOPE, 2 * (tile - 8) + e, :], b, rstd_kv, slice(NOPE * e, NOPE * (e + 1)))
                            evacuated(ins)
                        else:
                            v = tile - 12
                            if v >= 2:
                                dve.wait_ge(vt_done, vt.value - 1)
                            vt.add()
                            evacuated(scaled(tmp[v % 2][:], b, rstd_kv))
                    split(UP + c + 2)
                    if c == 1:
                        factor(lat_std, rstd_kv)
                attention(oa_hi, oa_lo, 0, sum(LAT_TAPS))
                todo = [(3, k) for k in range(TAPS)] + [(2, 0)] + [(1, k) for k in range(TAP1_FOX)]
                for c in range(QKV_CH):
                    b = tile_ready()
                    if c < 8:
                        to = (q_t, k_t)[c // 4]
                        for e in range(2):
                            ins = scaled(to[0:NOPE, 2 * (c % 4) + e, :], b, rstd_x, slice(NOPE * e, NOPE * (e + 1)),
                                         FOX_SCALE if c < 4 else None)
                        evacuated(ins)
                    else:
                        v = c - 8
                        if v >= 2:
                            dve.wait_ge(vt_done, vt.value - 1)
                        vt.add()
                        evacuated(scaled(tmp[v % 2][:], b, rstd_x))
                    split(QKV + c + 2)
                    for _ in range(QKV_TAPS[c]):
                        tap(*todo.pop(0))
                assert not todo
                attention(ob_hi, ob_lo, 1, TAP1_FOX)

                def pass1(j, turn=None):
                    todo = []
                    if turn is None:
                        todo = [(1, j * 2 + (TAP1_MERGE + k)) for k in range(2)] + [(2, j * 6 + (1 + k)) for k in range(6)]
                    for c in range(4):
                        b = tile_ready()
                        if c < 2:
                            evacuated(scaled(tmp[c][:], b, rstd_x))
                        else:
                            dve.wait_ge(sig_done, sg.add())
                            evacuated(scaled((y_sum[0], tmp[3])[c - 2][:], b, gate[c - 2]))
                        if c == 3:
                            evacuated_here()
                            mine(nc.vector.tensor_tensor(tile_of(y_ab, j), y_sum[0][:], tmp[3][:], ALU.add))
                        split(MERGE + c + 2)
                        if todo:
                            for _ in range((3, 3, 1, 1)[c]):
                                tap(*todo.pop(0))
                        if (turn, c) == (0, 1):
                            dve.wait_ge(stat_done, l * 6 + 4)
                            for k in range(CT):
                                nc.vector.scalar_tensor_tensor(c_acc[:, k, :], stat_bank[:], -1.0 / CONV, c_acc[:, k, :],
                                                               ALU.mult, ALU.add).then_inc(centred, 1)
                        if (turn, c) == (1, 1):
                            factor(ln_std, ln_rstd)
                        if (turn, c) == (1, 2):
                            for k in range(CT):
                                ins = nc.vector.tensor_tensor(c_acc[:, k, :], c_acc[:, k, :], ln_rstd[:], ALU.mult)
                            mine(ins)
                            for k in range(CT):
                                nc.vector.tensor_scalar(c_acc[:, k, :], c_acc[:, k, :], par[:, R_LNG + k:R_LNG + k + 1],
                                                        par[:, R_LNB + k:R_LNB + k + 1], ALU.mult, ALU.add).then_inc(conv_pre, 1)
                        if (turn, c) == (1, 3):
                            for k in range(CT):
                                dve.wait_ge(sig_done, sg.add())
                                nc.vector.tensor_tensor(c_acc[:, k, :], c_acc[:, k, :], ln_sig[:, k, :], ALU.mult).then_inc(conv_out, 1)
                            for k in range(CT):
                                feed_low(c_acc[:, k, :], None, oc_hi[:, k, :], oc_lo[:, k, :])

                with repeat(dve, PASS1_TURNS, [(hi, 4), (mm, 4), (out_n, 4), (own, 1), (sg, 2), (taps, 8)]) as i:
                    pass1(i)
                for turn in range(LN_TURNS):
                    pass1(PASS1_TURNS + turn, turn)
                ce.add(CT)
                stat.add(6)
                sqr.add(CT)
                with repeat(dve, DT // 2, [(hi, 4), (mm, 4), (out_n, 4), (sg, 2), (fh, 2)]) as i:
                    for c in range(4):
                        b, e = tile_ready(), c - 2
                        if c < 2:
                            evacuated(scaled(tmp[c][:], b, rstd_x))
                        else:
                            dve.wait_ge(sig_done, sg.add())
                            evacuated(scaled(tmp[c][:], b, gate[e]))
                            evacuated_here()
                            nc.vector.tensor_tensor(y_sum[e][:], tmp[c][:], tile_of(y_ab, i * 2 + e), ALU.add).then_inc(y_ready, 1)
                        split(MERGE2 + c + 2)
                        if c >= 2:
                            feed_low(y_sum[e][:], None, tile_of(y_hi, i * 2 + e), tile_of(y_lo, i * 2 + e))
                with repeat(dve, 2, [(hi, 4), (mm, 4), (out_n, 4), (fh, 4), (sqr, 4)]) as i:
                    for c in range(4):
                        b = tile_ready()
                        j = i * 4 + c
                        evacuated(nc.vector.tensor_tensor(tile_of(x_t, j), s_bank[b][:], tile_of(x_t, j), ALU.add))
                        split(OUT + c + 2)
                        feed_low(tile_of(x_t, j), par[:, bass.ds(j + R_FFN, 1)], tile_of(h_hi, j), tile_of(h_lo, j))
                        sqr.add()

                def hidden(i, first=False):
                    for c in range(4):
                        if first and c == 0:
                            split(FF + c + 2)
                            factor(x_std, rstd_x)
                        b = tile_ready()
                        evacuated(scaled(tmp[c % 2 * 3][:], b, rstd_x))
                        if c % 2 == 1:
                            evacuated_here()
                            nc.vector.tensor_tensor(tmp[2][:], tmp[2][:], tmp[3][:], ALU.mult).then_inc(ff_ready, 1)
                        if not (first and c == 0):
                            split(FF + c + 2)
                        if c % 2 == 0:
                            dve.wait_ge(sig_done, sg.add())
                            mine_later(nc.vector.tensor_tensor(tmp[2][:], tmp[0][:], tmp[1][:], ALU.mult))
                        else:
                            feed_low(tmp[2][:], None, tile_of(f_hi, i * 2 + c // 2), tile_of(f_lo, i * 2 + c // 2))

                hidden(0, True)
                with repeat(dve, FT // 2 - 1, [(hi, 4), (mm, 4), (out_n, 4), (own, 2), (sg, 2), (fh, 2)]) as i:
                    hidden(i + 1)
                with repeat(dve, 2, [(hi, 12), (mm, 12), (out_n, 4), (fh, 4), (sqr, 4)]) as i:
                    for c in range(12):
                        if c % 3 < 2:
                            mm.add()
                            split(DOWN + c + 2)
                            continue
                        b = tile_ready()
                        j = i * 4 + c // 3
                        evacuated(nc.vector.tensor_tensor(tile_of(x_t, j), s_bank[b][:], tile_of(x_t, j), ALU.add))
                        split(DOWN + c + 2)
                        feed_low(tile_of(x_t, j), par[:, bass.ds(j + ROWS, 1)], tile_of(h_hi, j), tile_of(h_lo, j))
                        sqr.add()
            factor(x_std, rstd_x)
            for j in range(DT):
                if j >= 2:
                    dve.wait_ge(out_turned, j - 1)
                nc.vector.scalar_tensor_tensor(tmp[j % 2][:], x_t[:, j, :], params[:, DEPTH * ROWS + j:DEPTH * ROWS + j + 1],
                                               rstd_x[:], ALU.mult, ALU.mult).then_inc(out_tile, 1)

        @block.tensor
        def _(pe):
            lo, ev, fl, sqa, std = Count(RAW_CREDIT), Count(), Count(), Count(), Count(STD_CREDIT)
            st, ex, nm, to, ol, vr, taps, nt = Count(), Count(), Count(), Count(TURN_CREDIT), Count(), Count(), Count(), [0]
            pair_lo = Count(O_CREDIT)
            cumc = Count()

            def products(bank_t, rows, slot, cols, m, k_tiles, rhs, k0, first, last, fresh):
                for k in range(k_tiles):
                    w = slice(k * cols + m * P, k * cols + m * P + rows)
                    a, b = rhs(k0 + k)
                    if fresh:
                        pe.wait_ge(feed_lo, fl.value + (k0 + k + 1))
                    for p, (wt, x) in enumerate(((w_hi, a), (w_hi, b), (w_lo, a))):
                        ins = nc.tensor.matmul(bank_t[0:rows, :], wt[slot][:, w], x,
                                               start=first and k == 0 and p == 0, stop=last and k == k_tiles - 1 and p == 2)
                return ins

            def chunk(i, rhs, tiles=1, k_tiles=DT, cols=P, k0=0, first=True, last=True, rows=P, between=None, fresh=False):
                pe.wait_ge(lo_done, lo.add())
                for m in range(tiles):
                    if first:
                        pe.wait_ge(evac_done, ev.add())
                        nt[0] += 1
                    products(s_bank[(nt[0] - 1) % BANKS], rows, i % SPLIT, cols, m, k_tiles, rhs, k0, first, last,
                             fresh and m == 0).then_inc(mm_done, 1)
                    if between:
                        between(m)

            h = lambda k: (h_hi[:, k, :], h_lo[:, k, :])

            def statistic(src, n_sq):
                pe.wait_ge(sq_added, sqa.add(n_sq))
                pe.wait_ge(std_ready, std.value)
                nc.tensor.matmul(stat_bank[:], ones[:], src[:], start=True, stop=True).then_inc(stat_done, 1)
                std.add()

            def turn_values(j, back):
                pe.wait_ge(evac_done, ev.value + (EVAC_CREDIT - back))
                if j >= 2:
                    pe.wait_ge(v_ready, vr.value - 1)
                vr.add()
                for t in range(TT):
                    ins = nc.tensor.transpose(t_bank[j % 2][:, t * P:(t + 1) * P], tmp[j % 2][:, t * P:(t + 1) * P], ident[:])
                ins.then_inc(vt_done, 1)

            def attention(rows, kind, dense, tail):
                def logits(pair, s):
                    e, q = s // 4, s % 4
                    pe.wait_ge(exp_done, ex.add())
                    if q == 0:
                        pe.wait_ge(st_ready, st.value + 1 + e)
                    w = (q + 1) * P
                    nc.tensor.matmul(s_bank[q][:, 0:w], q_st[e][0:rows, q * P:w], head_of(k_t, pair, e)[0:rows, 0:w],
                                     start=True, stop=True)
                    nc.tensor.matmul(s_bank[q][:, q * P:w], ident_b[:], mask_b[:, kind, :], start=False, stop=True,
                                     skip_group_check=True).then_inc(score_done, 1)

                def turn(s):
                    pe.wait_ge(norm_done, nm.add())
                    pe.wait_ge(turn_out, to.value - 1)
                    to.add()
                    for k in range(s % 4 + 1):
                        at_k = P_AT[s % 4] + k * P
                        ins = nc.tensor.transpose(t_bank[s % 2][:, k * P:(k + 1) * P], p_b[:, at_k:at_k + P], ident[:])
                    ins.then_inc(turn_done, 1)

                def values(e, ago):
                    if e == 0:
                        pe.wait_ge(o_lo_done, pair_lo.value)
                        pair_lo.add()
                        pe.wait_ge(st_ready, st.value + 3)
                    pe.wait_ge(turn_out, to.value - ago)
                    for k in range(TT):
                        ins = nc.tensor.matmul(o_bank[e * VDIM:(e + 1) * VDIM, k * P:T], v_st[:, k, e * VDIM:(e + 1) * VDIM],
                                               p_t[:, k, k * P:T], start=(k == 0), stop=True, skip_group_check=True)
                    ins.then_inc(pv_done, 1)

                def body(pair, first=False, last=False):
                    for s in range(8):
                        if s == 5:
                            st.add(3)
                        if s < 5:
                            logits(pair, s + 3)
                        elif not last:
                            logits(pair + 1, s - 5)
                        if last and s == 6:
                            tail()
                        turn(s)
                        if s == 0 and not first:
                            values(1, 1)
                        if s == 4:
                            values(0, 1)

                pe.wait_ge(evac_done, ev.value + (EVAC_CREDIT - 1))
                logits(0, 0)
                dense()
                pe.wait_ge(evac_done, ev.value + EVAC_CREDIT)
                nt[0] = 0
                logits(0, 1)
                logits(0, 2)
                body(0, first=True)
                with repeat(pe, PAIRS - 2, [(st, 3), (ex, 8), (nm, 8), (to, 8), (pair_lo, 1)]) as i:
                    body(i + 1)
                body(PAIRS - 1, last=True)
                values(1, 0)

            pe.wait_ge(const_ok, 1)
            pe.wait_ge(in_par, 16 * (8 * DEPTH + 1))
            nc.tensor.transpose(t_bank[0][:, 0:PARAM_ROWS], par_rows[0:PARAM_ROWS, :], ident[0:PARAM_ROWS, 0:PARAM_ROWS]).then_inc(par_turned, 1)
            pe.wait_ge(in_dw, 16)
            R = DEPTH * TAPS
            for c in range(CT):
                if c >= 1:
                    pe.wait_ge(par_ok, c)
                nc.tensor.transpose(t_bank[(c + 1) % 2][:, 0:R], dw_rows[0:R, c * P:(c + 1) * P], ident[0:R, 0:R]).then_inc(par_turned, 1)
            pe.wait_ge(in_x, 16 * TT)
            for j in range(DT):
                pe.wait_ge(par_ok, CT if j == 0 else 1 + CT)
                if j >= 2:
                    pe.wait_ge(x_ready, j - 1)
                for t in range(TT):
                    ins = nc.tensor.transpose(t_bank[(j + 1) % 2][:, t * P:(t + 1) * P], x_rows[:, t, j * P:(j + 1) * P], ident[:])
                ins.then_inc(x_turned, 1)
            pe.wait_ge(zero_ok, 1)
            pe.wait_ge(const_ok, 3)

            with repeat(pe, DEPTH, [(lo, CHUNKS), (ev, TILES), (fl, FEEDS), (sqa, SQUARES), (std, 5), (st, 3 * HEADS), (ex, STEPS),
                                    (nm, STEPS), (to, STEPS), (pair_lo, HEADS), (vr, 8), (taps, CT * TAPS), (cumc, 16)]):
                chunk(0, h, fresh=True)
                fl.add(DT)
                statistic(x_acc, DT)
                for c in range(1, CONV_CH):
                    chunk(c, h)
                chunk(LAT, h)
                chunk(LAT + 1, h)
                chunk(LAT + 2, h, k_tiles=4, last=False)
                chunk(LAT + 3, h, k_tiles=4, k0=4, first=False)
                chunk(LAT + 4, h)
                statistic(lat_acc, 3)
                chunk(LAT + 5, h)
                chunk(LAT + 6, h, k_tiles=4, cols=MISC, rows=MISC, last=False)
                chunk(LAT + 7, h, k_tiles=4, k0=4, cols=MISC, rows=MISC, first=False)
                cq = lambda k: (c_hi[:, k, :], c_lo[:, k, :])
                ckv = lambda k: (c_hi[:, 3 + k, :], c_lo[:, 3 + k, :])
                pe.wait_ge(feed_lo, fl.add(5))
                for c in range(4):
                    chunk(UP + c, cq, tiles=2, k_tiles=3, cols=2 * P)
                    if c == 0:
                        statistic(lat_acc, 2)
                for c in range(4, 6):
                    chunk(UP + c, ckv, tiles=2, k_tiles=2, cols=2 * P)
                chunk(UP + 6, ckv, tiles=2, k_tiles=2, cols=2 * P, between=lambda m: turn_values(0, 1) if m == 1 else None)
                chunk(UP + 7, ckv, tiles=2, k_tiles=2, cols=2 * P, between=lambda m: turn_values(1 + m, 1))

                def dense_at(i, rhs):
                    pe.wait_ge(exp_done, ex.value + 1)
                    chunk(i, rhs)

                attention(NOPE + ROPE, 0, lambda: turn_values(3, 0), lambda: dense_at(QKV, h))
                for c in range(1, QKV_CH):
                    if c < BANKS:
                        pe.wait_ge(exp_done, ex.value + 1 + c)
                    chunk(QKV + c, h)
                    if c >= 9:
                        turn_values(c - 9, 1)
                pe.wait_ge(cum_put, cumc.add(16))
                attention(NOPE + 1, 1, lambda: turn_values(3, 0), lambda: dense_at(MERGE, h))
                for c in range(1, BANKS):
                    pe.wait_ge(exp_done, ex.value + 1 + c)

                outs = [lambda k, a=a, b=b: (a[:, k, :], b[:, k, :]) for a, b in ((oa_hi, oa_lo), (ob_hi, ob_lo), (oc_hi, oc_lo))]

                def pass1(turn=None, c0=0):
                    for c in range(c0, 4):
                        if c == 2:
                            pe.wait_ge(o_lo_done, pair_lo.value)
                        chunk(MERGE + c, h if c < 2 else outs[c - 2], k_tiles=DT if c < 2 else PAIRS)
                        if (turn, c) == (0, 0):
                            pe.wait_ge(tap_done, taps.add(CT * TAPS))
                            for k in range(CT):
                                ins = nc.tensor.matmul(stat_bank[:], ones[:], c_acc[:, k, :], start=(k == 0), stop=(k == CT - 1))
                            ins.then_inc(stat_done, 1)
                        if (turn, c) == (1, 0):
                            statistic(ln_acc, CT)

                pass1(c0=1)
                with repeat(pe, PASS1_TURNS - 1, [(lo, 4), (ev, 4)]):
                    pass1()
                for turn in range(LN_TURNS):
                    pass1(turn)
                pe.wait_ge(feed_lo, fl.add(CT))
                passed(pe)
                with repeat(pe, DT // 2, [(lo, 4), (ev, 4)]):
                    for c in range(4):
                        chunk(MERGE2 + c, h if c < 2 else outs[2], k_tiles=DT if c < 2 else CT)
                y = lambda k: (y_hi[:, k, :], y_lo[:, k, :])
                with repeat(pe, 2, [(lo, 4), (ev, 4)]):
                    for c in range(4):
                        chunk(OUT + c, y, fresh=(c == 0))
                fl.add(DT)

                def hidden(first=False):
                    for c in range(4):
                        chunk(FF + c, h, fresh=(first and c == 0))
                        if first and c == 0:
                            fl.add(DT)
                            statistic(x_acc, DT)

                hidden(True)
                with repeat(pe, FT // 2 - 1, [(lo, 4), (ev, 4)]):
                    hidden()
                f = lambda k: (f_hi[:, k, :], f_lo[:, k, :])
                with repeat(pe, 2, [(lo, 12), (ev, 4)]):
                    for c in range(12):
                        b = c % 3
                        chunk(DOWN + c, f, k_tiles=DOWN_K[b], k0=8 * b, first=(b == 0), last=(b == 2), fresh=(c < 3))
                fl.add(FT)
            fl.add(DT)
            pe.wait_ge(feed_lo, fl.value)
            statistic(x_acc, DT)
            for j in range(DT):
                pe.wait_ge(out_tile, j + 1)
                if j >= 2:
                    pe.wait_ge(out_copied, j - 1)
                for t in range(TT):
                    ins = nc.tensor.transpose(t_bank[j % 2][:, t * P:(t + 1) * P], tmp[j % 2][:, t * P:(t + 1) * P], ident[:])
                ins.then_inc(out_turned, 1)


def kernel(**inputs):
    import concourse.bacc as bacc
    from concourse.bass_utils import run_bass_kernel_spmd

    shapes = {
        "x": (T, D), "positions": (1, T), "norm_mix_g": (DEPTH, D), "w_in": (DEPTH * D, IN_WIDTH),
        "b_gate": (DEPTH, 3 * D), "q_norm_g": (DEPTH, Q_LORA), "w_uq": (DEPTH * Q_LORA, HEADS * (NOPE + ROPE)),
        "kv_norm_g": (DEPTH, KV_LORA), "w_ukv": (DEPTH * KV_LORA, HEADS * (NOPE + VDIM)), "b_forget": (DEPTH, HEADS),
        "dw_kernel": (DEPTH * TAPS, CONV), "dw_bias": (DEPTH, CONV), "conv_ln_g": (DEPTH, CONV), "conv_ln_b": (DEPTH, CONV),
        "w_bo_a": (DEPTH * 512, D), "w_bo_b": (DEPTH * 512, D), "w_bo_c": (DEPTH * CONV, D), "w_out": (DEPTH * D, D),
        "norm_ffn_g": (DEPTH, D), "w_ffn_gate": (DEPTH * D, FFN), "w_ffn_up": (DEPTH * D, FFN),
        "w_ffn_down": (DEPTH * FFN, D), "final_norm_g": (D,),
    }
    consts = np.zeros((P, 3 * P + 2), np.float32)
    q, k = np.arange(P)[:, None], np.arange(P)[None, :]
    consts[:, 0:P] = q == k
    consts[:, P:2 * P] = np.where(q // CHUNK_MASK >= k // CHUNK_MASK, 0, MASKED)
    consts[:, 2 * P:3 * P] = np.where(q >= k, 0, MASKED)
    freq = np.float32(1) / np.float32(THETA) ** (np.arange(0, ROPE, 2, dtype=np.float32) / np.float32(ROPE))
    consts[:, 3 * P] = freq[np.arange(P) % (ROPE // 2)]
    consts[:, 3 * P + 1] = np.where(np.arange(P) % ROPE < ROPE // 2, -1, 1)

    nc = bacc.Bacc("TRN2", target_bir_lowering=False, num_devices=1)
    arrays, dram = {}, {}
    for name, shape in shapes.items():
        arrays["in_" + name] = np.ascontiguousarray(inputs[name]).reshape(shape)
    arrays["in_consts"] = consts
    for name, a in arrays.items():
        dram[name[3:]] = nc.dram_tensor(name, a.shape, mybir.dt.from_np(a.dtype), kind="ExternalInput").ap()
    out = nc.dram_tensor("out_x", (T, D), F32, kind="ExternalOutput").ap()
    trunk(nc, dram, out)
    r = run_bass_kernel_spmd(nc, [arrays], core_ids=[0])
    return r.results[0]["out_x"].reshape(1, T, D)
```

```python
from contextlib import ExitStack, contextmanager

import numpy as np

import concourse.bass as bass
from concourse import mybir

F32 = mybir.dt.float32
F32R = mybir.dt.float32r
BF16 = mybir.dt.bfloat16
I32 = mybir.dt.int32
ALU = mybir.AluOpType
ACT = mybir.ActivationFunctionType
AX_X = mybir.AxisListType.X

P = 128
DEPTH, D, T = 2, 1024, 512
DT = D // P
TT = T // P
Q_LORA, KV_LORA = 384, 256
NOPE, ROPE, VDIM, HEADS = 64, 32, 64, 8
PAIRS = HEADS // 2
CONV, TAPS = 512, 31
CT = CONV // P
FFN = 2816
FT = FFN // P
THETA = 10000.0
RMS_EPS, LN_EPS = 1e-6, 1e-5
MLA_SCALE = (NOPE + ROPE) ** -0.5
FOX_SCALE = NOPE ** -0.5
CHUNK_MASK = 64
MASKED = -1e30

C_Q = 0
C_KV = C_Q + Q_LORA
C_KR = C_KV + KV_LORA
C_QB = C_KR + ROPE
C_KB = C_QB + HEADS * NOPE
C_VB = C_KB + HEADS * NOPE
C_F = C_VB + HEADS * NOPE
C_CONV = C_F + HEADS
C_GATE = C_CONV + 2 * CONV
IN_WIDTH = C_GATE + 3 * D

PARAMS = (("norm_mix_g", 8), ("norm_ffn_g", 8), ("b_gate", 24), ("q_norm_g", 3), ("kv_norm_g", 2), ("dw_bias", 4),
          ("conv_ln_g", 4), ("conv_ln_b", 4))
R_MIX, R_FFN, R_BG, R_Q, R_KV, R_DWB, R_LNG, R_LNB = (sum(n for _, n in PARAMS[:i]) for i in range(8))
ROWS = sum(n for _, n in PARAMS)
G_ROWS = [DEPTH * sum(n for _, n in PARAMS[:i]) + (DT if i else 0) for i in range(8)]
PARAM_ROWS = DEPTH * ROWS + DT
MISC = 2 * ROPE + HEADS

CONV_CH, LAT_CH, UP_CH, QKV_CH, MERGE_CH, OUT_CH, FFN_CH, DOWN_CH = 8, 8, 8, 12, 48, 8, 44, 24
CHUNKS = CONV_CH + LAT_CH + UP_CH + QKV_CH + MERGE_CH + OUT_CH + FFN_CH + DOWN_CH
TILES = 8 + 6 + 16 + 12 + 48 + 8 + 44 + 8
EVENTS = 8 + 8 + 16 + 12 + 48 + 8 + 44 + 24
EVACS = TILES - 8
BANKS = 4
STEPS = 2 * HEADS * TT
RAW, SPLIT = 4, 2
DOWN_K = (8, 8, 6)

RAW_CREDIT, EVAC_CREDIT, EXP_CREDIT, TURN_CREDIT, O_CREDIT, STD_CREDIT = RAW, BANKS, BANKS, 2, 1, 1

CONV_TAPS = (0, 0, 1, 1, 2, 2, 3, 3)
UP_TAPS = (1, 1, 1, 1, 1, 1, 1, 0)
PAIR_TAPS = 3
QKV_TAPS = (4, 4, 4, 4, 4, 4, 4, 4, 4, 3, 1, 1)
LN_TURNS = 3
PASS1_TURNS = D // P - LN_TURNS
PASS2_TURNS = D // P // 2
assert sum(CONV_TAPS) + sum(UP_TAPS) + PAIRS * PAIR_TAPS == TAPS
SPREAD = ((1, 4 + PAIRS * PAIR_TAPS, 3), (2, 16, 3), (3, 21, 2))
assert all(before + PASS1_TURNS * n == TAPS for _, before, n in SPREAD) and sum(QKV_TAPS) == 4 + 16 + 21
SWISH = ((), (0, 1), (2,), (3,))
TURN_TAPS = (3, 3, 1, 1)
TAP_STEPS = (3, 5, 7)
P_AT = (0, P, 3 * P, 6 * P)


CHUNK_LIST = (
    [(1024, None, 1, 1)] * 2 + [(512, None, 1, 1)] * 2 + [(1024, None, 1, 1)] * 2 + [(0, "misc", 1, 2)] * 2
    + [(1024, None, 1, 1)] * 8
    + [(768, None, 2, 3)] * 2 + [(0, "rope", 2, 3)] * 2 + [(512, None, 2, 2)] * 4
    + [(1024, None, 1, 1)] * 12
    + ([(1024, None, 1, 1)] * 2 + [(512, None, 1, 1)] * 2) * 8
    + [(1024, None, 1, 1), (512, None, 1, 1)] * 8
    + [(1024, None, 1, 1)] * 8
    + [(1024, None, 1, 1)] * 44
    + [(P * k, None, 1, 1) for k in DOWN_K] * 8
)
assert len(CHUNK_LIST) == CHUNKS and sum(c[2] for c in CHUNK_LIST) == EVENTS
RING_COUNTS = [16 * sum(c[3] for c in CHUNK_LIST[i::RAW]) for i in range(RAW)]
SQUARES, FEEDS = 5 + CT + 2 * DT, 5 + CT + DT + DT + FT + DT
LAT_AT = {2: (0, 1), 3: (2,), 4: (3, 4)}
UP_BANK = (6 + 8) % BANKS
LAT, CONVS, UP, QKV, MERGE, MERGE2, OUT, FF, DOWN = 0, 8, 16, 24, 36, 68, 84, 92, 136
OWN = 1 + 1 + 4 + STEPS + DT + 1 + FT

TWO_PI = 2 * np.pi
ROUND = 1.5 * 2.0 ** 23
PI_PARTS = (6.28125, 4058 / 2.0 ** 21, 3.0199160e-7)
PI_DOWN = 3.1415925


def split_views(kind, size, to, of):
    H = ROPE // 2
    if kind == "misc":
        a = of[:, 0:4 * (ROPE + HEADS)].rearrange("p (k c) -> p k c", k=4)
        b = to[:, 0:4 * MISC].rearrange("p (k c) -> p k c", k=4)
        return [(b[:, :, 0:ROPE], a[:, :, 0:ROPE]), (b[:, :, ROPE:ROPE + H], a[:, :, H:ROPE]),
                (b[:, :, ROPE + H:2 * ROPE], a[:, :, 0:H]), (b[:, :, 2 * ROPE:MISC], a[:, :, ROPE:ROPE + HEADS])]
    if kind == "rope":
        a = of[:, 0:3 * P].rearrange("p (k g c) -> p k g c", k=3, c=ROPE)
        b = to[:, 0:6 * P].rearrange("p (k s g c) -> p k s g c", k=3, s=2, c=ROPE)
        straight = [(b[:, k, 0], a[:, k]) for k in range(3)]
        return straight + [x for k in range(3) for x in ((b[:, k, 1, :, 0:H], a[:, k, :, H:ROPE]),
                                                         (b[:, k, 1, :, H:ROPE], a[:, k, :, 0:H]))]
    return [(to[:, 0:size], of[:, 0:size])]


def tile_of(t, j):
    return t[:, bass.ds(j, 1), :].rearrange("p a t -> p (a t)")


def head_of(t, pair, e):
    return t[:, bass.ds(pair * 2 + e, 1), :].rearrange("p a t -> p (a t)")


class Count:

    def __init__(self, start=0):
        self.n, self.dyn = start, 0

    def add(self, by=1):
        self.n += by
        return self.value

    @property
    def value(self):
        return self.dyn + self.n


@contextmanager
def repeat(eng, times, per):
    with eng.Fori(0, times) as i:
        old = [(c, c.n, c.dyn) for c, _ in per]
        for c, by in per:
            if by:
                c.dyn = c.dyn + i * by
        yield i
        for (c, by), (_, n, _) in zip(per, old):
            assert c.n - n == by, f"a turn adds {c.n - n}, not {by} ({[k for k, (q, _) in enumerate(per) if q is c]})"
        for (c, by), (_, n, dyn) in zip(per, old):
            c.n, c.dyn = n + by * times, dyn


def trunk(nc, dram, out):
    KB = 1024
    base = nc.sbuf_base + (-nc.sbuf_base) % 64
    free = [base]

    def at(name, off, shape, dt=F32):
        return nc.alloc_sbuf_tensor_at(name, shape, dt, offset=off)

    def sb(name, shape, dt=F32):
        size = int(np.prod(shape[1:])) * (2 if dt == BF16 else 4)
        t = at(name, free[0], shape, dt)
        free[0] += size + (-size) % 32
        assert free[0] <= nc.sbuf_usable_end, (name, free[0] - nc.sbuf_usable_end)
        return t

    x_t = sb("x_t", [P, DT, T])
    h_hi = sb("h_hi", [P, DT, T], F32R)
    h_lo = sb("h_lo", [P, DT, T], F32R)
    raw = [sb(f"raw{i}", [P, 1024]) for i in range(RAW)]
    w_hi = [sb(f"w_hi{i}", [P, 1024], F32R) for i in range(SPLIT)]
    w_lo = [sb(f"w_lo{i}", [P, 1024], F32R) for i in range(SPLIT)]
    rstd_x = sb("rstd_x", [P, T])
    cos_t = sb("cos_t", [P, T])
    sin_t = sb("sin_t", [P, T])
    tmp_off = free[0]
    tmp = [sb(f"tmp{i}", [P, T]) for i in range(4)]
    v_st = sb("v_st", [P, TT, P])
    u_pad = sb("u_pad", [P, CT, TAPS - 1 + T])
    c_off = free[0]
    c_acc = sb("c_acc", [P, CT, T])
    ones = sb("ones", [P, P])
    ident = sb("ident", [P, P])
    ident_b = sb("ident_b", [P, P], BF16)
    mask_b = sb("mask_b", [P, 2, P], BF16)
    params = sb("params", [P, PARAM_ROWS])
    par = sb("par", [P, ROWS + DT])
    dwk = sb("dwk", [P, CT, DEPTH * TAPS])
    dwk_l = sb("dwk_l", [P, CT, TAPS])
    b_f = sb("b_f", [P, DEPTH])
    exp_sink = sb("exp_sink", [P, 1])
    b_l = sb("b_l", [P, 1])
    eps_t = sb("eps_t", [P, 3])
    neg_max = sb("neg_max", [P, 4])
    row_sum = sb("row_sum", [P, 4])
    row_inv = sb("row_inv", [P, 4])
    std_col = sb("std_col", [P, TT])
    rstd_col = sb("rstd_col", [P, TT])
    f_sum = sb("f_sum", [P, T])
    r0 = free[0]
    free[0] += 89 * KB
    assert free[0] <= nc.sbuf_usable_end, free[0] - nc.sbuf_usable_end
    q_t = at("q_t", r0, [P, HEADS, T])
    k_t = at("k_t", r0 + 16 * KB, [P, HEADS, T])
    v_n = at("v_n", r0 + 32 * KB, [P, TT, HEADS * VDIM])
    oa_hi = at("oa_hi", r0 + 40 * KB, [P, PAIRS, T], F32R)
    oa_lo = at("oa_lo", r0 + 48 * KB, [P, PAIRS, T], F32R)
    ob_hi = at("ob_hi", r0 + 56 * KB, [P, PAIRS, T], F32R)
    ob_lo = at("ob_lo", r0 + 64 * KB, [P, PAIRS, T], F32R)
    p_b = at("p_b", r0 + 72 * KB, [P, 10 * P])
    p_t = at("p_t", r0 + 77 * KB, [P, TT, T])
    q_st = [at(f"q_st{i}", r0 + (85 + 2 * i) * KB, [P, T]) for i in range(2)]
    o_raw = at("o_raw", tmp_off + 4 * KB, [P, T])
    c_hi = at("c_hi", r0 + 40 * KB, [P, 5, T], F32R)
    c_lo = at("c_lo", r0 + 50 * KB, [P, 5, T], F32R)
    rstd_q = at("rstd_q", r0 + 60 * KB, [P, T])
    rstd_kv = at("rstd_kv", r0 + 62 * KB, [P, T])
    lat_sq = [at(f"lat_sq{i}", r0 + (64 + 2 * i) * KB, [P, T]) for i in range(2)]
    lat_acc = at("lat_acc", r0 + 68 * KB, [P, T])
    lat_std = at("lat_std", r0 + 70 * KB, [P, T])
    kv_std = at("kv_std", c_off + 2 * KB, [P, T])
    c_raw = at("c_raw", r0 + 72 * KB, [P, 5, T])
    rope_t = at("rope_t", r0 + 72 * KB, [P, 4, T])
    misc_t = at("misc_t", r0 + 82 * KB, [P, T])
    key_a = at("key_a", r0 + 84 * KB, [P, T])
    key_b = at("key_b", r0 + 86 * KB, [P, T])
    x_sq = [at(f"x_sq{i}", c_off + 2 * i * KB, [P, T]) for i in range(2)]
    x_acc = at("x_acc", c_off + 4 * KB, [P, T])
    x_std = at("x_std", c_off + 6 * KB, [P, T])
    ln_sq = [at(f"ln_sq{i}", r0 + 2 * i * KB, [P, T]) for i in range(2)]
    ln_acc = at("ln_acc", r0 + 4 * KB, [P, T])
    ln_std = at("ln_std", r0 + 6 * KB, [P, T])
    ln_rstd = ln_acc
    ln_sig = at("ln_sig", r0 + 8 * KB, [P, CT, T])
    oc_hi = at("oc_hi", r0 + 73 * KB, [P, CT, T], F32R)
    oc_lo = at("oc_lo", r0 + 81 * KB, [P, CT, T], F32R)
    gate = [at(f"gate{i}", r0 + (32 + 2 * i) * KB, [P, T]) for i in range(2)]
    y_sum = [at(f"y_sum{i}", r0 + (36 + 2 * i) * KB, [P, T]) for i in range(2)]
    y_hi = at("y_hi", r0, [P, DT, T], F32R)
    y_ab = at("y_ab", r0 + 16 * KB, [P, DT, T])
    y_lo = at("y_lo", r0 + 16 * KB, [P, DT, T], F32R)
    f_hi = at("f_hi", r0, [P, FT, T], F32R)
    f_lo = at("f_lo", r0 + 44 * KB, [P, FT, T], F32R)
    x_rows = at("x_rows", r0, [P, TT, D])
    out_rows = at("out_rows", r0, [P, TT, D])
    par_rows = at("par_rows", r0 + 16 * KB, [P, P])
    dw_rows = at("dw_rows", r0 + 17 * KB, [P, CONV])
    const_sb = at("const_sb", r0 + 20 * KB, [P, 3 * P + 2])
    pos_i = at("pos_i", r0 + 22 * KB, [P, T], I32)
    pos_f = at("pos_f", r0 + 24 * KB, [P, T])
    ang = at("ang", r0 + 26 * KB, [P, T])

    with ExitStack() as ctx:
        bank = [ctx.enter_context(nc.psum_tensor(f"bank{i}", [P, 512], F32)) for i in range(8)]
        s_bank, t_bank, o_bank, stat_bank = bank[0:4], bank[4:6], bank[6], bank[7]

        def sem(name):
            return ctx.enter_context(nc.semaphore(name))

        raw_ready = [sem(f"raw_ready{i}") for i in range(RAW)]
        hi_done = sem("hi_done")
        lo_done = sem("lo_done")
        mm_done = sem("mm_done")
        evac_done = sem("evac_done")
        evac_act = sem("evac_act")
        rope_put = sem("rope_put")
        lat_ready = sem("lat_ready")
        pool_own = sem("pool_own")
        forget_m = sem("forget_m")
        x_ready = sem("x_ready")
        feed_hi = sem("feed_hi")
        feed_lo = sem("feed_lo")
        sq_ready = sem("sq_ready")
        sq_added = sem("sq_added")
        acc_zero = sem("acc_zero")
        stat_done = sem("stat_done")
        std_ready = sem("std_ready")
        rstd_ready = sem("rstd_ready")
        sig_done = sem("sig_done")
        act_own = sem("act_own")
        dve_own = sem("dve_own")
        forget_z = sem("forget_z")
        forget_l = sem("forget_l")
        cum_ready = sem("cum_ready")
        cum_put = sem("cum_put")
        kr_ready = sem("kr_ready")
        kr_put = sem("kr_put")
        vt_done = sem("vt_done")
        v_ready = sem("v_ready")
        st_ready = sem("st_ready")
        ones_put = sem("ones_put")
        score_done = sem("score_done")
        max_ready = sem("max_ready")
        exp_done = sem("exp_done")
        norm_done = sem("norm_done")
        turn_done = sem("turn_done")
        turn_out = sem("turn_out")
        pv_done = sem("pv_done")
        o_hi_done = sem("o_hi_done")
        o_lo_done = sem("o_lo_done")
        tap_done = sem("tap_done")
        centred = sem("centred")
        conv_pre = sem("conv_pre")
        conv_out = sem("conv_out")
        y_ready = sem("y_ready")
        ff_ready = sem("ff_ready")
        out_tile = sem("out_tile")
        out_turned = sem("out_turned")
        out_scaled = sem("out_scaled")
        out_copied = sem("out_copied")
        put_done = sem("put_done")
        in_x = sem("in_x")
        in_par = sem("in_par")
        in_dw = sem("in_dw")
        in_const = sem("in_const")
        in_pos = sem("in_pos")
        in_bf = sem("in_bf")
        const_ok = sem("const_ok")
        par_turned = sem("par_turned")
        par_ok = sem("par_ok")
        x_turned = sem("x_turned")
        angles = sem("angles")
        trig = sem("trig")
        wait_held = sem("wait_held")
        zero_ok = sem("zero_ok")

        def passed(eng):
            eng.sem_inc(wait_held, 1)

        block = ctx.enter_context(nc.Block())

        @block.sync
        def _(sp):
            n = [0]
            freed = Count()

            def load(*parts):
                slot = n[0] % RAW
                sp.wait_ge(lo_done, freed.add())
                for to, src in parts:
                    sp.dma_start(to(raw[slot]), src).then_inc(raw_ready[slot], 16)
                n[0] += 1

            def block_of(w, row, k_tiles, col):
                src = w[bass.ds(row, k_tiles * P), bass.ds(col, P)].rearrange("(k p) c -> p k c", p=P)
                load((lambda r: r[:, 0:k_tiles * P].rearrange("p (k c) -> p k c", k=k_tiles), src))

            w_in, w_out, w_gate, w_up, w_down = (dram[k] for k in ("w_in", "w_out", "w_ffn_gate", "w_ffn_up", "w_ffn_down"))
            w_bo = [dram[k] for k in ("w_bo_a", "w_bo_b", "w_bo_c")]

            sp.dma_start(pos_i[:], dram["positions"].broadcast_to([P, T])).then_inc(in_pos, 16)
            sp.dma_start(const_sb[:], dram["consts"]).then_inc(in_const, 16)
            for t in range(TT):
                sp.dma_start(x_rows[:, t, :], dram["x"][t * P:(t + 1) * P, :]).then_inc(in_x, 16)
            sp.wait_ge(in_x, 16 * TT)

            with repeat(sp, DEPTH, [(freed, CHUNKS)]) as l:
                row = l * D
                block_of(w_in, row, DT, C_Q)
                block_of(w_in, row, DT, C_Q + P)
                block_of(w_in, row, 4, C_Q + 2 * P)
                block_of(w_in, row + 4 * P, 4, C_Q + 2 * P)
                block_of(w_in, row, DT, C_KV)
                block_of(w_in, row, DT, C_KV + P)
                with nc.allow_non_contiguous_dma("narrow columns"):
                    for half in range(2):
                        rows = w_in[bass.ds(row + half * 4 * P, 4 * P), :]
                        view = lambda r, a, b: r[:, 0:4 * (ROPE + HEADS)].rearrange("p (k c) -> p k c", k=4)[:, :, a:b]
                        load((lambda r: view(r, 0, ROPE), rows[:, C_KR:C_KR + ROPE].rearrange("(k p) c -> p k c", p=P)),
                             (lambda r: view(r, ROPE, ROPE + HEADS), rows[:, C_F:C_F + HEADS].rearrange("(k p) c -> p k c", p=P)))
                with repeat(sp, 2, [(freed, 4)]) as i:
                    for e in range(2):
                        block_of(w_in, row, DT, i * (2 * P) + (C_CONV + CONV + e * P))
                        block_of(w_in, row, DT, i * (2 * P) + (C_CONV + e * P))
                def heads_of(w, row, k_tiles, width, col, cols, b):
                    parts = []
                    for k in range(k_tiles):
                        src = w[bass.ds(row + k * P, P), 4 * b * width:(4 * b + 4) * width].rearrange("p (h c) -> p h c", c=width)
                        to = lambda r, k=k: r[:, 4 * cols * k:4 * cols * (k + 1)].rearrange("p (h c) -> p h c", h=4)
                        parts.append((to, src[:, :, col:col + cols]))
                    load(*parts)

                for b in range(2):
                    heads_of(dram["w_uq"], l * Q_LORA, 3, NOPE + ROPE, 0, NOPE, b)
                for b in range(2):
                    heads_of(dram["w_uq"], l * Q_LORA, 3, NOPE + ROPE, NOPE, ROPE, b)
                for part in (0, NOPE):
                    for b in range(2):
                        heads_of(dram["w_ukv"], l * KV_LORA, 2, NOPE + VDIM, part, NOPE, b)
                for i in range(QKV_CH):
                    block_of(w_in, row, DT, C_QB + i * P)
                    if i == 3:
                        sp.wait_ge(cum_ready, l + 1)
                        sp.wait_ge(score_done, l * STEPS + STEPS // 2)
                        sp.dma_start(k_t[NOPE:NOPE + 1, :, :], f_sum[2 * ROPE:MISC, :]).then_inc(cum_put, 16)
                with repeat(sp, DT, [(freed, 4)]) as i:
                    for b in range(2):
                        block_of(w_in, row, DT, i * P + (C_GATE + b * D))
                    for b in range(2):
                        block_of(w_bo[b], l * 512, 4, i * P)
                with repeat(sp, DT // 2, [(freed, 4)]) as i:
                    for e in range(2):
                        block_of(w_in, row, DT, i * (2 * P) + (C_GATE + 2 * D + e * P))
                        block_of(w_bo[2], l * 512, 4, i * (2 * P) + e * P)
                with repeat(sp, 2, [(freed, 4)]) as i:
                    for e in range(4):
                        block_of(w_out, row, DT, i * (4 * P) + e * P)
                with repeat(sp, FT // 2, [(freed, 4)]) as i:
                    for e in range(2):
                        block_of(w_gate, row, DT, i * (2 * P) + e * P)
                        block_of(w_up, row, DT, i * (2 * P) + e * P)
                with repeat(sp, 2, [(freed, 12)]) as i:
                    for e in range(4):
                        for b in range(3):
                            block_of(w_down, l * FFN + 8 * b * P, DOWN_K[b], i * (4 * P) + e * P)
            block_of(w_in, 0, DT, C_Q)
            block_of(w_in, 0, DT, C_Q + P)

            for n in range(2 * TT):
                t, half = n // 2, n % 2
                sp.wait_ge((out_copied, out_scaled)[half], t + 1)
                sp.dma_start(out[t * P:(t + 1) * P, half * T:(half + 1) * T], out_rows[:, t, half * T:(half + 1) * T]).then_inc(put_done, 16)
            sp.wait_ge(put_done, 2 * TT * 16)

        @block.gpsimd
        def _(pool):
            sq, zero, stat = Count(), Count(), Count()
            score, pv, evac, vr, fed, op, ohi, ol = Count(), Count(), Count(EVAC_CREDIT), Count(), Count(DT), Count(), Count(O_CREDIT), Count(O_CREDIT)
            own, fz, ea, rp = Count(), Count(), Count(), Count()

            def clear(acc):
                nc.gpsimd.memset(acc[:], 0.0).then_inc(acc_zero, 1)
                pool.wait_ge(acc_zero, zero.add())

            def add_square(acc, ring, i):
                pool.wait_ge(sq_ready, sq.add())
                nc.gpsimd.tensor_tensor(acc[:], acc[:], ring[i % 2][:], ALU.add).then_inc(sq_added, 1)
                pool.wait_ge(sq_added, sq.value)

            def attention(rows, hi_out, lo_out):
                pool.wait_ge(evac_done, evac.value)
                passed(pool)

                def stage(pair, first):
                    for e in range(2):
                        if not first:
                            pool.wait_ge(score_done, score.value - 4 + 4 * e)
                            passed(pool)
                        nc.gpsimd.tensor_copy(q_st[e][0:rows, :], head_of(q_t, pair, e)[0:rows, :]).then_inc(st_ready, 1)
                    if first:
                        pool.wait_ge(v_ready, vr.add(4))
                    else:
                        pool.wait_ge(pv_done, pv.value)
                    passed(pool)
                    nc.gpsimd.tensor_copy(v_st[:], v_n[:, :, bass.ds(pair * P, P)]).then_inc(st_ready, 1)
                    score.add(8)
                    pv.add(2)

                def pair_low(pair):
                    pool.wait_ge(o_hi_done, ohi.add())
                    nc.gpsimd.tensor_tensor(tile_of(lo_out, pair), o_raw[:], tile_of(hi_out, pair).bitcast(F32),
                                            ALU.subtract).then_inc(o_lo_done, 1)
                    pool.wait_ge(o_lo_done, ol.add())
                    passed(pool)

                stage(0, True)
                with repeat(pool, PAIRS - 1, [(score, 8), (pv, 2), (ohi, 1), (ol, 1)]) as i:
                    stage(i + 1, False)
                    pair_low(i)
                pair_low(PAIRS - 1)

            for s, credit in ((lo_done, RAW_CREDIT), (evac_done, EVAC_CREDIT), (exp_done, EXP_CREDIT),
                              (turn_out, TURN_CREDIT), (o_hi_done, O_CREDIT), (o_lo_done, O_CREDIT), (std_ready, STD_CREDIT)):
                pool.sem_inc(s, credit)
            nc.gpsimd.memset(ones[:], 1.0).then_inc(zero_ok, 1)
            nc.gpsimd.memset(eps_t[:, 0:1], RMS_EPS).then_inc(zero_ok, 1)
            nc.gpsimd.memset(eps_t[:, 1:2], LN_EPS).then_inc(zero_ok, 1)
            nc.gpsimd.memset(eps_t[:, 2:3], RMS_EPS / MLA_SCALE ** 2).then_inc(zero_ok, 1)
            nc.gpsimd.memset(u_pad[:, :, 0:TAPS - 1], 0.0).then_inc(zero_ok, 1)
            clear(x_acc)
            for j in range(DT):
                add_square(x_acc, x_sq, j)
            with repeat(pool, DEPTH, [(sq, SQUARES), (zero, 5), (stat, 6), (score, STEPS), (pv, 2 * HEADS),
                                      (evac, EVACS), (vr, 8), (fed, FEEDS), (op, 2), (ohi, HEADS), (ol, HEADS), (own, 2), (fz, 1), (ea, 8), (rp, HEADS)]):
                pool.wait_ge(stat_done, stat.add())
                passed(pool)
                clear(lat_acc)
                for j in range(3):
                    add_square(lat_acc, lat_sq, j)
                pool.wait_ge(stat_done, stat.add())
                passed(pool)
                clear(lat_acc)
                for j in range(2):
                    add_square(lat_acc, lat_sq, j + 1)
                stat.add()
                F = slice(2 * ROPE, MISC)
                pool.wait_ge(evac_done, evac.add(6))
                passed(pool)
                nc.gpsimd.tensor_scalar(key_a[F, :], misc_t[F, :], b_l[F, :], 0.0, ALU.add, ALU.min).then_inc(forget_m, 1)
                nc.gpsimd.tensor_scalar(misc_t[F, :], misc_t[F, :], b_l[F, :], None, ALU.add).then_inc(pool_own, 1)
                pool.wait_ge(forget_m, fz.add())
                passed(pool)
                nc.gpsimd.tensor_scalar(f_sum[F, :], key_a[F, :], 2.0, None, ALU.mult).then_inc(pool_own, 1)
                pool.wait_ge(pool_own, own.add(2))
                nc.gpsimd.tensor_tensor(f_sum[F, :], f_sum[F, :], misc_t[F, :], ALU.subtract).then_inc(forget_z, 1)
                pool.wait_ge(forget_z, fz.value)
                evac.add(CONV_CH)
                for g in range(HEADS):
                    if g % 4 == 0:
                        pool.wait_ge(evac_done, evac.add(2))
                    rows = slice(ROPE * (g % 4), ROPE * (g % 4 + 1))
                    nc.gpsimd.tensor_tensor(q_t[NOPE:NOPE + ROPE, g, :], rope_t[rows, g // 4 * 2, :],
                                            rope_t[rows, g // 4 * 2 + 1, :], ALU.add).then_inc(rope_put, 1)
                pool.wait_ge(rope_put, rp.add(HEADS))
                evac.add(4)
                pool.wait_ge(evac_act, ea.add(4))
                ea.add(4)
                attention(NOPE + ROPE, oa_hi, oa_lo)
                pool.wait_ge(score_done, score.value)
                pool.wait_ge(pv_done, pv.value)
                passed(pool)
                for e in range(2):
                    nc.gpsimd.memset(q_st[e][NOPE:NOPE + 1, :], 1.0).then_inc(ones_put, 1)
                pool.wait_ge(ones_put, op.add(2))
                evac.add(8)
                attention(NOPE, ob_hi, ob_lo)
                pool.wait_ge(pv_done, pv.value)
                passed(pool)
                clear(ln_acc)
                for j in range(CT):
                    add_square(ln_acc, ln_sq, j)
                stat.add(2)
                pool.wait_ge(feed_lo, fed.add(5 + CT))
                passed(pool)
                clear(x_acc)
                for j in range(DT):
                    add_square(x_acc, x_sq, j)
                pool.wait_ge(stat_done, stat.add())
                passed(pool)
                clear(x_acc)
                for j in range(DT):
                    add_square(x_acc, x_sq, j)
                evac.add(EVACS - 22 - 8)
                fed.add(FEEDS - 5 - CT)

        @block.scalar
        def _(act):
            ev, evac, sqa, stat, own, lr = Count(), Count(EVAC_CREDIT), Count(), Count(), Count(), Count()
            mt, olo = Count(), Count(O_CREDIT)
            vt, mx, tn, pv, ohi, fl, kr, yr, fr, ce, cp, co = (Count() for _ in range(12))
            rr = [Count() for _ in range(RAW)]

            def split(i):
                size, kind, _, dmas = CHUNK_LIST[i % CHUNKS]
                slot = i % RAW
                act.wait_ge(raw_ready[slot], rr[slot].add(16 * dmas))
                act.wait_ge(mm_done, ev.add(CHUNK_LIST[(i - 2) % CHUNKS][2]))
                last = None
                for to, of in split_views(kind, size, w_hi[i % SPLIT], raw[slot]):
                    last = nc.scalar.copy(to, of)
                last.then_inc(hi_done, 1)

            def feed(src, gain, hi, sq, i, first=False):
                nc.scalar.activation(hi, src, ACT.Copy, scale=gain).then_inc(feed_hi, 1)
                if not first:
                    act.wait_ge(sq_added, sqa.value - 1)
                    passed(act)
                sqa.add()
                nc.scalar.activation(sq[i % 2][:], src, ACT.Square).then_inc(sq_ready, 1)

            def root(std, size, eps, scale=1.0):
                act.wait_ge(stat_done, stat.add())
                nc.scalar.activation(std[:], stat_bank[:], ACT.Sqrt, scale=1.0 / (size * scale ** 2),
                                     bias=eps_t[:, eps:eps + 1]).then_inc(std_ready, 1)

            def exp_table():
                nc.scalar.activation(exp_sink[:], eps_t[:, 0:1], ACT.Exp)

            def attention(hi_out):
                def turn(s, first=False):
                    act.wait_ge(turn_done, tn.add())
                    if s % 4 == 0:
                        if not (first and s == 0):
                            act.wait_ge(pv_done, pv.value)
                        pv.add()
                    q = s % 4
                    nc.scalar.copy(p_t[:, 0:q + 1, q * P:(q + 1) * P],
                                   t_bank[s % 2][:, 0:(q + 1) * P].rearrange("p (k q) -> p k q", q=P)).then_inc(turn_out, 1)

                def pair_out(pair):
                    act.wait_ge(pv_done, ohi.add(2))
                    act.wait_ge(o_lo_done, olo.value)
                    olo.add()
                    nc.scalar.copy(o_raw[:], o_bank[:])
                    nc.scalar.copy(tile_of(hi_out, pair), o_bank[:]).then_inc(o_hi_done, 1)

                def body(pair, first):
                    for s in range(8):
                        act.wait_ge(max_ready, mx.add())
                        w = (s % 4 + 1) * P
                        nc.scalar.activation(p_b[:, P_AT[s % 4]:P_AT[s % 4] + w], s_bank[s % 4][:, 0:w], ACT.Exp,
                                             bias=neg_max[:, s % 4:s % 4 + 1],
                                             accum_out=row_sum[:, s % 4:s % 4 + 1]).then_inc(exp_done, 1)
                        if s >= 2 or not first:
                            turn((s - 2) % 8, first)
                        if s == 2 and not first:
                            pair_out(pair - 1)

                body(0, True)
                with repeat(act, PAIRS - 1, [(mx, 8), (tn, 8), (pv, 2), (ohi, 2), (olo, 1)]) as i:
                    body(i + 1, False)
                turn(6)
                turn(7)
                pair_out(PAIRS - 1)

            def value_tile(j):
                act.wait_ge(vt_done, vt.add())
                nc.scalar.copy(v_n[:, :, j * P:(j + 1) * P],
                               t_bank[j % 2][:].rearrange("p (t c) -> p t c", t=TT)).then_inc(v_ready, 1)

            for (name, rows), row in zip(PARAMS, G_ROWS):
                act.dma_start(par_rows[row:row + DEPTH * rows, :], dram[name].rearrange("l (r c) -> (l r) c", c=P)).then_inc(in_par, 16)
            act.dma_start(par_rows[DEPTH * DT:(DEPTH + 1) * DT, :], dram["final_norm_g"].rearrange("(r c) -> r c", c=P)).then_inc(in_par, 16)
            act.dma_start(dw_rows[0:DEPTH * TAPS, :], dram["dw_kernel"]).then_inc(in_dw, 16)
            with nc.allow_non_contiguous_dma("16 biases"):
                act.dma_start(b_f[2 * ROPE:MISC, :], dram["b_forget"].rearrange("l h -> h l")).then_inc(in_bf, 16)
            act.wait_ge(angles, 2)
            nc.scalar.activation(cos_t[:], tmp[2][:], ACT.Sin).then_inc(trig, 1)
            nc.scalar.activation(sin_t[:], tmp[3][:], ACT.Sin, scale=const_sb[:, 3 * P + 1:3 * P + 2]).then_inc(trig, 1)
            act.wait_ge(par_turned, 1)
            nc.scalar.copy(params[:], t_bank[0][:, 0:PARAM_ROWS]).then_inc(par_ok, 1)
            act.wait_ge(par_ok, 1)
            act.wait_ge(acc_zero, 1)
            for j in range(DT):
                act.wait_ge(x_ready, j + 1)
                feed(x_t[:, j, :], params[:, j:j + 1], h_hi[:, j, :], x_sq, j, j < 2)
                if j in (2, DT - 1):
                    c = j // (DT - 1)
                    act.wait_ge(raw_ready[c], rr[c].add(16))
                    nc.scalar.copy(w_hi[c][:], raw[c][:]).then_inc(hi_done, 1)
            act.wait_ge(par_turned, 2)
            nc.scalar.copy(dwk[:], t_bank[1][:, 0:CT * DEPTH * TAPS].rearrange("p (c k) -> p c k", c=CT)).then_inc(par_ok, 1)
            act.wait_ge(zero_ok, 4)

            with repeat(act, DEPTH, [(ev, EVENTS), (evac, EVACS), (sqa, SQUARES), (stat, 6), (own, 1), (lr, 5), (mt, EVENTS), (olo, HEADS), (vt, 8),
                                     (mx, STEPS), (tn, STEPS), (pv, 2 * HEADS), (ohi, 2 * HEADS), (fl, 1), (kr, 1),
                                     (yr, DT), (fr, FT), (ce, CT), (cp, CT), (co, CT), *zip(rr, RING_COUNTS)]):
                j = 0
                for c in range(LAT_CH):
                    split(LAT + c + 2)
                    if c == 0:
                        root(x_std, D, 0)
                    if c in (0, 1, 3, 4, 5):
                        act.wait_ge(evac_done, evac.add())
                        act.wait_ge(sq_added, sqa.value - 1)
                        sqa.add()
                        nc.scalar.activation(lat_sq[j % 2][:], c_raw[:, j, :], ACT.Square).then_inc(sq_ready, 1)
                        j += 1
                    if c == 5:
                        root(lat_std, Q_LORA, 2, MLA_SCALE)
                    if c == 7:
                        root(kv_std, KV_LORA, 0)
                evac.add()
                for c in range(CONV_CH):
                    split(CONVS + c + 2)
                    evac.add()
                    if c % 2 == 0:
                        act.wait_ge(evac_done, evac.value)
                        nc.scalar.activation(tmp[1][:], tmp[0][:], ACT.Sigmoid).then_inc(sig_done, 1)
                    if c == 1:
                        act.wait_ge(forget_z, fl.add())
                        nc.scalar.activation(f_sum[2 * ROPE:MISC, :], f_sum[2 * ROPE:MISC, :], ACT.Exp).then_inc(act_own, 1)
                        act.wait_ge(act_own, own.add())
                        nc.scalar.activation(tmp[3][2 * ROPE:MISC, :], f_sum[2 * ROPE:MISC, :], ACT.Ln, bias=1.0).then_inc(forget_l, 1)
                    for j in LAT_AT.get(c, ()):
                        act.wait_ge(lat_ready, lr.add())
                        nc.scalar.copy(c_hi[:, j, :], c_raw[:, j, :]).then_inc(feed_hi, 1)
                    if 3 <= c < 7:
                        if c == 3:
                            act.wait_ge(kr_ready, kr.add())
                        nc.scalar.copy(k_t[NOPE:NOPE + ROPE, 2 * c - 6:2 * c - 4, :],
                                       key_a[0:ROPE, :].unsqueeze(1).broadcast_to([ROPE, 2, T])).then_inc(kr_put, 1)
                mt.add(LAT_CH + CONV_CH)
                for c in range(UP_CH):
                    for m in range(2):
                        tile = 2 * c + m
                        b = s_bank[(UP_BANK + tile) % BANKS]
                        if c < 2:
                            act.wait_ge(mm_done, mt.add())
                            for e in range(2):
                                ins = nc.scalar.copy(q_t[0:NOPE, 2 * tile + e, :], b[NOPE * e:NOPE * (e + 1), :])
                            ins.then_inc(evac_act, 1)
                        elif c < 6:
                            mt.add()
                            evac.add()
                        else:
                            v = tile - 12
                            if v == 0:
                                act.wait_ge(evac_done, evac.value - 3)
                            act.wait_ge(mm_done, mt.add())
                            nc.scalar.copy(tmp[v % 2][:], b[:]).then_inc(evac_act, 1)
                            if v:
                                value_tile(v - 1)
                    split(UP + c + 2)
                    if c == 5:
                        exp_table()
                mt.add(EVENTS - 2 * UP_CH - LAT_CH - CONV_CH)
                value_tile(3)
                attention(oa_hi)
                for c in range(QKV_CH):
                    split(QKV + c + 2)
                    evac.add()
                    if c == 7:
                        exp_table()
                    if c >= 9:
                        value_tile(c - 9)
                value_tile(3)
                attention(ob_hi)

                def pass1(j, turn=None):
                    for c in range(4):
                        if (turn, c) == (1, 1):
                            stat.add()
                            root(ln_std, CONV, 1)
                        split(MERGE + 4 * (0 if turn is None else PASS1_TURNS + turn) + c + 2)
                        evac.add()
                        if c < 2:
                            act.wait_ge(evac_done, evac.value)
                            nc.scalar.activation(gate[c][:], tmp[c][:], ACT.Sigmoid,
                                                 bias=par[:, bass.ds(j + (R_BG + c * DT), 1)]).then_inc(sig_done, 1)
                        if (turn, c) == (0, 2):
                            for k in range(CT):
                                act.wait_ge(centred, ce.add())
                                act.wait_ge(sq_added, sqa.value - 1)
                                sqa.add()
                                nc.scalar.activation(ln_sq[k % 2][:], c_acc[:, k, :], ACT.Square).then_inc(sq_ready, 1)
                        if (turn, c) == (2, 0):
                            for k in range(CT):
                                act.wait_ge(conv_pre, cp.add())
                                nc.scalar.activation(ln_sig[:, k, :], c_acc[:, k, :], ACT.Sigmoid).then_inc(sig_done, 1)
                        if turn == 2 and c >= 1:
                            for k in SWISH[c]:
                                act.wait_ge(conv_out, co.add())
                                nc.scalar.copy(oc_hi[:, k, :], c_acc[:, k, :]).then_inc(feed_hi, 1)

                with repeat(act, PASS1_TURNS, [(ev, 4), (evac, 4), *((r, 16) for r in rr)]) as i:
                    pass1(i)
                for turn in range(LN_TURNS):
                    pass1(PASS1_TURNS + turn, turn)
                def pass2(i, turn=0):
                    for c in range(4):
                        split(MERGE2 + 4 * turn + c + 2)
                        evac.add()
                        e = c // 2
                        if c % 2 == 0:
                            act.wait_ge(evac_done, evac.value)
                            nc.scalar.activation(gate[e][:], tmp[e][:], ACT.Sigmoid,
                                                 bias=par[:, bass.ds(i * 2 + (R_BG + 2 * DT + e), 1)]).then_inc(sig_done, 1)
                        else:
                            act.wait_ge(y_ready, yr.add())
                            nc.scalar.copy(tile_of(y_hi, i * 2 + e), y_sum[e][:]).then_inc(feed_hi, 1)

                with repeat(act, PASS2_TURNS - 1, [(ev, 4), (evac, 4), (yr, 2), *((r, 16) for r in rr)]) as i:
                    pass2(i)
                pass2(PASS2_TURNS - 1, PASS2_TURNS - 1)
                with repeat(act, 2, [(ev, 4), (evac, 4), (sqa, 4), *((r, 16) for r in rr)]) as i:
                    for c in range(4):
                        split(OUT + c + 2)
                        act.wait_ge(evac_done, evac.add())
                        j = i * 4 + c
                        feed(tile_of(x_t, j), par[:, bass.ds(j + R_FFN, 1)], tile_of(h_hi, j), x_sq, c)

                def hidden(i, first=False):
                    for c in range(4):
                        split(FF + c + 2)
                        if first and c == 0:
                            root(x_std, D, 0)
                        evac.add()
                        if c % 2 == 0:
                            act.wait_ge(evac_done, evac.value)
                            nc.scalar.activation(tmp[1][:], tmp[0][:], ACT.Sigmoid).then_inc(sig_done, 1)
                        else:
                            act.wait_ge(ff_ready, fr.add())
                            nc.scalar.copy(tile_of(f_hi, i * 2 + c // 2), tmp[2][:]).then_inc(feed_hi, 1)

                hidden(0, True)
                with repeat(act, FT // 2 - 1, [(ev, 4), (evac, 4), (fr, 2), *((r, 16) for r in rr)]) as i:
                    hidden(i + 1)
                with repeat(act, 2, [(ev, 12), (evac, 4), (sqa, 4), *((r, 48) for r in rr)]) as i:
                    for c in range(12):
                        split(DOWN + c + 2)
                        if c % 3 == 2:
                            act.wait_ge(evac_done, evac.add())
                            j = i * 4 + c // 3
                            feed(tile_of(x_t, j), par[:, bass.ds(j + ROWS, 1)], tile_of(h_hi, j), x_sq, c // 3)
            act.wait_ge(stat_done, stat.add())
            nc.scalar.activation(std_col[:], stat_bank[:, 0:TT], ACT.Sqrt, scale=1.0 / D, bias=eps_t[:, 0:1]).then_inc(std_ready, 1)
            act.wait_ge(rstd_ready, 5 * DEPTH + 1)
            for t in range(TT):
                act.wait_ge(out_turned, t + 1)
                nc.scalar.activation(out_rows[:, t, 0:T], bank[t][:], ACT.Copy, scale=rstd_col[:, t:t + 1]).then_inc(out_copied, 1)

        @block.vector
        def _(dve):
            hi, mm, own, taps = Count(), Count(), Count(), Count()
            sg, fh, std, score, ex, krp, vt, fl, ce, rst, stat = (Count() for _ in range(11))
            std.n, out_n = STD_CREDIT, Count(EVAC_CREDIT)
            ex.n = EXP_CREDIT

            def mine(ins):
                ins.then_inc(dve_own, 1)
                dve.wait_ge(dve_own, own.add())

            def mine_later(ins):
                ins.then_inc(dve_own, 1)
                own.add()

            def mine_now():
                dve.wait_ge(dve_own, own.value)

            def split(i):
                size, kind = CHUNK_LIST[i % CHUNKS][:2]
                dve.wait_ge(hi_done, hi.add())
                h, last = w_hi[i % SPLIT], None
                for (to, of), (part, _) in zip(split_views(kind, size, w_lo[i % SPLIT], raw[i % RAW]),
                                               split_views(kind, size, h, raw[i % RAW])):
                    last = nc.vector.tensor_tensor(to, of, part.bitcast(F32), ALU.subtract)
                last.then_inc(lo_done, 1)

            tiles = [0]

            def tile_ready():
                dve.wait_ge(mm_done, mm.add())
                tiles[0] += 1
                return (tiles[0] - 1) % BANKS

            def evacuated(ins):
                ins.then_inc(evac_done, 1)
                out_n.add()

            def evacuated_here():
                dve.wait_ge(evac_done, out_n.value)

            def scaled(to, b, by, rows=slice(0, P), scale=None):
                if scale is None:
                    return nc.vector.tensor_tensor(to, s_bank[b][rows, :], by[rows, :], ALU.mult)
                return nc.vector.scalar_tensor_tensor(to, s_bank[b][rows, :], scale, by[rows, :], ALU.mult, ALU.mult)

            def feed_low(src, gain, h, lo):
                dve.wait_ge(feed_hi, fh.add())
                if gain is None:
                    ins = nc.vector.tensor_tensor(lo, src, h.bitcast(F32), ALU.subtract)
                else:
                    ins = nc.vector.scalar_tensor_tensor(lo, src, gain, h.bitcast(F32), ALU.mult, ALU.subtract)
                ins.then_inc(feed_lo, 1)

            def factor(root_t, to):
                dve.wait_ge(std_ready, std.add())
                nc.vector.reciprocal(to[:], root_t[:]).then_inc(rstd_ready, 1)
                dve.wait_ge(rstd_ready, rst.add())
                passed(dve)

            def part_of_factor(n, root_t, to):
                if n == 0:
                    dve.wait_ge(std_ready, std.add())
                part = slice(n * P, (n + 1) * P)
                ins = nc.vector.reciprocal(to[:, part], root_t[:, part])
                if n == 3:
                    ins.then_inc(rstd_ready, 1)
                    dve.wait_ge(rstd_ready, rst.add())

            last_tile = [None]

            def tap(c, k, first=False):
                if not first:
                    dve.wait_ge(tap_done, taps.value - (last_tile[0] not in (None, c)))
                last_tile[0] = c
                if isinstance(k, int) and k == 0:
                    ins = nc.vector.tensor_scalar(c_acc[:, c, :], u_pad[:, c, 0:T], dwk_l[:, c, 0:1],
                                                  par[:, R_DWB + c:R_DWB + c + 1], ALU.mult, ALU.add)
                else:
                    ins = nc.vector.scalar_tensor_tensor(c_acc[:, c, :], u_pad[:, c, bass.ds(k, T)], dwk_l[:, c, bass.ds(k, 1)],
                                                         c_acc[:, c, :], ALU.mult, ALU.add)
                ins.then_inc(tap_done, 1)
                taps.add()

            def attention(channel, tap0, last_split):
                def normalise(s):
                    dve.wait_ge(exp_done, ex.add())
                    mine(nc.vector.reciprocal(row_inv[:, s % 4:s % 4 + 1], row_sum[:, s % 4:s % 4 + 1]))
                    p = p_b[:, P_AT[s % 4]:P_AT[s % 4] + (s % 4 + 1) * P]
                    nc.vector.tensor_scalar(p, p, row_inv[:, s % 4:s % 4 + 1], None, ALU.mult).then_inc(norm_done, 1)

                def body(pair, first):
                    last_tile[0] = None
                    for s in range(8):
                        dve.wait_ge(score_done, score.add())
                        w = (s % 4 + 1) * P
                        nc.vector.tensor_reduce(neg_max[:, s % 4:s % 4 + 1], s_bank[s % 4][:, 0:w], AX_X, ALU.max,
                                                negate=True).then_inc(max_ready, 1)
                        if s > 0 or not first:
                            normalise((s - 1) % 8)
                        if first and s == 6:
                            last_split()
                        if s in TAP_STEPS:
                            tap(channel, pair * PAIR_TAPS + (tap0 + TAP_STEPS.index(s)))

                body(0, True)
                with repeat(dve, PAIRS - 1, [(score, 8), (ex, 8), (own, 8), (taps, PAIR_TAPS)]) as i:
                    body(i + 1, False)
                normalise(7)
                tiles[0] = 0

            dve.wait_ge(in_const, 16)
            nc.vector.tensor_copy(ident[:], const_sb[:, 0:P]).then_inc(const_ok, 1)
            dve.wait_ge(in_pos, 16)
            mine(nc.vector.tensor_copy(pos_f[:], pos_i[:]))
            mine(nc.vector.tensor_scalar(ang[:], pos_f[:], const_sb[:, 3 * P:3 * P + 1], None, ALU.mult))
            turns = ((0.25, tmp[2], tmp[0]), (0.0, tmp[3], tmp[1]))
            for shift, to, k in turns:
                ins = nc.vector.tensor_scalar(k[:], ang[:], 1.0 / TWO_PI, shift, ALU.mult, ALU.add)
            mine(ins)
            for step in (ROUND, -ROUND):
                for shift, to, k in turns:
                    ins = nc.vector.tensor_scalar(k[:], k[:], step, None, ALU.add)
                mine(ins)
            for part, first in zip(PI_PARTS, (True, False, False)):
                for shift, to, k in turns:
                    ins = nc.vector.scalar_tensor_tensor(to[:], k[:], -part, (ang if first else to)[:], ALU.mult, ALU.add)
                mine(ins)
            mine(nc.vector.tensor_scalar(tmp[2][:], tmp[2][:], TWO_PI / 4, None, ALU.add))
            for shift, to, k in turns:
                nc.vector.tensor_scalar(to[:], to[:], PI_DOWN, -PI_DOWN, ALU.min, ALU.max).then_inc(angles, 1)
            nc.vector.tensor_copy(ident_b[:], const_sb[:, 0:P]).then_inc(const_ok, 1)
            nc.vector.tensor_copy(mask_b[:], const_sb[:, P:3 * P].rearrange("p (m k) -> p m k", m=2)).then_inc(const_ok, 1)
            def first_split(i):
                dve.wait_ge(hi_done, hi.add())
                nc.vector.tensor_tensor(w_lo[i][:], raw[i][:], w_hi[i][:].bitcast(F32), ALU.subtract).then_inc(lo_done, 1)

            dve.wait_ge(par_ok, 1)
            for j in range(DT + 2):
                if j < DT:
                    dve.wait_ge(x_turned, j + 1)
                    nc.vector.tensor_copy(x_t[:, j, :], s_bank[j % BANKS][:]).then_inc(x_ready, 1)
                if j >= 2:
                    feed_low(x_t[:, j - 2, :], params[:, j - 2:j - 1], h_hi[:, j - 2, :], h_lo[:, j - 2, :])
                if j == 4:
                    first_split(0)
            first_split(1)
            dve.wait_ge(par_ok, 2)
            dve.wait_ge(trig, 2)
            dve.wait_ge(in_bf, 16)
            dve.wait_ge(zero_ok, 5)

            with repeat(dve, DEPTH, [(hi, CHUNKS), (mm, EVENTS), (out_n, EVACS), (own, OWN), (taps, CT * TAPS), (sg, 4 + 4 + 24 + 22),
                                     (fh, FEEDS), (std, 5), (score, STEPS), (ex, STEPS),
                                     (krp, 4), (vt, 8), (fl, 1), (ce, CT), (rst, 5), (stat, 6)]) as l:
                dve.wait_ge(feed_lo, fh.value)
                for (_, rows), g, r in zip(PARAMS, G_ROWS, (R_MIX, R_FFN, R_BG, R_Q, R_KV, R_DWB, R_LNG, R_LNB)):
                    nc.vector.tensor_copy(par[:, r:r + rows], params[:, bass.ds(l * rows + g, rows)])
                nc.vector.tensor_copy(par[:, ROWS:ROWS + DT], params[:, bass.ds(l * DT + DT, DT)])
                nc.vector.tensor_copy(b_l[2 * ROPE:MISC, :], b_f[2 * ROPE:MISC, bass.ds(l, 1)])
                mine(nc.vector.tensor_copy(dwk_l[:], dwk[:, :, bass.ds(l * TAPS, TAPS)]))
                j = 0
                for c in range(LAT_CH):
                    if c == 0:
                        split(c + 2)
                        factor(x_std, rstd_x)
                    if c in (0, 1, 3, 4, 5):
                        b = tile_ready()
                        evacuated(scaled(c_raw[:, j, :], b, rstd_x))
                        j += 1
                    elif c == 7:
                        b = tile_ready()
                        evacuated(nc.vector.tensor_tensor(misc_t[0:MISC, :], s_bank[b][0:MISC, :], rstd_x[0:MISC, :], ALU.mult))
                    else:
                        mm.add()
                    if c > 0:
                        split(LAT + c + 2)
                F = slice(2 * ROPE, MISC)
                k = 0
                for c in range(CONV_CH):
                    b = tile_ready()
                    evacuated(scaled(tmp[c % 2 * 2][:], b, rstd_x))
                    split(CONVS + c + 2)
                    if c % 2 == 1:
                        evacuated_here()
                        dve.wait_ge(sig_done, sg.add())
                        mine(nc.vector.tensor_tensor(u_pad[:, c // 2, TAPS - 1:], tmp[2][:], tmp[1][:], ALU.mult))
                    if c == 0:
                        factor(lat_std, rstd_q)
                    if c == 1:
                        factor(kv_std, rstd_kv)
                    if c == 2:
                        nc.vector.tensor_tensor(key_a[0:ROPE, :], misc_t[0:ROPE, :], cos_t[0:ROPE, :], ALU.mult)
                        mine_later(nc.vector.tensor_tensor(key_b[0:ROPE, :], misc_t[ROPE:2 * ROPE, :], sin_t[ROPE:2 * ROPE, :], ALU.mult))
                    if c == 3:
                        mine_now()
                        nc.vector.tensor_tensor(key_a[0:ROPE, :], key_a[0:ROPE, :], key_b[0:ROPE, :], ALU.add).then_inc(kr_ready, 1)
                    for j in LAT_AT.get(c - 1, ()):
                        feed_low(c_raw[:, j, :], None, c_hi[:, j, :], c_lo[:, j, :])
                    for j in LAT_AT.get(c, ()):
                        nc.vector.scalar_tensor_tensor(c_raw[:, j, :], c_raw[:, j, :], par[:, R_Q + j:R_Q + j + 1],
                                                       (rstd_q if j < 3 else rstd_kv)[:], ALU.mult, ALU.mult).then_inc(lat_ready, 1)
                    for _ in range(CONV_TAPS[c]):
                        tap(0, k, first=(k == 0))
                        k += 1
                    if c == 6:
                        dve.wait_ge(forget_l, fl.add())
                        dve.wait_ge(forget_m, fl.value)
                        nc.vector.tensor_tensor_scan(f_sum[F, :], tmp[3][F, :], key_a[F, :], 0.0, ALU.add, ALU.subtract).then_inc(cum_ready, 1)
                for c in range(UP_CH):
                    for m in range(2):
                        tile = 2 * c + m
                        if c < 2 or c >= 6:
                            mm.add()
                            tiles[0] += 1
                            continue
                        b = tile_ready()
                        if c < 4:
                            evacuated(scaled(rope_t[:, tile - 4, :], b, (cos_t, sin_t)[m]))
                        else:
                            for e in range(2):
                                ins = nc.vector.tensor_copy(k_t[0:NOPE, 2 * (tile - 8) + e, :], s_bank[b][NOPE * e:NOPE * (e + 1), :])
                            evacuated(ins)
                    if c < UP_CH - 1:
                        split(UP + c + 2)
                    for _ in range(UP_TAPS[c]):
                        tap(0, k)
                        k += 1
                vt.add(4)
                dve.wait_ge(kr_put, krp.add(4))
                attention(0, k, lambda: split(QKV + 1))
                todo = [(3 - k % 2, k // 2) for k in range(2 * 16)] + [(3, k) for k in range(16, 21)] + [(1, k) for k in range(4)]
                for c in range(QKV_CH):
                    b = tile_ready()
                    if c < 8:
                        to = (q_t, k_t)[c // 4]
                        for e in range(2):
                            ins = scaled(to[0:NOPE, 2 * (c % 4) + e, :], b, rstd_x, slice(NOPE * e, NOPE * (e + 1)),
                                         FOX_SCALE if c < 4 else None)
                        evacuated(ins)
                    else:
                        v = c - 8
                        if v >= 2:
                            dve.wait_ge(vt_done, vt.value - 1)
                        vt.add()
                        evacuated(scaled(tmp[v % 2][:], b, rstd_x))
                    if c < QKV_CH - 1:
                        split(QKV + c + 2)
                    for _ in range(QKV_TAPS[c]):
                        tap(*todo.pop(0))
                assert not todo
                attention(1, 4, lambda: split(MERGE + 1))

                def pass1(j, turn=None):
                    last_tile[0] = None
                    todo = []
                    if turn is None:
                        todo = [(c, j * n + (before + k)) for k in range(3) for c, before, n in SPREAD if k < n]
                    for c in range(4):
                        b = tile_ready()
                        if c < 2:
                            evacuated(scaled(tmp[c][:], b, rstd_x))
                        else:
                            dve.wait_ge(sig_done, sg.add())
                            evacuated(scaled((y_sum[0], tmp[3])[c - 2][:], b, gate[c - 2]))
                        if c == 3:
                            evacuated_here()
                            mine(nc.vector.tensor_tensor(tile_of(y_ab, j), y_sum[0][:], tmp[3][:], ALU.add))
                        split(MERGE + 4 * (0 if turn is None else PASS1_TURNS + turn) + c + 2)
                        if todo:
                            for _ in range(TURN_TAPS[c]):
                                tap(*todo.pop(0))
                        if (turn, c) == (0, 1):
                            dve.wait_ge(stat_done, l * 6 + 4)
                            for k in range(CT):
                                nc.vector.scalar_tensor_tensor(c_acc[:, k, :], stat_bank[:], -1.0 / CONV, c_acc[:, k, :],
                                                               ALU.mult, ALU.add).then_inc(centred, 1)
                        if turn == 1 and c >= 1:
                            for n in ((0, 1), (2,), (3,))[c - 1]:
                                part_of_factor(n, ln_std, ln_rstd)
                        if (turn, c) == (2, 0):
                            for k in range(CT):
                                ins = nc.vector.tensor_tensor(c_acc[:, k, :], c_acc[:, k, :], ln_rstd[:], ALU.mult)
                            mine(ins)
                            for k in range(CT):
                                nc.vector.tensor_scalar(c_acc[:, k, :], c_acc[:, k, :], par[:, R_LNG + k:R_LNG + k + 1],
                                                        par[:, R_LNB + k:R_LNB + k + 1], ALU.mult, ALU.add).then_inc(conv_pre, 1)
                        if turn == 2 and c >= 1:
                            for k in SWISH[c - 1]:
                                feed_low(c_acc[:, k, :], None, oc_hi[:, k, :], oc_lo[:, k, :])
                            for k in SWISH[c]:
                                dve.wait_ge(sig_done, sg.add())
                                nc.vector.tensor_tensor(c_acc[:, k, :], c_acc[:, k, :], ln_sig[:, k, :], ALU.mult).then_inc(conv_out, 1)

                with repeat(dve, PASS1_TURNS, [(hi, 4), (mm, 4), (out_n, 4), (own, 1), (sg, 2), (taps, 8)]) as i:
                    pass1(i)
                for turn in range(LN_TURNS):
                    pass1(PASS1_TURNS + turn, turn)
                for k in SWISH[3]:
                    feed_low(c_acc[:, k, :], None, oc_hi[:, k, :], oc_lo[:, k, :])
                ce.add(CT)
                stat.add(6)
                def pass2(i, turn=0):
                    for c in range(4):
                        b, e = tile_ready(), c // 2
                        if c % 2 == 0:
                            evacuated(scaled(tmp[e][:], b, rstd_x))
                            split(MERGE2 + 4 * turn + c + 2)
                        else:
                            split(MERGE2 + 4 * turn + c + 2)
                            dve.wait_ge(sig_done, sg.add())
                            evacuated(scaled(tmp[2 + e][:], b, gate[e]))
                            evacuated_here()
                            nc.vector.tensor_tensor(y_sum[e][:], tmp[2 + e][:], tile_of(y_ab, i * 2 + e), ALU.add).then_inc(y_ready, 1)
                            feed_low(y_sum[e][:], None, tile_of(y_hi, i * 2 + e), tile_of(y_lo, i * 2 + e))

                with repeat(dve, PASS2_TURNS - 1, [(hi, 4), (mm, 4), (out_n, 4), (sg, 2), (fh, 2)]) as i:
                    pass2(i)
                pass2(PASS2_TURNS - 1, PASS2_TURNS - 1)
                with repeat(dve, 2, [(hi, 4), (mm, 4), (out_n, 4), (fh, 4)]) as i:
                    for c in range(4):
                        b = tile_ready()
                        j = i * 4 + c
                        evacuated(nc.vector.tensor_tensor(tile_of(x_t, j), s_bank[b][:], tile_of(x_t, j), ALU.add))
                        split(OUT + c + 2)
                        feed_low(tile_of(x_t, j), par[:, bass.ds(j + R_FFN, 1)], tile_of(h_hi, j), tile_of(h_lo, j))

                def hidden(i, first=False):
                    for c in range(4):
                        if first and c == 0:
                            split(FF + c + 2)
                            factor(x_std, rstd_x)
                        b = tile_ready()
                        evacuated(scaled(tmp[c % 2 * 3][:], b, rstd_x))
                        if c % 2 == 1:
                            evacuated_here()
                            nc.vector.tensor_tensor(tmp[2][:], tmp[2][:], tmp[3][:], ALU.mult).then_inc(ff_ready, 1)
                        if not (first and c == 0):
                            split(FF + c + 2)
                        if c % 2 == 0:
                            dve.wait_ge(sig_done, sg.add())
                            mine_later(nc.vector.tensor_tensor(tmp[2][:], tmp[0][:], tmp[1][:], ALU.mult))
                        else:
                            feed_low(tmp[2][:], None, tile_of(f_hi, i * 2 + c // 2), tile_of(f_lo, i * 2 + c // 2))

                hidden(0, True)
                with repeat(dve, FT // 2 - 1, [(hi, 4), (mm, 4), (out_n, 4), (own, 2), (sg, 2), (fh, 2)]) as i:
                    hidden(i + 1)
                with repeat(dve, 2, [(hi, 12), (mm, 12), (out_n, 4), (fh, 4)]) as i:
                    for c in range(12):
                        if c % 3 < 2:
                            mm.add()
                            split(DOWN + c + 2)
                            continue
                        b = tile_ready()
                        j = i * 4 + c // 3
                        evacuated(nc.vector.tensor_tensor(tile_of(x_t, j), s_bank[b][:], tile_of(x_t, j), ALU.add))
                        split(DOWN + c + 2)
                        feed_low(tile_of(x_t, j), par[:, bass.ds(j + ROWS, 1)], tile_of(h_hi, j), tile_of(h_lo, j))
            dve.wait_ge(feed_lo, fh.value)
            for j in range(DT):
                dve.wait_ge(sq_ready, DEPTH * SQUARES + j + 1)
                nc.vector.tensor_scalar(x_t[:, j, :], x_t[:, j, :], params[:, DEPTH * DT + j:DEPTH * DT + j + 1], None,
                                        ALU.mult).then_inc(out_tile, 1)
            dve.wait_ge(std_ready, std.add())
            nc.vector.reciprocal(rstd_col[:], std_col[:]).then_inc(rstd_ready, 1)
            dve.wait_ge(rstd_ready, rst.add())
            for t in range(TT):
                dve.wait_ge(out_turned, TT + t + 1)
                nc.vector.tensor_scalar(out_rows[:, t, T:2 * T], bank[TT + t][:], rstd_col[:, t:t + 1], None,
                                        ALU.mult).then_inc(out_scaled, 1)

        @block.tensor
        def _(pe):
            lo, ev, fl, sqa, std = Count(RAW_CREDIT), Count(), Count(), Count(), Count(STD_CREDIT)
            st, ex, nm, to, ol, vr, taps, nt = Count(), Count(), Count(), Count(TURN_CREDIT), Count(), Count(), Count(), [0]
            pairs_in = Count(O_CREDIT)
            cumc, ea = Count(), Count()

            def products(bank_t, rows, slot, cols, m, k_tiles, rhs, k0, first, last, fresh):
                for k in range(k_tiles):
                    w = slice(k * cols + m * P, k * cols + m * P + rows)
                    a, b = rhs(k0 + k)
                    if fresh:
                        pe.wait_ge(feed_lo, fl.value + (k0 + k + 1))
                    for p, (wt, x) in enumerate(((w_hi, a), (w_hi, b), (w_lo, a))):
                        ins = nc.tensor.matmul(bank_t[0:rows, :], wt[slot][:, w], x,
                                               start=first and k == 0 and p == 0, stop=last and k == k_tiles - 1 and p == 2)
                return ins

            def chunk(i, rhs, tiles=1, k_tiles=DT, cols=P, k0=0, first=True, last=True, rows=P, between=None, fresh=False,
                      bank_free=None):
                pe.wait_ge(lo_done, lo.add())
                for m in range(tiles):
                    if first:
                        if bank_free:
                            bank_free(m)
                        else:
                            pe.wait_ge(evac_done, ev.add())
                        nt[0] += 1
                    products(s_bank[(nt[0] - 1) % BANKS], rows, i % SPLIT, cols, m, k_tiles, rhs, k0, first, last,
                             fresh and m == 0).then_inc(mm_done, 1)
                    if between:
                        between(m)

            h = lambda k: (h_hi[:, k, :], h_lo[:, k, :])

            def statistic(src, n_sq):
                pe.wait_ge(sq_added, sqa.add(n_sq))
                pe.wait_ge(std_ready, std.value)
                nc.tensor.matmul(stat_bank[:], ones[:], src[:], start=True, stop=True).then_inc(stat_done, 1)
                std.add()

            def turn_values(j, back, latent=False):
                if latent:
                    pe.wait_ge(evac_act, ea.value - back)
                else:
                    pe.wait_ge(evac_done, ev.value + (EVAC_CREDIT - back))
                if j >= 2:
                    pe.wait_ge(v_ready, vr.value - 1)
                vr.add()
                for t in range(TT):
                    ins = nc.tensor.transpose(t_bank[j % 2][:, t * P:(t + 1) * P], tmp[j % 2][:, t * P:(t + 1) * P], ident[:])
                ins.then_inc(vt_done, 1)

            def attention(rows, kind, dense, tail):
                def logits(pair, s):
                    e, q = s // 4, s % 4
                    pe.wait_ge(exp_done, ex.add())
                    if q == 0:
                        pe.wait_ge(st_ready, st.value + 1 + e)
                    w = (q + 1) * P
                    nc.tensor.matmul(s_bank[q][:, 0:w], q_st[e][0:rows, q * P:w], head_of(k_t, pair, e)[0:rows, 0:w],
                                     start=True, stop=True)
                    nc.tensor.matmul(s_bank[q][:, q * P:w], ident_b[:], mask_b[:, kind, :], start=False, stop=True,
                                     skip_group_check=True).then_inc(score_done, 1)

                def turn(s):
                    pe.wait_ge(norm_done, nm.add())
                    pe.wait_ge(turn_out, to.value - 1)
                    to.add()
                    for k in range(s % 4 + 1):
                        at_k = P_AT[s % 4] + k * P
                        ins = nc.tensor.transpose(t_bank[s % 2][:, k * P:(k + 1) * P], p_b[:, at_k:at_k + P], ident[:])
                    ins.then_inc(turn_done, 1)

                def values(e, ago):
                    if e == 0:
                        pe.wait_ge(o_hi_done, pairs_in.value)
                        pairs_in.add()
                        pe.wait_ge(st_ready, st.value + 3)
                    pe.wait_ge(turn_out, to.value - ago)
                    for k in range(TT):
                        ins = nc.tensor.matmul(o_bank[e * VDIM:(e + 1) * VDIM, k * P:T], v_st[:, k, e * VDIM:(e + 1) * VDIM],
                                               p_t[:, k, k * P:T], start=(k == 0), stop=True, skip_group_check=True)
                    ins.then_inc(pv_done, 1)

                def body(pair, first=False, last=False):
                    for s in range(8):
                        if s == 5:
                            st.add(3)
                        if s < 5:
                            logits(pair, s + 3)
                        elif not last:
                            logits(pair + 1, s - 5)
                        if last and s == 6:
                            tail()
                        turn(s)
                        if s == 0 and not first:
                            values(1, 1)
                        if s == 4:
                            values(0, 1)

                if kind == 0:
                    pe.wait_ge(evac_done, ev.value + EVAC_CREDIT)
                    pe.wait_ge(evac_act, ea.value - 1)
                else:
                    pe.wait_ge(evac_done, ev.value + (EVAC_CREDIT - 1))
                logits(0, 0)
                dense()
                if kind == 0:
                    pe.wait_ge(evac_act, ea.value)
                else:
                    pe.wait_ge(evac_done, ev.value + EVAC_CREDIT)
                nt[0] = 0
                logits(0, 1)
                logits(0, 2)
                body(0, first=True)
                with repeat(pe, PAIRS - 2, [(st, 3), (ex, 8), (nm, 8), (to, 8), (pairs_in, 1)]) as i:
                    body(i + 1)
                body(PAIRS - 1, last=True)
                values(1, 0)

            pe.wait_ge(const_ok, 1)
            pe.wait_ge(in_par, 16 * (len(PARAMS) + 1))
            nc.tensor.transpose(t_bank[0][:, 0:PARAM_ROWS], par_rows[0:PARAM_ROWS, :], ident[0:PARAM_ROWS, 0:PARAM_ROWS]).then_inc(par_turned, 1)
            pe.wait_ge(in_x, 16 * TT)
            for j in range(DT):
                if j >= BANKS:
                    pe.wait_ge(x_ready, j - BANKS + 1)
                for t in range(TT):
                    ins = nc.tensor.transpose(s_bank[j % BANKS][:, t * P:(t + 1) * P], x_rows[:, t, j * P:(j + 1) * P], ident[:])
                ins.then_inc(x_turned, 1)
            pe.wait_ge(in_dw, 16)
            R = DEPTH * TAPS
            for c in range(CT):
                ins = nc.tensor.transpose(t_bank[1][:, c * R:(c + 1) * R], dw_rows[0:R, c * P:(c + 1) * P], ident[0:R, 0:R])
            ins.then_inc(par_turned, 1)
            pe.wait_ge(x_ready, BANKS + 1)
            pe.wait_ge(zero_ok, 1)
            pe.wait_ge(const_ok, 3)

            with repeat(pe, DEPTH, [(lo, CHUNKS), (ev, EVACS), (ea, 8), (fl, FEEDS), (sqa, SQUARES), (std, 5), (st, 3 * HEADS), (ex, STEPS),
                                    (nm, STEPS), (to, STEPS), (pairs_in, HEADS), (vr, 8), (taps, CT * TAPS), (cumc, 16)]):
                chunk(0, h, fresh=True)
                fl.add(DT)
                statistic(x_acc, DT)
                chunk(LAT + 1, h)
                chunk(LAT + 2, h, k_tiles=4, last=False)
                chunk(LAT + 3, h, k_tiles=4, k0=4, first=False)
                chunk(LAT + 4, h)
                chunk(LAT + 5, h)
                statistic(lat_acc, 3)
                chunk(LAT + 6, h, k_tiles=4, cols=MISC, rows=MISC, last=False)
                chunk(LAT + 7, h, k_tiles=4, k0=4, cols=MISC, rows=MISC, first=False)
                statistic(lat_acc, 2)
                for c in range(CONV_CH):
                    chunk(CONVS + c, h)
                cq = lambda k: (c_hi[:, k, :], c_lo[:, k, :])
                ckv = lambda k: (c_hi[:, 3 + k, :], c_lo[:, 3 + k, :])
                pe.wait_ge(feed_lo, fl.add(5))

                def after_dense(t):
                    pe.wait_ge(evac_done, ev.value + (EVAC_CREDIT - 3 + t))
                    ea.add()

                def after_queries(t):
                    pe.wait_ge(evac_act, ea.value - 3 + t)
                    ev.add()

                for c in range(2):
                    chunk(UP + c, cq, tiles=2, k_tiles=3, cols=2 * P, bank_free=lambda m: after_dense(2 * c + m))
                for c in range(2):
                    chunk(UP + 2 + c, cq, tiles=2, k_tiles=3, cols=2 * P, bank_free=lambda m: after_queries(2 * c + m))
                for c in range(2):
                    chunk(UP + 4 + c, ckv, tiles=2, k_tiles=2, cols=2 * P)
                chunk(UP + 6, ckv, tiles=2, k_tiles=2, cols=2 * P, bank_free=lambda m: after_dense(m),
                      between=lambda m: turn_values(0, 1, True) if m == 1 else None)
                chunk(UP + 7, ckv, tiles=2, k_tiles=2, cols=2 * P, bank_free=lambda m: after_dense(2 + m),
                      between=lambda m: turn_values(1 + m, 1, True))

                def dense_at(i, rhs):
                    pe.wait_ge(exp_done, ex.value + 1)
                    chunk(i, rhs)

                attention(NOPE + ROPE, 0, lambda: turn_values(3, 0, True), lambda: dense_at(QKV, h))
                for c in range(1, QKV_CH):
                    if c < BANKS:
                        pe.wait_ge(exp_done, ex.value + 1 + c)
                    chunk(QKV + c, h)
                    if c >= 9:
                        turn_values(c - 9, 1)
                pe.wait_ge(cum_put, cumc.add(16))
                attention(NOPE + 1, 1, lambda: turn_values(3, 0), lambda: dense_at(MERGE, h))
                for c in range(1, BANKS):
                    pe.wait_ge(exp_done, ex.value + 1 + c)

                outs = [lambda k, a=a, b=b: (a[:, k, :], b[:, k, :]) for a, b in ((oa_hi, oa_lo), (ob_hi, ob_lo), (oc_hi, oc_lo))]

                def pass1(turn=None, c0=0):
                    for c in range(c0, 4):
                        if c == 2:
                            pe.wait_ge(o_lo_done, pairs_in.value)
                        chunk(MERGE + c, h if c < 2 else outs[c - 2], k_tiles=DT if c < 2 else PAIRS)
                        if (turn, c) == (0, 0):
                            pe.wait_ge(tap_done, taps.add(CT * TAPS))
                            for k in range(CT):
                                ins = nc.tensor.matmul(stat_bank[:], ones[:], c_acc[:, k, :], start=(k == 0), stop=(k == CT - 1))
                            ins.then_inc(stat_done, 1)
                        if (turn, c) == (1, 0):
                            statistic(ln_acc, CT)

                pass1(c0=1)
                with repeat(pe, PASS1_TURNS - 1, [(lo, 4), (ev, 4)]):
                    pass1()
                for turn in range(LN_TURNS):
                    pass1(turn)
                fl.add(CT)
                with repeat(pe, DT // 2, [(lo, 4), (ev, 4)]):
                    for c in range(4):
                        if c == 1:
                            pe.wait_ge(feed_lo, fl.value)
                        chunk(MERGE2 + c, outs[2] if c % 2 else h, k_tiles=CT if c % 2 else DT)
                y = lambda k: (y_hi[:, k, :], y_lo[:, k, :])
                with repeat(pe, 2, [(lo, 4), (ev, 4)]):
                    for c in range(4):
                        chunk(OUT + c, y, fresh=(c == 0))
                fl.add(DT)

                def hidden(first=False):
                    for c in range(4):
                        chunk(FF + c, h, fresh=(first and c == 0))
                        if first and c == 0:
                            fl.add(DT)
                            statistic(x_acc, DT)

                hidden(True)
                with repeat(pe, FT // 2 - 1, [(lo, 4), (ev, 4)]):
                    hidden()
                f = lambda k: (f_hi[:, k, :], f_lo[:, k, :])
                with repeat(pe, 2, [(lo, 12), (ev, 4)]):
                    for c in range(12):
                        b = c % 3
                        chunk(DOWN + c, f, k_tiles=DOWN_K[b], k0=8 * b, first=(b == 0), last=(b == 2), fresh=(c < 3))
                fl.add(FT)
            pe.wait_ge(evac_done, ev.value + EVAC_CREDIT)
            for j in range(TT):
                pe.wait_ge(out_tile, j + 1)
                for t in range(TT):
                    ins = nc.tensor.transpose(bank[t][:, j * P:(j + 1) * P], x_t[:, j, t * P:(t + 1) * P], ident[:])
                    if j == TT - 1:
                        ins.then_inc(out_turned, 1)
            pe.wait_ge(sq_added, sqa.add(DT))
            pe.wait_ge(std_ready, std.value)
            for t in range(TT):
                ins = nc.tensor.matmul(stat_bank[:, t:t + 1], x_acc[:, t * P:(t + 1) * P], ones[:, 0:1], start=(t == 0), stop=True,
                                       skip_group_check=True)
            ins.then_inc(stat_done, 1)
            std.add()
            pe.wait_ge(out_tile, DT)
            for t in range(TT):
                if t == TT - 1:
                    pe.wait_ge(std_ready, std.value)
                for j in range(TT, DT):
                    ins = nc.tensor.transpose(bank[TT + t][:, (j - TT) * P:(j - TT + 1) * P], x_t[:, j, t * P:(t + 1) * P], ident[:])
                ins.then_inc(out_turned, 1)


def kernel(**inputs):
    import concourse.bacc as bacc
    from concourse.bass_utils import run_bass_kernel_spmd

    shapes = {
        "x": (T, D), "positions": (1, T), "norm_mix_g": (DEPTH, D), "w_in": (DEPTH * D, IN_WIDTH),
        "b_gate": (DEPTH, 3 * D), "q_norm_g": (DEPTH, Q_LORA), "w_uq": (DEPTH * Q_LORA, HEADS * (NOPE + ROPE)),
        "kv_norm_g": (DEPTH, KV_LORA), "w_ukv": (DEPTH * KV_LORA, HEADS * (NOPE + VDIM)), "b_forget": (DEPTH, HEADS),
        "dw_kernel": (DEPTH * TAPS, CONV), "dw_bias": (DEPTH, CONV), "conv_ln_g": (DEPTH, CONV), "conv_ln_b": (DEPTH, CONV),
        "w_bo_a": (DEPTH * 512, D), "w_bo_b": (DEPTH * 512, D), "w_bo_c": (DEPTH * CONV, D), "w_out": (DEPTH * D, D),
        "norm_ffn_g": (DEPTH, D), "w_ffn_gate": (DEPTH * D, FFN), "w_ffn_up": (DEPTH * D, FFN),
        "w_ffn_down": (DEPTH * FFN, D), "final_norm_g": (D,),
    }
    consts = np.zeros((P, 3 * P + 2), np.float32)
    q, k = np.arange(P)[:, None], np.arange(P)[None, :]
    consts[:, 0:P] = q == k
    consts[:, P:2 * P] = np.where(q // CHUNK_MASK >= k // CHUNK_MASK, 0, MASKED)
    consts[:, 2 * P:3 * P] = np.where(q >= k, 0, MASKED)
    freq = np.float32(1) / np.float32(THETA) ** (np.arange(0, ROPE, 2, dtype=np.float32) / np.float32(ROPE))
    consts[:, 3 * P] = freq[np.arange(P) % (ROPE // 2)]
    consts[:, 3 * P + 1] = np.where(np.arange(P) % ROPE < ROPE // 2, -1, 1)

    nc = bacc.Bacc("TRN2", target_bir_lowering=False, num_devices=1)
    arrays, dram = {}, {}
    for name, shape in shapes.items():
        arrays["in_" + name] = np.ascontiguousarray(inputs[name]).reshape(shape)
    arrays["in_consts"] = consts
    for name, a in arrays.items():
        dram[name[3:]] = nc.dram_tensor(name, a.shape, mybir.dt.from_np(a.dtype), kind="ExternalInput").ap()
    out = nc.dram_tensor("out_x", (T, D), F32, kind="ExternalOutput").ap()
    trunk(nc, dram, out)
    r = run_bass_kernel_spmd(nc, [arrays], core_ids=[0])
    return r.results[0]["out_x"].reshape(1, T, D)
```
